# Optimizing a Trainium2 kernel written in Bass

```python
import math
import jax, jax.numpy as jnp
from jax import lax
import numpy as np

D_MODEL = 1024
BATCH = 1
SEQ = 128
DEPTH = 2
DEC_BATCH = 1
DEC_SEQ = 256
PAST_LEN = 128

GRID_W = 64
EPS = 1e-6
N_EVEN = (DEPTH + 1) // 2
N_ODD = DEPTH // 2
ML_HEADS = 4
ML_DK = 128
ML_DV = 128
ML_CHUNK = 64
MLA_HEADS = 8
MLA_Q_RANK = 384
MLA_KV_RANK = 256
MLA_NOPE = 64
MLA_ROPE = 32
MLA_V = 64
ATTN_BLOCK = 128
ROPE_BASE = 10000.0
SSD_HEADS = 8
SSD_P = 64
SSD_GROUPS = 2
SSD_N = 128
SSD_CHUNK = 64
GDN_HEADS = 4
GDN_DK = 128
GDN_DV = 128
GDN_CHUNK = 64
CONV_W = 5
MOE_GROUPS = 4
MOE_PER_GROUP = 8
MOE_EXPERTS = MOE_GROUPS * MOE_PER_GROUP
MOE_TOPK = 2
MOE_FF = 256

ML_W = ML_HEADS * ML_DK
MLA_OUT = MLA_HEADS * MLA_V
EVEN_SPLIT = [ML_W, ML_W, ML_HEADS * ML_DV, ML_HEADS * ML_DV, 2 * ML_HEADS, 2 * ML_HEADS,
              MLA_Q_RANK, MLA_KV_RANK, MLA_ROPE]
IN_EVEN = sum(EVEN_SPLIT)
OUT_EVEN = ML_HEADS * ML_DV + MLA_OUT
SSD_W = SSD_HEADS * SSD_P
SSD_BC = SSD_GROUPS * SSD_N
SSD_CONV_CH = SSD_W + 2 * SSD_BC
GDN_W = GDN_HEADS * GDN_DK
GDN_CONV_CH = 2 * GDN_W + GDN_HEADS * GDN_DV
ODD_SPLIT = [SSD_W, SSD_CONV_CH, 2 * SSD_HEADS, GDN_CONV_CH, GDN_HEADS * GDN_DV, 2 * GDN_HEADS, 2 * GDN_HEADS]
IN_ODD = sum(ODD_SPLIT)
OUT_ODD = SSD_W + GDN_HEADS * GDN_DV

kernel_name = 'hybrid_mlstm_mla_ssd_gdn_hmoe_prefix_dit'

def rms_norm(x, g):
    xf = x.astype(jnp.float32)
    y = xf * lax.rsqrt(jnp.mean(xf * xf, axis=-1, keepdims=True) + EPS)
    return (y * g.astype(jnp.float32)).astype(x.dtype)

def l2_norm(x):
    return x * lax.rsqrt(jnp.sum(x * x, axis=-1, keepdims=True) + EPS)

def split_cols(y, sizes):
    idx = [int(s) for s in np.cumsum(sizes)[:-1]]
    return jnp.split(y, idx, axis=-1)

def heads_first(x, n_heads):
    B, T, _ = x.shape
    return x.reshape(B, T, n_heads, -1).transpose(0, 2, 1, 3)

def flip_t(x):
    return jnp.flip(x, axis=2)

def to_chunks(x, L):
    B, H, T = x.shape[:3]
    return jnp.moveaxis(x.reshape(B, H, T // L, L, *x.shape[3:]), 2, 0)

def from_chunks(y):
    nc, B, H, L = y.shape[:4]
    return jnp.moveaxis(y, 0, 2).reshape(B, H, nc * L, *y.shape[4:])

def centred_dwconv(x, w, b):
    pad = CONV_W // 2
    y = lax.conv_general_dilated(x, w[:, None, :].astype(x.dtype), window_strides=(1,),
                                 padding=[(pad, pad)], dimension_numbers=('NWC', 'WIO', 'NWC'),
                                 feature_group_count=x.shape[-1])
    return jax.nn.silu(y + b.astype(x.dtype))

def axial_rope(x):
    T = x.shape[1]
    rows = T // GRID_W
    row, col = jnp.meshgrid(jnp.arange(rows), jnp.arange(GRID_W), indexing='ij')
    row = row.reshape(-1).astype(jnp.float32)
    col = col.reshape(-1).astype(jnp.float32)
    half = MLA_ROPE // 2
    nf = half // 2
    inv = ROPE_BASE ** (-jnp.arange(nf, dtype=jnp.float32) / nf)

    def rot(xa, pos):
        ang = pos[:, None] * inv
        cos = jnp.cos(ang)[None, :, None, :]
        sin = jnp.sin(ang)[None, :, None, :]
        x1, x2 = xa[..., :nf], xa[..., nf:]
        return jnp.concatenate([x1 * cos - x2 * sin, x1 * sin + x2 * cos], axis=-1)

    xf = x.astype(jnp.float32)
    return jnp.concatenate([rot(xf[..., :half], row), rot(xf[..., half:], col)], axis=-1).astype(x.dtype)

def mla_attend(q, k, v):
    B, Tq, H, dq = q.shape
    nb = Tq // ATTN_BLOCK
    qb = q.reshape(B, nb, ATTN_BLOCK, H, dq).transpose(1, 0, 2, 3, 4)
    scale = dq ** -0.5

    def one_block(qi):
        s = jnp.einsum('bqhd,bkhd->bhqk', qi, k).astype(jnp.float32) * scale
        p = jax.nn.softmax(s, axis=-1).astype(v.dtype)
        return jnp.einsum('bhqk,bkhd->bqhd', p, v)

    o = lax.map(one_block, qb)
    return o.transpose(1, 0, 2, 3, 4).reshape(B, Tq, H, -1)

def mlstm_scan(q, k, v, logi, logf, C0, n0, m0):
    L = ML_CHUNK
    tril = jnp.tril(jnp.ones((L, L), dtype=bool))

    def step(carry, xs):
        C, n, m = carry
        qc, kc, vc, li, lf = xs
        b = jnp.cumsum(lf, axis=-1)
        dmat = jnp.where(tril, b[..., :, None] - b[..., None, :] + li[..., None, :], -jnp.inf)
        inter = b + m[..., None]
        mq = jnp.maximum(inter, jnp.max(dmat, axis=-1))
        s = jnp.einsum('bhtd,bhsd->bhts', qc, kc) * jnp.exp(dmat - mq[..., None])
        a = jnp.exp(inter - mq)
        num = jnp.einsum('bhts,bhsv->bhtv', s, vc) + a[..., None] * jnp.einsum('bhtk,bhkv->bhtv', qc, C)
        den = jnp.sum(s, axis=-1) + a * jnp.einsum('bhtk,bhk->bht', qc, n)
        h = num / jnp.maximum(jnp.abs(den), jnp.exp(-mq))[..., None]
        bl = b[..., -1]
        g = bl[..., None] - b + li
        m_new = jnp.maximum(bl + m, jnp.max(g, axis=-1))
        wk = jnp.exp(g - m_new[..., None])
        dec = jnp.exp(bl + m - m_new)
        C = dec[..., None, None] * C + jnp.einsum('bhs,bhsk,bhsv->bhkv', wk, kc, vc)
        n = dec[..., None] * n + jnp.einsum('bhs,bhsk->bhk', wk, kc)
        return (C, n, m_new), h

    xs = tuple(to_chunks(a, L) for a in (q, k, v, logi, logf))
    (C, n, m), h = lax.scan(step, (C0, n0, m0), xs)
    return from_chunks(h), C, n, m

def ssd_scan(x, dt, A, Bh, Ch, h0):
    L = SSD_CHUNK
    tril = jnp.tril(jnp.ones((L, L), dtype=bool))

    def step(hs, xs):
        xc, dtc, Bc, Cc = xs
        a = jnp.cumsum(dtc * A[None, :, None], axis=-1)
        seg = jnp.exp(jnp.where(tril, a[..., :, None] - a[..., None, :], -jnp.inf))
        gmat = jnp.einsum('bhtn,bhsn->bhts', Cc, Bc) * seg * dtc[..., None, :]
        y = jnp.einsum('bhts,bhsp->bhtp', gmat, xc) + jnp.exp(a)[..., None] * jnp.einsum('bhtn,bhpn->bhtp', Cc, hs)
        al = a[..., -1]
        wgt = jnp.exp(al[..., None] - a) * dtc
        hs = jnp.exp(al)[..., None, None] * hs + jnp.einsum('bhs,bhsp,bhsn->bhpn', wgt, xc, Bc)
        return hs, y

    hs, y = lax.scan(step, h0, tuple(to_chunks(a, L) for a in (x, dt, Bh, Ch)))
    return from_chunks(y), hs

def gdn_scan(q, k, v, beta, g, S0):
    L = GDN_CHUNK
    qc, kc, vc, bc, gc = (to_chunks(a, L) for a in (q, k, v, beta, g))
    gc = jnp.cumsum(gc, axis=-1)
    diff = gc[..., :, None] - gc[..., None, :]
    incl = jnp.tril(jnp.ones((L, L), dtype=bool))
    strict = jnp.tril(jnp.ones((L, L), dtype=bool), -1)
    dec_strict = jnp.exp(jnp.where(strict, diff, -jnp.inf))
    dec_incl = jnp.exp(jnp.where(incl, diff, -jnp.inf))
    amat = jnp.eye(L, dtype=q.dtype) + dec_strict * jnp.einsum('...tk,...sk->...ts', kc, kc) * bc[..., None, :]
    u0 = lax.linalg.triangular_solve(amat, vc, left_side=True, lower=True, unit_diagonal=True)
    w = lax.linalg.triangular_solve(amat, jnp.exp(gc)[..., None] * kc, left_side=True, lower=True,
                                    unit_diagonal=True)
    pmat = dec_incl * jnp.einsum('...tk,...sk->...ts', qc, kc) * bc[..., None, :]

    def step(S, xs):
        qi, ki, u0i, wi, pi, gi, bi = xs
        u = u0i - jnp.einsum('bhtk,bhkv->bhtv', wi, S)
        o = jnp.exp(gi)[..., None] * jnp.einsum('bhtk,bhkv->bhtv', qi, S) + jnp.einsum('bhts,bhsv->bhtv', pi, u)
        gl = gi[..., -1]
        S = jnp.exp(gl)[..., None, None] * S + jnp.einsum('bhs,bhsk,bhsv->bhkv', jnp.exp(gl[..., None] - gi) * bi, ki, u)
        return S, o

    S, o = lax.scan(step, S0, (qc, kc, u0, w, pmat, gc, bc))
    return from_chunks(o), S

def even_mixer(h, P, e, ctx):
    B, T, _ = h.shape
    f32 = jnp.float32
    y = h @ P['w_in_even'][e]
    q, k, v, o, ig, fg, cq, ckv, kpe = split_cols(y, EVEN_SPLIT)
    qh = heads_first(q, ML_HEADS).astype(f32) * ML_DK ** -0.5
    kh = heads_first(k, ML_HEADS).astype(f32)
    vh = heads_first(v, ML_HEADS).astype(f32)
    logi = (ig.astype(f32).reshape(B, T, 2, ML_HEADS) + P['ml_i_bias'][e]).transpose(2, 0, 3, 1)
    logf = jax.nn.log_sigmoid(fg.astype(f32).reshape(B, T, 2, ML_HEADS) + P['ml_f_bias'][e]).transpose(2, 0, 3, 1)
    if ctx is None:
        C0 = jnp.zeros((B, 2, ML_HEADS, ML_DK, ML_DV), f32)
        n0 = jnp.zeros((B, 2, ML_HEADS, ML_DK), f32)
        m0 = jnp.zeros((B, 2, ML_HEADS), f32)
    else:
        C0, n0, m0 = ctx[2].astype(f32), ctx[3].astype(f32), ctx[4].astype(f32)
    hf, Cf, nf, mf = mlstm_scan(qh, kh, vh, logi[0], logf[0], C0[:, 0], n0[:, 0], m0[:, 0])
    hb, Cb, nb, mb = mlstm_scan(flip_t(qh), flip_t(kh), flip_t(vh), flip_t(logi[1]), flip_t(logf[1]),
                                C0[:, 1], n0[:, 1], m0[:, 1])
    hm = (hf + flip_t(hb)).transpose(0, 2, 1, 3)
    hm = rms_norm(hm, P['ml_norm'][e]).reshape(B, T, ML_HEADS * ML_DV) * jax.nn.sigmoid(o.astype(f32))
    cq = rms_norm(cq, P['mla_q_norm'][e])
    qf = (cq @ P['mla_w_uq'][e]).reshape(B, T, MLA_HEADS, MLA_NOPE + MLA_ROPE)
    q_nope, q_pe = qf[..., :MLA_NOPE], qf[..., MLA_NOPE:]
    ckv = rms_norm(ckv, P['mla_kv_norm'][e])
    if ctx is None:
        kv_all, kpe_all = ckv, kpe
    else:
        q_pe = axial_rope(q_pe)
        kv_all = jnp.concatenate([ctx[0].astype(ckv.dtype), ckv], axis=1)
        kpe_all = jnp.concatenate([ctx[1].astype(kpe.dtype), axial_rope(kpe[:, :, None, :])[:, :, 0]], axis=1)
    Tk = kv_all.shape[1]
    kvh = (kv_all @ P['mla_w_ukv'][e]).reshape(B, Tk, MLA_HEADS, MLA_NOPE + MLA_V)
    k_full = jnp.concatenate([kvh[..., :MLA_NOPE],
                              jnp.broadcast_to(kpe_all[:, :, None, :], (B, Tk, MLA_HEADS, MLA_ROPE))], axis=-1)
    q_full = jnp.concatenate([q_nope, q_pe], axis=-1)
    att = mla_attend(q_full, k_full, kvh[..., MLA_NOPE:]).reshape(B, T, MLA_OUT)
    out = jnp.concatenate([hm.astype(h.dtype), att.astype(h.dtype)], axis=-1) @ P['w_out_even'][e]
    if ctx is None:
        return out, (ckv, kpe, jnp.stack([Cf, Cb], axis=1), jnp.stack([nf, nb], axis=1), jnp.stack([mf, mb], axis=1))
    return out, None

def odd_mixer(h, P, oi, ctx):
    B, T, _ = h.shape
    f32 = jnp.float32
    y = h @ P['w_in_odd'][oi]
    z_s, xbc, dt, qkv, z_g, ga, gb = split_cols(y, ODD_SPLIT)
    if ctx is None:
        h0 = jnp.zeros((B, 2, SSD_HEADS, SSD_P, SSD_N), f32)
        S0 = jnp.zeros((B, 2, GDN_HEADS, GDN_DK, GDN_DV), f32)
    else:
        h0, S0 = ctx[0].astype(f32), ctx[1].astype(f32)
    xbc = centred_dwconv(xbc, P['ssd_conv_w'][oi], P['ssd_conv_b'][oi]).astype(f32)
    xs_, Bm, Cm = split_cols(xbc, [SSD_W, SSD_BC, SSD_BC])
    xh = heads_first(xs_, SSD_HEADS)
    rep = SSD_HEADS // SSD_GROUPS
    Bh = jnp.repeat(heads_first(Bm, SSD_GROUPS), rep, axis=1)
    Ch = jnp.repeat(heads_first(Cm, SSD_GROUPS), rep, axis=1)
    dts = jax.nn.softplus(dt.astype(f32).reshape(B, T, 2, SSD_HEADS) + P['ssd_dt_bias'][oi]).transpose(2, 0, 3, 1)
    A = -jnp.exp(P['ssd_A_log'][oi].astype(f32))
    yf, sf = ssd_scan(xh, dts[0], A[0], Bh, Ch, h0[:, 0])
    yb, sb = ssd_scan(flip_t(xh), flip_t(dts[1]), A[1], flip_t(Bh), flip_t(Ch), h0[:, 1])
    ys = yf + flip_t(yb) + P['ssd_D'][oi][None, :, None, None] * xh
    ys = ys.transpose(0, 2, 1, 3).reshape(B, T, SSD_W)
    ys = rms_norm(ys * jax.nn.silu(z_s.astype(f32)), P['ssd_norm'][oi])
    qkv = centred_dwconv(qkv, P['gdn_conv_w'][oi], P['gdn_conv_b'][oi]).astype(f32)
    qg, kg, vg = split_cols(qkv, [GDN_W, GDN_W, GDN_HEADS * GDN_DV])
    qg = l2_norm(heads_first(qg, GDN_HEADS)) * GDN_DK ** -0.5
    kg = l2_norm(heads_first(kg, GDN_HEADS))
    vg = heads_first(vg, GDN_HEADS)
    beta = jax.nn.sigmoid(gb.astype(f32).reshape(B, T, 2, GDN_HEADS)).transpose(2, 0, 3, 1)
    gdec = -jnp.exp(P['gdn_A_log'][oi].astype(f32))[:, None, :, None] * jax.nn.softplus(
        ga.astype(f32).reshape(B, T, 2, GDN_HEADS) + P['gdn_dt_bias'][oi]).transpose(2, 0, 3, 1)
    of, Sf = gdn_scan(qg, kg, vg, beta[0], gdec[0], S0[:, 0])
    ob, Sb = gdn_scan(flip_t(qg), flip_t(kg), flip_t(vg), flip_t(beta[1]), flip_t(gdec[1]), S0[:, 1])
    og = (of + flip_t(ob)).transpose(0, 2, 1, 3)
    og = rms_norm(og, P['gdn_norm'][oi]) * jax.nn.silu(z_g.astype(f32).reshape(B, T, GDN_HEADS, GDN_DV))
    og = og.reshape(B, T, GDN_HEADS * GDN_DV)
    out = jnp.concatenate([ys, og], axis=-1).astype(h.dtype) @ P['w_out_odd'][oi]
    if ctx is None:
        return out, (jnp.stack([sf, sb], axis=1), jnp.stack([Sf, Sb], axis=1))
    return out, None

def hier_moe(h, P, l):
    B, T, D = h.shape
    f32 = jnp.float32
    x = h.reshape(B * T, D)
    glog = (x @ P['moe_w_group'][l] + P['moe_b_group'][l]).astype(f32)
    gprob = jax.nn.softmax(glog, axis=-1)
    gsel = jnp.argmax(glog, axis=-1)
    gw = jnp.take_along_axis(gprob, gsel[:, None], axis=-1)
    elog = (x @ P['moe_w_expert'][l] + P['moe_b_expert'][l]).astype(f32).reshape(-1, MOE_GROUPS, MOE_PER_GROUP)
    elog = jnp.take_along_axis(elog, gsel[:, None, None], axis=1)[:, 0]
    tv, ti = lax.top_k(elog, MOE_TOPK)
    tw = jax.nn.softmax(tv, axis=-1) * gw
    eid = gsel[:, None] * MOE_PER_GROUP + ti
    combine = jnp.einsum('nk,nke->ne', tw, jax.nn.one_hot(eid, MOE_EXPERTS, dtype=f32))
    hg = jnp.einsum('nd,edf->nef', x, P['moe_w_gate'][l])
    hu = jnp.einsum('nd,edf->nef', x, P['moe_w_up'][l])
    act = jax.nn.silu(hg) * hu * combine[..., None].astype(x.dtype)
    y = jnp.einsum('nef,efd->nd', act, P['moe_w_down'][l])
    return y.reshape(B, T, D)

def trunk_layer(x, mod, P, l, ctx):
    sh1, sc1, g1, sh2, sc2, g2 = jnp.split(mod, 6, axis=-1)
    h = rms_norm(x, P['norm_mix'][l]) * (1 + sc1) + sh1
    if l % 2 == 0:
        out, st = even_mixer(h, P, l // 2, ctx)
    else:
        out, st = odd_mixer(h, P, l // 2, ctx)
    x = x + g1 * out
    h = rms_norm(x, P['norm_ffn'][l]) * (1 + sc2) + sh2
    x = x + g2 * hier_moe(h, P, l)
    return x, st

def setup_inputs(seed: int = 0) -> dict:
    key = jax.random.key(seed)
    ks = iter(jax.random.split(key, 64))
    f32 = jnp.float32
    D = D_MODEL

    def nrm(shape, scale):
        return jax.random.normal(next(ks), shape, f32) * scale

    def gain(shape):
        return 1.0 + nrm(shape, 0.05)

    def dt_bias(shape):
        dt = jnp.exp(jax.random.uniform(next(ks), shape, f32, math.log(1e-3), math.log(1e-1)))
        return dt + jnp.log(-jnp.expm1(-dt))

    def a_log(shape):
        return jnp.log(jax.random.uniform(next(ks), shape, f32, 1.0, 16.0))

    return {
        'x_prompt': nrm((BATCH, SEQ, D), 1.0),
        'x_sample': nrm((DEC_BATCH, DEC_SEQ, D), 1.0),
        'c': nrm((DEC_BATCH, D), 1.0),
        'cache_mla_kv': nrm((DEC_BATCH, N_EVEN, PAST_LEN, MLA_KV_RANK), 1.0),
        'cache_mla_krope': nrm((DEC_BATCH, N_EVEN, PAST_LEN, MLA_ROPE), 1.0),
        'state_mlstm_C': nrm((DEC_BATCH, N_EVEN, 2, ML_HEADS, ML_DK, ML_DV), 1.0),
        'state_mlstm_n': nrm((DEC_BATCH, N_EVEN, 2, ML_HEADS, ML_DK), 1.0),
        'state_mlstm_m': nrm((DEC_BATCH, N_EVEN, 2, ML_HEADS), 1.0),
        'state_ssd': nrm((DEC_BATCH, N_ODD, 2, SSD_HEADS, SSD_P, SSD_N), 0.1),
        'state_gdn': nrm((DEC_BATCH, N_ODD, 2, GDN_HEADS, GDN_DK, GDN_DV), 0.3),
        'c_ctx': nrm((D,), 1.0),
        'ada_w': nrm((DEPTH, D, 6 * D), D ** -0.5),
        'ada_b': nrm((DEPTH, 6 * D), 0.02),
        'norm_mix': gain((DEPTH, D)),
        'norm_ffn': gain((DEPTH, D)),
        'w_in_even': nrm((N_EVEN, D, IN_EVEN), D ** -0.5),
        'ml_i_bias': nrm((N_EVEN, 2, ML_HEADS), 0.1),
        'ml_f_bias': 3.0 + nrm((N_EVEN, 2, ML_HEADS), 0.1),
        'ml_norm': gain((N_EVEN, ML_HEADS, ML_DV)),
        'mla_q_norm': gain((N_EVEN, MLA_Q_RANK)),
        'mla_w_uq': nrm((N_EVEN, MLA_Q_RANK, MLA_HEADS * (MLA_NOPE + MLA_ROPE)), MLA_Q_RANK ** -0.5),
        'mla_kv_norm': gain((N_EVEN, MLA_KV_RANK)),
        'mla_w_ukv': nrm((N_EVEN, MLA_KV_RANK, MLA_HEADS * (MLA_NOPE + MLA_V)), MLA_KV_RANK ** -0.5),
        'w_out_even': nrm((N_EVEN, OUT_EVEN, D), OUT_EVEN ** -0.5),
        'w_in_odd': nrm((N_ODD, D, IN_ODD), D ** -0.5),
        'ssd_conv_w': nrm((N_ODD, CONV_W, SSD_CONV_CH), CONV_W ** -0.5),
        'ssd_conv_b': nrm((N_ODD, SSD_CONV_CH), 0.02),
        'ssd_dt_bias': dt_bias((N_ODD, 2, SSD_HEADS)),
        'ssd_A_log': a_log((N_ODD, 2, SSD_HEADS)),
        'ssd_D': 1.0 + nrm((N_ODD, SSD_HEADS), 0.1),
        'ssd_norm': gain((N_ODD, SSD_W)),
        'gdn_conv_w': nrm((N_ODD, CONV_W, GDN_CONV_CH), CONV_W ** -0.5),
        'gdn_conv_b': nrm((N_ODD, GDN_CONV_CH), 0.02),
        'gdn_dt_bias': dt_bias((N_ODD, 2, GDN_HEADS)),
        'gdn_A_log': a_log((N_ODD, 2, GDN_HEADS)),
        'gdn_norm': gain((N_ODD, GDN_DV)),
        'w_out_odd': nrm((N_ODD, OUT_ODD, D), OUT_ODD ** -0.5),
        'moe_w_group': nrm((DEPTH, D, MOE_GROUPS), D ** -0.5),
        'moe_b_group': nrm((DEPTH, MOE_GROUPS), 0.01),
        'moe_w_expert': nrm((DEPTH, D, MOE_EXPERTS), D ** -0.5),
        'moe_b_expert': nrm((DEPTH, MOE_EXPERTS), 0.01),
        'moe_w_gate': nrm((DEPTH, MOE_EXPERTS, D, MOE_FF), D ** -0.5),
        'moe_w_up': nrm((DEPTH, MOE_EXPERTS, D, MOE_FF), D ** -0.5),
        'moe_w_down': nrm((DEPTH, MOE_EXPERTS, MOE_FF, D), MOE_FF ** -0.5),
        'norm_final': gain((D,)),
    }

def reference(x_prompt, x_sample, c, cache_mla_kv, cache_mla_krope, state_mlstm_C, state_mlstm_n,
              state_mlstm_m, state_ssd, state_gdn, c_ctx, ada_w, ada_b, norm_mix, norm_ffn,
              w_in_even, ml_i_bias, ml_f_bias, ml_norm, mla_q_norm, mla_w_uq, mla_kv_norm, mla_w_ukv,
              w_out_even, w_in_odd, ssd_conv_w, ssd_conv_b, ssd_dt_bias, ssd_A_log, ssd_D, ssd_norm,
              gdn_conv_w, gdn_conv_b, gdn_dt_bias, gdn_A_log, gdn_norm, w_out_odd,
              moe_w_group, moe_b_group, moe_w_expert, moe_b_expert, moe_w_gate, moe_w_up, moe_w_down,
              norm_final):
    P = dict(norm_mix=norm_mix, norm_ffn=norm_ffn, w_in_even=w_in_even, ml_i_bias=ml_i_bias,
             ml_f_bias=ml_f_bias, ml_norm=ml_norm, mla_q_norm=mla_q_norm, mla_w_uq=mla_w_uq,
             mla_kv_norm=mla_kv_norm, mla_w_ukv=mla_w_ukv, w_out_even=w_out_even, w_in_odd=w_in_odd,
             ssd_conv_w=ssd_conv_w, ssd_conv_b=ssd_conv_b, ssd_dt_bias=ssd_dt_bias, ssd_A_log=ssd_A_log,
             ssd_D=ssd_D, ssd_norm=ssd_norm, gdn_conv_w=gdn_conv_w, gdn_conv_b=gdn_conv_b,
             gdn_dt_bias=gdn_dt_bias, gdn_A_log=gdn_A_log, gdn_norm=gdn_norm, w_out_odd=w_out_odd,
             moe_w_group=moe_w_group, moe_b_group=moe_b_group, moe_w_expert=moe_w_expert,
             moe_b_expert=moe_b_expert, moe_w_gate=moe_w_gate, moe_w_up=moe_w_up, moe_w_down=moe_w_down)
    x = x_prompt
    even_st, odd_st = [], []
    for l in range(DEPTH):
        mod = (jax.nn.silu(c_ctx) @ ada_w[l] + ada_b[l])[None, None, :]
        x, st = trunk_layer(x, mod, P, l, None)
        if l % 2 == 0:
            even_st.append(st)
        else:
            odd_st.append(st)
    y_prompt = rms_norm(x, norm_final)
    new_mla_kv = jnp.stack([s[0] for s in even_st], axis=1)
    new_mla_krope = jnp.stack([s[1] for s in even_st], axis=1)
    new_mlstm_C = jnp.stack([s[2] for s in even_st], axis=1)
    new_mlstm_n = jnp.stack([s[3] for s in even_st], axis=1)
    new_mlstm_m = jnp.stack([s[4] for s in even_st], axis=1)
    new_ssd = jnp.stack([s[0] for s in odd_st], axis=1)
    new_gdn = jnp.stack([s[1] for s in odd_st], axis=1)
    x = x_sample
    for l in range(DEPTH):
        mod = (jax.nn.silu(c) @ ada_w[l] + ada_b[l])[:, None, :]
        if l % 2 == 0:
            e = l // 2
            ctx = (cache_mla_kv[:, e], cache_mla_krope[:, e], state_mlstm_C[:, e], state_mlstm_n[:, e],
                   state_mlstm_m[:, e])
        else:
            oi = l // 2
            ctx = (state_ssd[:, oi], state_gdn[:, oi])
        x, _ = trunk_layer(x, mod, P, l, ctx)
    y_sample = rms_norm(x, norm_final)
    return (y_prompt, y_sample, new_mla_kv, new_mla_krope, new_mlstm_C, new_mlstm_n, new_mlstm_m, new_ssd, new_gdn)


_drawn_inputs = setup_inputs


def setup_inputs(seed=0):
    import zlib

    import numpy as np

    out = dict(_drawn_inputs(seed))
    spreads = {}
    factors = {'state_mlstm_C': 4.916,
     'state_mlstm_n': 7.606,
     'state_mlstm_m': 4.783,
     'mla_q_norm': 8.0,
     'gdn_conv_b': 2.674}
    for name, (base, spread) in spreads.items():
        noise = np.random.default_rng([zlib.crc32(name.encode()), seed]).standard_normal(out[name].shape)
        drawn = base * np.exp(spread * noise) if base else spread * noise
        out[name] = __import__('jax').numpy.asarray(drawn.astype(out[name].dtype))
    for name, factor in factors.items():
        out[name] = (out[name] * factor).astype(out[name].dtype)
    return out
```

```python
from contextlib import ExitStack

import numpy as np

import concourse.bass as bass
from concourse import mybir

F32 = mybir.dt.float32
ALU = mybir.AluOpType
ACT = mybir.ActivationFunctionType
AX = mybir.AxisListType.X

P = 128
D = 1024
KD = D // P
PROMPT, SAMPLE = 128, 256
T = PROMPT + SAMPLE
TILES = T // P
SEGS = ((0, 0, PROMPT), (1, PROMPT, T))
EPS = 1e-6
NEG = -1e30

ML_H, DK = 4, 128
Q_RANK, KV_RANK, NOPE, ROPE, V_DIM, MLA_H = 384, 256, 64, 32, 64, 8
QK_DIM = NOPE + ROPE
PAST = 128
KEYS = PROMPT + PAST + SAMPLE
EVEN_TAIL = 2048
IN_EVEN = EVEN_TAIL + 16 + Q_RANK + KV_RANK + ROPE
TAIL = IN_EVEN - EVEN_TAIL
CQ0, CKV0, KPE0 = 16, 16 + Q_RANK, 16 + Q_RANK + KV_RANK

SSD_H, SSD_P, SSD_N = 8, 64, 128
GDN_H = 4
SSD_CH, GDN_CH, CONV_W = 1024, 1536, 5
Z_S, XBC, DT, QKV, Z_G, GA = 0, 512, 1536, 1552, 3088, 3600
IN_ODD = 3616
CONV_TILES = (SSD_CH + GDN_CH) // P
PAD = CONV_W // 2
CIN = PROMPT + SAMPLE + 4 * PAD
COUT = CIN - 2 * PAD
CO = (0, PROMPT + 2 * PAD, PROMPT + 2 * PAD + P)

GROUPS, EXPERTS, FF = 4, 32, 256
ROUTES = GROUPS + EXPERTS

BANKS = 8
RING = 3
SLOT = 4096

C_ID, C_ONE, C_UP, C_LO, C_NUP, C_NLO = (i * P for i in range(6))
C_LVL = 6 * P
C_RANK = C_LVL + 7 * P
C_COS = C_RANK + EXPERTS
C_SIN = C_COS + SAMPLE
C_ROT = C_SIN + SAMPLE
C_ALL = C_ROT + ROPE


def const_table():
    c = np.zeros((P, C_ALL), np.float32)
    row, col = np.arange(P)[:, None], np.arange(P)[None, :]
    c[:, C_ID:C_ID + P] = row == col
    c[:, C_ONE:C_ONE + P] = 1.0
    c[:, C_UP:C_UP + P] = col >= row
    c[:, C_LO:C_LO + P] = col <= row
    c[:, C_NUP:C_NUP + P] = np.where(col >= row, 0.0, NEG)
    c[:, C_NLO:C_NLO + P] = np.where(col <= row, 0.0, NEG)
    for n in range(7):
        b = 1 << n
        c[:, C_LVL + n * P:C_LVL + (n + 1) * P] = (row // (2 * b) == col // (2 * b)) & (row // b != col // b)
    c[:, C_RANK:C_RANK + EXPERTS] = EXPERTS - np.arange(EXPERTS)
    half, nf = ROPE // 2, ROPE // 4
    inv = np.float32(10000.0) ** (-np.arange(nf, dtype=np.float32) / np.float32(nf))
    t = np.arange(SAMPLE)
    for part, pos in ((0, t // 64), (1, t % 64)):
        ang = (pos.astype(np.float32)[None, :] * inv[:, None]).astype(np.float32)
        for two in range(2):
            r = NOPE + part * half + two * nf
            c[r:r + nf, C_COS:C_COS + SAMPLE] = np.cos(ang)
            c[r:r + nf, C_SIN:C_SIN + SAMPLE] = np.sin(ang)
        for f in range(nf):
            a, b = part * half + f, part * half + nf + f
            c[NOPE + b, C_ROT + a] = -1.0
            c[NOPE + a, C_ROT + b] = 1.0
    return c


def scan_units():
    return [(0, 0), (1, 0), (0, 1), (1, 2), (0, 2), (1, 1)]


def first_chunk(d, c):
    return (d, c) in ((0, 1), (1, 2))


def plan_jobs():
    jobs = [("xt", k) for k in range(KD)] + [("cols",)]
    jobs += [("mod", l, i) for l in range(2) for i in range(6)]

    def norm(n):
        return [("ss", n)]

    jobs += norm(0)
    jobs += [("qT", h) for h in range(4)] + [("kT", h) for h in range(4)]
    jobs += [(n, c) for n in ("kN", "vN", "oN", "ta", "tb") for c in range(TILES)]
    jobs += [("cum", 0)]
    for u, (d, c) in enumerate(scan_units()):
        jobs += [(n, u) for n in ("R", "MR", "SK", "N1", "DN")]
        if c:
            jobs += [("N2", u)]
        if c == 0 or first_chunk(d, c):
            jobs += [("CU", u), ("NU", u)]
    jobs += [("hmT", h) for h in range(4)]
    jobs += [("cqT", k) for k in range(3)] + [("kvT", k) for k in range(2)] + [("kpT",), ("kpR",)]
    jobs += [("qf", h) for h in range(MLA_H)] + [("qR", i) for i in range(4)]
    jobs += [("kn", h) for h in range(MLA_H)] + [("vv", k) for k in range(4)]
    for c in range(TILES):
        for h in range(MLA_H):
            jobs += [("sc", c, h), ("pT", c, h)]
            if h % 2:
                jobs += [("pv", c, h // 2)]
    jobs += [("o", 0, m) for m in range(KD)]
    jobs += norm(1) + [("rt", 0)] + [("yt", 0, m) for m in range(KD)]
    jobs += norm(2)
    jobs += [("zs", c) for c in range(TILES)] + [("xb", i) for i in range(CONV_TILES)]
    jobs += [("zg", c) for c in range(TILES)] + [("dg",)]
    jobs += [("l2", i) for i in range(8)]
    jobs += [(n, c) for c in range(TILES) for n in ("tx", "tB", "tk", "tv")]
    jobs += [("cum", 1)] + [("h0T", d) for d in range(2)]
    for u, (d, c) in enumerate(scan_units()):
        for g in range(2):
            jobs += [("Es", u, g), ("GB", u, g)]
        jobs += [("Y1", u)]
        if c:
            jobs += [("Y2", u)]
        if c == 0 or first_chunk(d, c):
            jobs += [("HU", u)]
        jobs += [("Eg", u), ("KK", u), ("KQ", u), ("X0", u)]
        for n in range(1, 7):
            jobs += [("T1", u, n), ("XT", u, n)] + [("XX", u, n)] * (n < 6)
        if c:
            jobs += [("KS", u)]
        jobs += [("U", u), ("O1", u)]
        if c:
            jobs += [("O2", u)]
        if c == 0 or first_chunk(d, c):
            jobs += [("SU", u)]
        if c == 0:
            jobs += [("hT", d)]
    jobs += [("mT", f) for f in range(8)]
    jobs += [("o", 1, m) for m in range(KD)]
    jobs += norm(3) + [("rt", 1)] + [("yt", 1, m) for m in range(KD)]
    jobs += norm(4) + [("fin", c, k // 4) for c in range(TILES) for k in range(0, KD, 4)]
    return jobs


def plan_weights():
    items = []
    for l in range(2):
        for i in range(6):
            items += [("ada", (l, i, half), ("mod", l, i)) for half in range(2)]
    last = [("qT", 3), ("kN", 2), ("vN", 2), ("oN", 2), ("ta", 2), ("tb", 2)]
    items += [("even", n, last[n]) for n in range(6)]
    items += [("out", (0, half), ("o", 0, KD - 1)) for half in range(2)]
    last = [("zs", 2), ("xb", 3), ("xb", 7), ("xb", 11), ("xb", 15), ("xb", 19), ("zg", 2), ("dg",)]
    items += [("odd", n, last[n]) for n in range(8)]
    items += [("out", (1, half), ("o", 1, KD - 1)) for half in range(2)]
    return items


ODD_COLS = [(Z_S, 512), (XBC, 512), (XBC + 512, 512), (QKV, 512), (QKV + 512, 512), (QKV + 1024, 512),
            (Z_G, 512)]


def build(nc, a, o):
    jobs = plan_jobs()
    job_at = {j: n for n, j in enumerate(jobs)}
    assert len(job_at) == len(jobs)
    weights = plan_weights()
    weight_at = {(w, what): n for n, (w, what, _) in enumerate(weights)}
    units = scan_units()
    es = ExitStack()
    with es:
        sems = {}

        def S(name):
            if name not in sems:
                sems[name] = es.enter_context(nc.semaphore(name))
            return sems[name]

        def sb(name, shape):
            return es.enter_context(nc.sbuf_tensor(name, shape, F32))

        psum = es.enter_context(nc.psum_tensor("psum", [P, BANKS, 512], F32))
        full = [S(f"bank{b}_full") for b in range(BANKS)]
        free = [S(f"bank{b}_read") for b in range(BANKS)]

        def bank(*job):
            return psum[:, job_at[job] % BANKS, :]

        def computed(*job):
            n = job_at[job]
            return full[n % BANKS], n // BANKS + 1

        def taken(*job):
            n = job_at[job]
            return free[n % BANKS], n // BANKS + 1

        def bc(ap, axis, shape):
            return ap.unsqueeze(axis).to_broadcast(shape)

        def heads(ap, h):
            return ap.rearrange("p (h n) -> p h n", h=h)

        cst = sb("cst", [P, C_ALL])
        ident, ones = cst[:, C_ID:C_ID + P], cst[:, C_ONE:C_ONE + P]
        cum01 = (cst[:, C_UP:C_UP + P], cst[:, C_LO:C_LO + P])
        neg_st = (cst[:, C_NUP:C_NUP + P], cst[:, C_NLO:C_NLO + P])
        neg_ts = (neg_st[1], neg_st[0])
        lvl = [cst[:, C_LVL + n * P:C_LVL + (n + 1) * P] for n in range(7)]
        rank = cst[:, C_RANK:C_RANK + EXPERTS]
        cosT, sinT = cst[:, C_COS:C_COS + SAMPLE], cst[:, C_SIN:C_SIN + SAMPLE]
        rot = cst[:, C_ROT:C_ROT + ROPE]

        xT = sb("xT", [P, KD, T])
        hT = sb("hT", [P, KD, T])
        mix = sb("mix", [P, KD, T])
        rB = sb("rB", [P, T])
        ring = sb("ring", [P, RING, SLOT])
        cc = sb("cc", [P, 2, KD])
        sil = sb("sil", [P, 2, KD])
        adab = sb("adab", [P, 2, 6, KD])
        gains = sb("gains", [P, 5, KD])
        modT = sb("modT", [P, 2, 6, KD, 2])
        amp = sb("amp", [P, 2, 2, KD, 2])
        rows = sb("rows", [P, P])
        colsT = sb("colsT", [P, P])
        wr = sb("wr", [P, 2, KD, ROUTES])
        br = sb("br", [P, 2, ROUTES])
        route = sb("route", [P, 12, TILES, ROUTES])
        comb = sb("comb", [P, TILES, EXPERTS])
        small = sb("small", [P, 1024])
        bias_e = sb("bias_e", [P, 16])
        bias_o = sb("bias_o", [P, 2, 12])
        alog = sb("alog", [P, 2, 12])
        dskip = sb("dskip", [P, SSD_H])
        mprev0 = sb("mprev0", [P, 8])
        eps = sb("eps", [P, 1])
        gain_row = sb("gain_row", [P, 1152])
        gml, gq, gkv = gain_row[:, 0:512], gain_row[:, 512:896], gain_row[:, 896:1152]
        gssd, ggdn = gain_row[:, 0:512], gain_row[:, 512:640]

        room = (nc.sbuf_usable_end - nc.sbuf_base) // 4 - 64
        arena = sb("arena", [P, room])
        used = [0, 0]

        def carve(n, at=None):
            if at is None:
                at = used[0]
                used[0] += n
            assert at + n <= room, (at, n, room)
            used[1] = max(used[1], at + n)
            return arena[:, at:at + n]

        gu = [carve(2 * KD * FF).rearrange("p (w k f) -> p w k f", w=2, k=KD) for _ in range(2)]
        dn = [carve(2 * D).rearrange("p (j d) -> p j d", j=2) for _ in range(2)]
        sg = carve(2 * T).rearrange("p (j t) -> p j t", j=2)
        actT = [carve(2 * T).rearrange("p (j t) -> p j t", j=2) for _ in range(2)]
        yacc = mix[:].rearrange("p k t -> p (k t)").rearrange("p (c d) -> p c d", c=TILES)

        used[0] = 0
        tail = carve(TILES * TAIL).rearrange("p (c n) -> p c n", c=TILES)
        w_ukv = carve(2 * 1024).rearrange("p (k n) -> p k n", k=2)
        w_uq = carve(3 * 768).rearrange("p (k n) -> p k n", k=3)
        kpin = carve(QK_DIM)
        kvpast = carve(KV_RANK)
        base = used[0]
        qT = carve(4 * T).rearrange("p (h t) -> p h t", h=4)
        kT = carve(4 * T).rearrange("p (h t) -> p h t", h=4)
        kN = carve(TILES * 512).rearrange("p (c n) -> p c n", c=TILES)
        vN = carve(TILES * 512).rearrange("p (c n) -> p c n", c=TILES)
        oS = carve(TILES * 512).rearrange("p (c n) -> p c n", c=TILES)
        hsum = carve(TILES * 512).rearrange("p (c n) -> p c n", c=TILES)
        mlC = carve(4 * 512).rearrange("p (s d n) -> p s d n", s=2, d=2)
        mln = carve(16).rearrange("p (s d n) -> p s d n", s=2, d=2)
        Rm, mrt, ET, ST, num, kw, t512 = (carve(512) for _ in range(7))
        used[0] = base
        cqn = carve(TILES * Q_RANK).rearrange("p (c n) -> p c n", c=TILES)
        ckn = carve(TILES * KV_RANK).rearrange("p (c n) -> p c n", c=TILES)
        sqt = carve(TILES * Q_RANK)
        cqT = carve(3 * T).rearrange("p (k t) -> p k t", k=3)
        kvT = carve(2 * KEYS).rearrange("p (k t) -> p k t", k=2)
        qfT = carve(MLA_H * T).rearrange("p (h t) -> p h t", h=MLA_H)
        kfT = carve(MLA_H * KEYS).rearrange("p (h t) -> p h t", h=MLA_H)
        vv = carve(4 * 512).rearrange("p (k n) -> p k n", k=4)
        kpe = carve(KEYS)
        rtmp = carve(512)
        pr = carve(2 * T).rearrange("p (b t) -> p b t", b=2)
        prT = carve(2 * T).rearrange("p (b t) -> p b t", b=2)

        used[0] = 0
        conv = carve(CONV_TILES * COUT).rearrange("p (i t) -> p i t", i=CONV_TILES)
        zs = carve(TILES * 512).rearrange("p (c n) -> p c n", c=TILES)
        zg = carve(TILES * 512).rearrange("p (c n) -> p c n", c=TILES)
        dg = carve(TILES * 32).rearrange("p (c n) -> p c n", c=TILES)
        spin, sp, lg, cb, tot, ecb, etot, edif, ncb = (
            carve(72).rearrange("p (d c h) -> p d c h", d=2, c=TILES) for _ in range(9))
        beta, edb = (carve(24).rearrange("p (d c h) -> p d c h", d=2, c=TILES) for _ in range(2))
        wA = carve(24)
        base = used[0]
        cin = carve(CONV_TILES * CIN).rearrange("p (i t) -> p i t", i=CONV_TILES)
        used[0] = base
        l2 = carve(8 * COUT).rearrange("p (i t) -> p i t", i=8)
        used[0] = base
        xN = carve(TILES * 512).rearrange("p (c n) -> p c n", c=TILES)
        BN = carve(TILES * 256).rearrange("p (c n) -> p c n", c=TILES)
        hsT = carve(4 * 512).rearrange("p (s d n) -> p s d n", s=2, d=2)
        hsO = carve(2 * 512).rearrange("p (d n) -> p d n", d=2)
        Sg = carve(4 * 512).rearrange("p (s d n) -> p s d n", s=2, d=2)
        G = carve(1024)
        h0 = G.rearrange("p (d i n) -> p d i n", d=2, i=4)
        E1, xdt, xw, y2, EB, PT = (carve(512) for _ in range(6))
        AT, XT, X, LT, TT, Rg, U, Uw = (ring[:, 0, 512 * n:512 * n + 512] for n in range(8))
        hflat = hT[:].rearrange("p k t -> p (k t)")
        gk = hflat[:, 0:1536].rearrange("p (c n) -> p c n", c=TILES)
        gv = hflat[:, 1536:3072].rearrange("p (c n) -> p c n", c=TILES)
        ysum = conv[:, 0:4, :].rearrange("p i t -> p (i t)")[:, 0:1536].rearrange("p (c n) -> p c n", c=TILES)
        ogsum = conv[:, 16:20, :].rearrange("p i t -> p (i t)")[:, 0:1536].rearrange("p (c n) -> p c n", c=TILES)

        def sm(at, n):
            return small[:, at:at + n]

        li = sm(0, 24).rearrange("p (d c h) -> p d c h", d=2, c=TILES)
        lf = sm(24, 24).rearrange("p (d c h) -> p d c h", d=2, c=TILES)
        tf = sm(48, 24).rearrange("p (d c h) -> p d c h", d=2, c=TILES)
        bcum = sm(72, 24).rearrange("p (d c h) -> p d c h", d=2, c=TILES)
        btot = sm(96, 24).rearrange("p (d c h) -> p d c h", d=2, c=TILES)
        rr = sm(120, 24).rearrange("p (d c h) -> p d c h", d=2, c=TILES)
        mst = sm(144, 16).rearrange("p (s d h) -> p s d h", s=2, d=2)
        mx, mxa, nmr, aexp, emq, dec, wk, den = (sm(160 + 4 * n, 4) for n in range(8))
        den2 = sm(192, 4)
        nmall = sm(196, 4)
        ms12 = sm(200, 12)
        ms3 = sm(212, 3)
        ms6 = sm(216, 3)
        nb = sm(220, 2)
        rs = sm(222, 2)
        rsi = sm(224, 2)
        nbm = sm(226, 2)

        block = es.enter_context(nc.Block())

        def every(eng):
            count = {}

            def done(ins, name):
                count[name] = count.get(name, 0) + 1
                ins.then_inc(S(name), 1)
                eng.wait_ge(S(name), count[name])

            def take(ins, *job):
                sem, n = taken(*job)
                ins.then_inc(sem, 1)
                eng.wait_ge(sem, n)

            return done, take

        @block.sync
        def _(sp):
            for c in range(TILES):
                src = a["x_prompt"][0] if c == 0 else a["x_sample"][0, (c - 1) * P:c * P, :]
                sp.dma_start(ring[:, 2, c * D:(c + 1) * D], src).then_inc(S("x_in"), 16)
            ring_full = [S(f"ring{n}_full") for n in range(RING)]

            def load(n):
                kind, what, _ = weights[n]
                slot = ring[:, n % RING, :]
                if n >= RING:
                    sp.wait_ge(*computed(*weights[n - RING][2]))
                elif n == 2:
                    sp.wait_ge(*taken("xt", KD - 1))
                if kind == "ada":
                    l, i, half = what
                    src = a["ada_w"][l].rearrange("(p k) n -> p k n", k=KD)[:, 4 * half:4 * half + 4, i * D:(i + 1) * D]
                    dst = slot.rearrange("p (k n) -> p k n", k=4)
                elif kind == "out":
                    l, half = what
                    w = a["w_out_even" if l == 0 else "w_out_odd"][0]
                    src = w.rearrange("(k p) n -> p k n", p=P)[:, 4 * half:4 * half + 4, :]
                    dst = slot.rearrange("p (k n) -> p k n", k=4)
                elif kind == "even":
                    w = a["w_in_even"][0].rearrange("(p k) n -> p k n", k=KD)
                    n0, n1 = what * 512, min(what * 512 + 512, IN_EVEN)
                    src = w[:, :, n0:n1]
                    dst = slot.rearrange("p (k n) -> p k n", k=KD)[:, :, 0:n1 - n0]
                else:
                    w = a["w_in_odd"][0].rearrange("(p k) n -> p k n", k=KD)
                    dst = slot.rearrange("p (k n) -> p k n", k=KD)
                    if what < 7:
                        n0, width = ODD_COLS[what]
                        src = w[:, :, n0:n0 + width]
                    else:
                        sp.dma_start(dst[:, :, 0:16], w[:, :, DT:DT + 16]).then_inc(ring_full[n % RING], 16)
                        src, dst = w[:, :, GA:GA + 16], dst[:, :, 16:32]
                sp.dma_start(dst, src).then_inc(ring_full[n % RING], 16)

            def experts(l):
                wg, wu, wd = (a[n][l] for n in ("moe_w_gate", "moe_w_up", "moe_w_down"))

                def load_expert(e, u):
                    for w, m in ((0, wg), (1, wu)):
                        sp.dma_start(gu[u][:, w], m[bass.ds(e, 1)].rearrange("e (p k) f -> p (e k) f", k=KD))\
                          .then_inc(S(f"gu{u}_full"), 16)
                    return lambda: sp.dma_start(dn[u], wd[bass.ds(e, 1)].rearrange("e (p j) d -> p (e j) d", j=2))\
                        .then_inc(S(f"dn{u}_full"), 16)

                sp.wait_ge(S("x"), 2 * l + 2)
                if l == 0:
                    sp.wait_ge(S("even_out"), 32)
                else:
                    sp.wait_ge(S("odd_out"), 64)
                for u in range(2):
                    load_expert(u, u)()
                with sp.Fori(1, EXPERTS // 2) as i:
                    for u in range(2):
                        e = i * 2 + u
                        sp.wait_ge(S("gu_computed"), e * 2 + (2 * EXPERTS * l - 2))
                        down = load_expert(e, u)
                        sp.wait_ge(S("y_computed"), e * 6 + (6 * EXPERTS * l - 6))
                        down()

            n_even = weight_at[("out", (0, 1))] + 1
            for n in range(n_even):
                load(n)
            experts(0)
            for n in range(n_even, len(weights)):
                load(n)
            experts(1)

        @block.gpsimd
        def _(pool):
            count = [0]

            def small_load(dst, src):
                pool.dma_start(dst, src).then_inc(S("small_in"), 16)
                count[0] += 1

            def along(v):
                return v.partition_broadcast(P)

            with nc.allow_non_contiguous_dma(reason="small vectors"):
                small_load(cst[:], a["consts"])
                small_load(cc[:, 0, :], a["c_ctx"].rearrange("(p k) -> p k", k=KD))
                small_load(cc[:, 1, :], a["c"][0].rearrange("(p k) -> p k", k=KD))
                for l in range(2):
                    small_load(adab[:, l], a["ada_b"][l].rearrange("(i p k) -> p i k", i=6, k=KD))
                    small_load(gains[:, l, :], a["norm_mix"][l].rearrange("(p k) -> p k", k=KD))
                    small_load(gains[:, 2 + l, :], a["norm_ffn"][l].rearrange("(p k) -> p k", k=KD))
                    small_load(wr[:, l, :, 0:GROUPS], a["moe_w_group"][l].rearrange("(p k) n -> p k n", k=KD))
                    small_load(wr[:, l, :, GROUPS:ROUTES], a["moe_w_expert"][l].rearrange("(p k) n -> p k n", k=KD))
                    small_load(br[:, l, 0:GROUPS], along(a["moe_b_group"][l]))
                    small_load(br[:, l, GROUPS:ROUTES], along(a["moe_b_expert"][l]))
                small_load(gains[:, 4, :], a["norm_final"].rearrange("(p k) -> p k", k=KD))
                small_load(rows[0:40, :], a["ssd_conv_w"][0].rearrange("w (i p) -> (w i) p", p=P))
                small_load(rows[40:100, :], a["gdn_conv_w"][0].rearrange("w (i p) -> (w i) p", p=P))
                small_load(rows[100:108, :], a["ssd_conv_b"][0].rearrange("(i p) -> i p", p=P))
                small_load(rows[108:120, :], a["gdn_conv_b"][0].rearrange("(i p) -> i p", p=P))
                small_load(rows[120:128, :], a["state_mlstm_n"][0, 0].rearrange("d h k -> (d h) k"))
                small_load(bias_e[:, 0:8], along(a["ml_i_bias"][0].rearrange("d h -> (d h)")))
                small_load(bias_e[:, 8:16], along(a["ml_f_bias"][0].rearrange("d h -> (d h)")))
                for d in range(2):
                    small_load(bias_o[:, d, 0:8], along(a["ssd_dt_bias"][0, d]))
                    small_load(bias_o[:, d, 8:12], along(a["gdn_dt_bias"][0, d]))
                    small_load(alog[:, d, 0:8], along(a["ssd_A_log"][0, d]))
                    small_load(alog[:, d, 8:12], along(a["gdn_A_log"][0, d]))
                small_load(dskip[:], along(a["ssd_D"][0]))
                small_load(mprev0[:], along(a["state_mlstm_m"][0, 0].rearrange("d h -> (d h)")))
                small_load(gml, along(a["ml_norm"][0].rearrange("h v -> (h v)")))
                small_load(gq, along(a["mla_q_norm"][0]))
                small_load(gkv, along(a["mla_kv_norm"][0]))
                small_load(w_uq, a["mla_w_uq"][0].rearrange("(k p) n -> p k n", p=P))
                small_load(w_ukv, a["mla_w_ukv"][0].rearrange("(k p) n -> p k n", p=P))
                small_load(kvpast, a["cache_mla_kv"][0, 0])
                pool.dma_start(kpin[:, NOPE:QK_DIM], a["cache_mla_krope"][0, 0]).then_inc(S("small_in"), 16)
                count[0] += 1
                for d in range(2):
                    small_load(mlC[:, 1, d, :].rearrange("p (h v) -> p h v", h=4),
                               a["state_mlstm_C"][0, 0, d].rearrange("h k v -> k h v"))
                build.n_small = count[0]

                pool.wait_ge(*taken("tb", 0))
                pool.dma_start(o["krope"][0, 0], tail[:, 0, KPE0:KPE0 + ROPE]).then_inc(S("even_out"), 16)
                pool.wait_ge(S("ml_states"), 2)
                for d in range(2):
                    pool.dma_start(o["C"][0, 0, d].rearrange("h k v -> k h v"),
                                   mlC[:, 0, d, :].rearrange("p (h v) -> p h v", h=4)).then_inc(S("ml_out"), 16)
                    pool.dma_start(o["n"][0, 0, d].rearrange("h k -> k h"), mln[:, 0, d, :]).then_inc(S("ml_out"), 16)
                pool.dma_start(o["m"][0, 0].rearrange("d h -> (d h)").unsqueeze(0),
                               mst[0:1, 0, :, :].rearrange("p d h -> p (d h)")).then_inc(S("ml_out"), 16)

                pool.wait_ge(S("kv_norm"), 1)
                pool.dma_start(o["kv"][0, 0], ckn[:, 0, :]).then_inc(S("even_out"), 16)

                pool.wait_ge(S("x"), 3)
                pool.dma_start(gssd, along(a["ssd_norm"][0])).then_inc(S("odd_in"), 16)
                pool.dma_start(ggdn, along(a["gdn_norm"][0])).then_inc(S("odd_in"), 16)
                pool.wait_ge(S("conv_done"), 1)
                for d in range(2):
                    pool.dma_start(h0[:, d], a["state_ssd"][0, 0, d].rearrange("(i g) q n -> (g q) i n", g=2))\
                        .then_inc(S("odd_in"), 16)
                for d in range(2):
                    pool.dma_start(Sg[:, 1, d, :].rearrange("p (h v) -> p h v", h=4),
                                   a["state_gdn"][0, 0, d].rearrange("h k v -> k h v")).then_inc(S("gdn_in"), 16)
                for d in range(2):
                    pool.wait_ge(S("gdn_state"), d + 1)
                    pool.dma_start(o["gdn"][0, 0, d].rearrange("h k v -> k h v"),
                                   Sg[:, 0, d, :].rearrange("p (h v) -> p h v", h=4)).then_inc(S("odd_out"), 16)
                    pool.wait_ge(*taken("hT", d))
                    pool.dma_start(o["ssd"][0, 0, d].rearrange("(i g) q n -> (g q) i n", g=2),
                                   hsO[:, d, :].rearrange("p (i n) -> p i n", i=4)).then_inc(S("odd_out"), 16)
                for c in range(TILES):
                    pool.wait_ge(S("y_rows"), 2 * (c + 1))
                    dst = o["yp"][0] if c == 0 else o["ys"][0, (c - 1) * P:c * P, :]
                    pool.dma_start(dst, mix[:].rearrange("p k t -> p (k t)")[:, c * D:(c + 1) * D]).then_inc(S("out"), 16)
                pool.wait_ge(S("odd_out"), 64)
                pool.wait_ge(S("out"), 16 * TILES)
                pool.wait_ge(S("even_out"), 32)
                pool.wait_ge(S("ml_out"), 80)

        SMALL = 16 * build.n_small

        @block.tensor
        def _(pe):
            at = [0]
            mm = nc.tensor.matmul

            def issue(*job):
                assert jobs[at[0]] == job, (jobs[at[0]], job)
                n = at[0]
                at[0] += 1
                if n >= BANKS:
                    pe.wait_ge(free[n % BANKS], n // BANKS)
                return psum[:, n % BANKS, :]

            def ready(ins):
                n = at[0] - 1
                ins.then_inc(full[n % BANKS], 1)

            ring_count = [0] * RING
            ring_at = [0]

            def weight(kind, what):
                n = ring_at[0]
                assert weights[n][0:2] == (kind, what), (weights[n], kind, what)
                ring_at[0] += 1
                ring_count[n % RING] += 32 if (kind, what) == ("odd", 7) else 16
                pe.wait_ge(S(f"ring{n % RING}_full"), ring_count[n % RING])
                return ring[:, n % RING, :]

            def wview(slot):
                return slot.rearrange("p (k n) -> p k n", k=KD)

            def contract(out, lhs, rhs, n):
                for k in range(n):
                    ins = mm(out, lhs(k), rhs(k), start=(k == 0), stop=(k == n - 1))
                return ins

            def tok(c):
                return slice(c * P, (c + 1) * P)

            pe.wait_ge(S("small_in"), SMALL)
            pe.wait_ge(S("x_in"), 16 * TILES)
            for k in range(KD):
                b = issue("xt", k)
                for c in range(TILES):
                    ins = nc.tensor.transpose(b[:, tok(c)], ring[:, 2, c * D + k:(c + 1) * D:KD], ident)
                ready(ins)
            b = issue("cols")
            ready(nc.tensor.transpose(b[:, 0:P], rows[:], ident))

            pe.wait_ge(S("silu_c"), 1)
            for l in range(2):
                for i in range(6):
                    w = [weight("ada", (l, i, half)).rearrange("p (k n) -> p k n", k=4) for half in range(2)]
                    b = issue("mod", l, i)
                    for m in range(KD):
                        ins = contract(b[:, 2 * m:2 * m + 2], lambda k: w[k // 4][:, k % 4, m::KD],
                                       lambda k: sil[:, :, k], KD)
                    ready(ins)

            def norm(n):
                pe.wait_ge(S("squares"), n + 1)
                b = issue("ss", n)
                ready(contract(b[:, 0:T], lambda k: ones, lambda k: mix[:, k, :], KD))

            norm(0)
            pe.wait_ge(S("h"), 1)
            for n, name in ((0, "qT"), (1, "kT")):
                w = wview(weight("even", n))
                for h in range(4):
                    b = issue(name, h)
                    ready(contract(b[:, 0:T], lambda k: w[:, k, h * P:(h + 1) * P], lambda k: hT[:, k, :], KD))
            for n, name in ((1, "kN"), (2, "vN"), (3, "oN"), (4, "ta"), (5, "tb")):
                if n > 1:
                    w = wview(weight("even", n))
                width = 512 if n < 5 else IN_EVEN - 5 * 512
                for c in range(TILES):
                    b = issue(name, c)
                    ready(contract(b[:, 0:width], lambda k: hT[:, k, tok(c)], lambda k: w[:, k, 0:width], KD))

            def cumulate(n, lf_, tri, width):
                pe.wait_ge(S("log_decay"), n + 1)
                b = issue("cum", n)
                for d in range(2):
                    mm(b[:, d * width:(d + 1) * width], tri[d], lf_[:, d].rearrange("p c h -> p (c h)"),
                       start=True, stop=True)
                ready(mm(b[:, 2 * width:4 * width], ones, lf_.rearrange("p d c h -> p (d c h)"), start=True, stop=True))

            cumulate(0, lf, cum01, 12)

            def spread(b, col):
                for h in range(4):
                    ins = mm(b[:, tok(h)], col(h).to_broadcast([P, P]), ident, start=True, stop=True)
                ready(ins)

            def four(b, lhs, rhs, width=P):
                for h in range(4):
                    ins = mm(b[:, h * width:(h + 1) * width], lhs(h), rhs(h), start=True, stop=True)
                ready(ins)

            pe.wait_ge(S("r"), 1)
            for u, (d, c) in enumerate(units):
                s = int(c > 0)
                spread(issue("R", u), lambda h: rr[:, d, c, h:h + 1])
                b = issue("MR", u)
                pe.wait_ge(S("neg_m"), u + 1)
                spread(b, lambda h: nmr[:, h:h + 1])
                pe.wait_ge(*taken("kT", 3))
                four(issue("SK", u), lambda h: kT[:, h, tok(c)], lambda h: qT[:, h, tok(c)])
                b = issue("N1", u)
                pe.wait_ge(S("st"), u + 1)
                pe.wait_ge(*taken("vN", 2))
                four(b, lambda h: ST[:, tok(h)], lambda h: vN[:, c, tok(h)])
                b = issue("DN", u)
                for h in range(4):
                    ins = mm(b[:, h:h + 1], ST[:, tok(h)], ones[:, 0:1], start=True, stop=True)
                if c:
                    if first_chunk(d, c):
                        pe.wait_ge(S("n_start"), 1)
                    else:
                        pe.wait_ge(S("ml_updated"), u - 3)
                    for h in range(4):
                        ins = mm(b[:, 4 + h:5 + h], qT[:, h, tok(c)], mln[:, 1, d, h:h + 1], start=True, stop=True)
                ready(ins)
                if c:
                    four(issue("N2", u), lambda h: qT[:, h, tok(c)], lambda h: mlC[:, 1, d, tok(h)])
                if c == 0 or first_chunk(d, c):
                    b = issue("CU", u)
                    pe.wait_ge(S("kw"), u + 1)
                    four(b, lambda h: kw[:, tok(h)], lambda h: vN[:, c, tok(h)])
                    four(issue("NU", u), lambda h: kw[:, tok(h)], lambda h: ones[:, 0:1], width=1)

            pe.wait_ge(S("hm"), 1)
            for h in range(4):
                b = issue("hmT", h)
                for c in range(TILES):
                    ins = nc.tensor.transpose(b[:, tok(c)], hsum[:, c, tok(h)], ident)
                ready(ins)

            pe.wait_ge(S("mla_norm"), 1)
            for k in range(3):
                b = issue("cqT", k)
                for c in range(TILES):
                    ins = nc.tensor.transpose(b[:, tok(c)], cqn[:, c, tok(k)], ident)
                ready(ins)
            for k in range(2):
                b = issue("kvT", k)
                for n, src in enumerate((ckn[:, 0], kvpast, ckn[:, 1], ckn[:, 2])):
                    ins = nc.tensor.transpose(b[:, tok(n)], src[:, tok(k)], ident)
                ready(ins)
            b = issue("kpT")
            for n, src in enumerate((tail[:, 0], None, tail[:, 1], tail[:, 2])):
                src = kpin[:, 0:QK_DIM] if src is None else src[:, KPE0 - NOPE:KPE0 + ROPE]
                ins = nc.tensor.transpose(b[0:QK_DIM, tok(n)], src, ident)
            ready(ins)
            b = issue("kpR")
            pe.wait_ge(*taken("kpT"))
            ready(mm(b[NOPE:QK_DIM, 0:SAMPLE], rot[NOPE:QK_DIM, :], kpe[NOPE:QK_DIM, 2 * P:4 * P], start=True, stop=True))
            for h in range(MLA_H):
                b = issue("qf", h)
                pe.wait_ge(*taken("cqT", 2))
                ready(contract(b[0:QK_DIM, 0:T], lambda k: w_uq[:, k, h * QK_DIM:(h + 1) * QK_DIM],
                               lambda k: cqT[:, k, :], 3))
            for i in range(4):
                b = issue("qR", i)
                pe.wait_ge(*taken("qf", 2 * i + 1))
                ready(mm(b[NOPE:QK_DIM, :].rearrange("p (h t) -> p h t", h=2), rot[NOPE:QK_DIM, :],
                         qfT[NOPE:QK_DIM, 2 * i:2 * i + 2, PROMPT:T], start=True, stop=True))
            for h in range(MLA_H):
                b = issue("kn", h)
                pe.wait_ge(*taken("kvT", 1))
                ready(contract(b[0:NOPE, :], lambda k: w_ukv[:, k, h * P:h * P + NOPE], lambda k: kvT[:, k, :], 2))
            for n in range(4):
                b = issue("vv", n)
                ready(contract(b[:, :].rearrange("p (h v) -> p h v", h=MLA_H), lambda k: kvT[:, k, tok(n)],
                               lambda k: w_ukv[:, k, :].rearrange("p (h v) -> p h v", h=MLA_H)[:, :, NOPE:P], 2))
            pe.wait_ge(*taken("vv", 3))
            pe.wait_ge(*taken("kn", 7))
            pe.wait_ge(S("keys"), 1)
            pe.wait_ge(S("q_rot"), 1)
            for c in range(TILES):
                tiles = [0] if c == 0 else [1, 2, 3]
                nk = len(tiles) * P
                for h in range(MLA_H):
                    n = c * MLA_H + h
                    b = issue("sc", c, h)
                    ready(mm(b[:, 0:nk], qfT[0:QK_DIM, h, tok(c)], kfT[0:QK_DIM, h, tiles[0] * P:tiles[0] * P + nk],
                             start=True, stop=True))
                    b = issue("pT", c, h)
                    pe.wait_ge(S("probs"), n + 1)
                    for t in range(len(tiles)):
                        ins = nc.tensor.transpose(b[:, tok(t)], pr[:, n % 2, tok(t)], ident)
                    ready(ins)
                    if h % 2:
                        b = issue("pv", c, h // 2)
                        for g in range(2):
                            hh = h - 1 + g
                            pe.wait_ge(*taken("pT", c, hh))
                            for t, kt in enumerate(tiles):
                                ins = mm(b[64 * g:64 * g + 64, 0:P], vv[:, kt, hh * 64:hh * 64 + 64],
                                         prT[:, (n - 1 + g) % 2, tok(t)], start=(t == 0), stop=(t == len(tiles) - 1))
                        ready(ins)

            def project_out(l):
                w = [weight("out", (l, half)).rearrange("p (k n) -> p k n", k=4) for half in range(2)]
                for m in range(KD):
                    b = issue("o", l, m)
                    ready(contract(b[:, 0:T], lambda k: w[k // 4][:, k % 4, m::KD], lambda k: mix[:, k, :], KD))

            def router(l):
                pe.wait_ge(S("h"), 2 * l + 2)
                b = issue("rt", l)
                for c in range(TILES):
                    ins = contract(b[:, c * ROUTES:(c + 1) * ROUTES], lambda k: hT[:, k, tok(c)],
                                   lambda k: wr[:, l, k, :], KD)
                ready(ins)

            def experts(l):
                for n in range(at[0] - BANKS, at[0]):
                    pe.wait_ge(free[n % BANKS], n // BANKS + 1)
                with pe.Fori(0, EXPERTS // 2) as i:
                    for u in range(2):
                        e = i * 2 + u
                        pe.wait_ge(S(f"gu{u}_full"), i * 32 + (32 + 16 * EXPERTS * l))
                        for j in range(2):
                            pe.wait_ge(S("act_ready"), e * 2 + (j + 1 + (2 * EXPERTS + 2) * l))
                            for w in range(2):
                                ins = contract(psum[:, 2 * j + w, 0:T], lambda k: gu[u][:, w, k, j::2],
                                               lambda k: hT[:, k, :], KD)
                            ins.then_inc(S("gu_computed"), 1)
                        pe.wait_ge(S(f"dn{u}_full"), i * 16 + (16 + 8 * EXPERTS * l))
                        pe.wait_ge(S("act_ready"), e * 2 + (4 + (2 * EXPERTS + 2) * l))
                        for q in range(6):
                            c, half = q // 2, q % 2
                            pe.wait_ge(S("y_taken"), e * 6 + (q + 1 + (6 * EXPERTS + 4) * l))
                            ins = contract(psum[:, 4 + (6 * u + q) % 4, :], lambda j: actT[u][:, j, tok(c)],
                                           lambda j: dn[u][:, j, half * 512:half * 512 + 512], 2)
                            ins.then_inc(S("y_computed"), 1)
                pe.wait_ge(S("y_taken"), (6 * EXPERTS + 4) * (l + 1))
                for m in range(KD):
                    b = issue("yt", l, m)
                    for c in range(TILES):
                        ins = nc.tensor.transpose(b[:, tok(c)], yacc[:, c, m::KD], ident)
                    ready(ins)

            for m in range(4):
                pe.wait_ge(*taken("hmT", m))
                pe.wait_ge(*taken("pv", 2, m))
            project_out(0)
            norm(1)
            router(0)
            experts(0)
            norm(2)

            pe.wait_ge(S("h"), 3)
            w = wview(weight("odd", 0))
            for c in range(TILES):
                b = issue("zs", c)
                ready(contract(b, lambda k: hT[:, k, tok(c)], lambda k: w[:, k, :], KD))
            for i in range(CONV_TILES):
                if i % 4 == 0:
                    w = wview(weight("odd", 1 + i // 4))
                b = issue("xb", i)
                ready(contract(b[:, 0:T], lambda k: w[:, k, tok(i % 4)], lambda k: hT[:, k, :], KD))
            w = wview(weight("odd", 6))
            for c in range(TILES):
                b = issue("zg", c)
                ready(contract(b, lambda k: hT[:, k, tok(c)], lambda k: w[:, k, :], KD))
            w = wview(weight("odd", 7))
            b = issue("dg")
            for c in range(TILES):
                ins = contract(b[:, c * 32:c * 32 + 32], lambda k: hT[:, k, tok(c)], lambda k: w[:, k, 0:32], KD)
            ready(ins)

            pe.wait_ge(S("l2_squares"), 1)
            for i in range(8):
                b = issue("l2", i)
                ready(mm(b[:, 0:COUT], ones, l2[:, i, :], start=True, stop=True))
            pe.wait_ge(S("l2_done"), 1)
            for c in range(TILES):
                for name, i0, n in (("tx", 0, 4), ("tB", 4, 2), ("tk", 12, 4), ("tv", 16, 4)):
                    b = issue(name, c)
                    for i in range(n):
                        ins = nc.tensor.transpose(b[:, tok(i)], conv[:, i0 + i, CO[c]:CO[c] + P], ident)
                    ready(ins)
            cumulate(1, lg, cum01, 36)
            pe.wait_ge(S("odd_in"), 64)
            for d in range(2):
                b = issue("h0T", d)
                for i in range(4):
                    ins = nc.tensor.transpose(b[:, tok(i)], h0[:, d, i, :], ident)
                ready(ins)

            pe.wait_ge(S("odd_gates"), 1)
            pe.wait_ge(*taken("tv", 2))
            pe.wait_ge(*taken("tk", 2))
            pe.wait_ge(*taken("h0T", 1))
            pe.wait_ge(S("gdn_in"), 32)
            for u, (d, c) in enumerate(units):
                s = int(c > 0)
                t = slice(CO[c], CO[c] + P)
                for g in range(2):
                    spread(issue("Es", u, g), lambda h: cb[:, d, c, 4 * g + h:4 * g + h + 1])
                    ready(mm(issue("GB", u, g)[:, 0:P], conv[:, 4 + g, t], conv[:, 6 + g, t], start=True, stop=True))
                b = issue("Y1", u)
                pe.wait_ge(S("ssd_in"), u + 1)
                for h in range(SSD_H):
                    ins = mm(b[:, h * SSD_P:(h + 1) * SSD_P], G[:, tok(h)], xdt[:, h * SSD_P:(h + 1) * SSD_P],
                             start=True, stop=True)
                ready(ins)
                if c:
                    b = issue("Y2", u)
                    if not first_chunk(d, c):
                        pe.wait_ge(S("ssd_updated"), u - 1)
                    for g in range(2):
                        ins = mm(b[:, g * 256:(g + 1) * 256], conv[:, 6 + g, t], hsT[:, 1, d, g * 256:(g + 1) * 256],
                                 start=True, stop=True)
                    ready(ins)
                if c == 0 or first_chunk(d, c):
                    b = issue("HU", u)
                    for g in range(2):
                        ins = mm(b[:, g * 256:(g + 1) * 256], BN[:, c, tok(g)], xw[:, g * 256:(g + 1) * 256],
                                 start=True, stop=True)
                    ready(ins)
                spread(issue("Eg", u), lambda h: cb[:, d, c, 8 + h:9 + h])
                four(issue("KK", u), lambda h: conv[:, 12 + h, t], lambda h: conv[:, 12 + h, t])
                four(issue("KQ", u), lambda h: conv[:, 12 + h, t], lambda h: conv[:, 8 + h, t])
                b = issue("X0", u)
                pe.wait_ge(S("xt_new"), 7 * u + 1)
                for h in range(4):
                    ins = nc.tensor.transpose(b[:, tok(h)], XT[:, tok(h)], ident)
                ready(ins)
                for n in range(1, 7):
                    b = issue("T1", u, n)
                    if n == 1:
                        pe.wait_ge(*taken("X0", u))
                    else:
                        pe.wait_ge(*taken("XX", u, n - 1))
                    pe.wait_ge(S("lt"), 6 * u + n)
                    four(b, lambda h: LT[:, tok(h)], lambda h: X[:, tok(h)])
                    b = issue("XT", u, n)
                    pe.wait_ge(*taken("T1", u, n))
                    four(b, lambda h: TT[:, tok(h)], lambda h: XT[:, tok(h)])
                    if n < 6:
                        four(issue("XX", u, n), lambda h: XT[:, tok(h)], lambda h: TT[:, tok(h)])
                if c:
                    if not first_chunk(d, c):
                        pe.wait_ge(S("gdn_updated"), u - 1)
                    four(issue("KS", u), lambda h: conv[:, 12 + h, t], lambda h: Sg[:, 1, d, tok(h)])
                b = issue("U", u)
                pe.wait_ge(S("xt_new"), 7 * u + 7)
                if c:
                    pe.wait_ge(S("rhs"), 1 + [j for j, v in enumerate(units) if v[1]].index(u))
                    four(b, lambda h: XT[:, tok(h)], lambda h: Rg[:, tok(h)])
                else:
                    four(b, lambda h: XT[:, tok(h)], lambda h: gv[:, c, tok(h)])
                b = issue("O1", u)
                pe.wait_ge(*taken("U", u))
                four(b, lambda h: PT[:, tok(h)], lambda h: U[:, tok(h)])
                if c:
                    four(issue("O2", u), lambda h: conv[:, 8 + h, t], lambda h: Sg[:, 1, d, tok(h)])
                if c == 0 or first_chunk(d, c):
                    b = issue("SU", u)
                    pe.wait_ge(S("uw"), u + 1)
                    four(b, lambda h: gk[:, c, tok(h)], lambda h: Uw[:, tok(h)])
                if c == 0:
                    b = issue("hT", d)
                    pe.wait_ge(S("ssd_updated"), u + 1)
                    for i in range(4):
                        ins = nc.tensor.transpose(b[:, tok(i)], hsT[:, 0, d, tok(i)], ident)
                    ready(ins)

            for f in range(8):
                b = issue("mT", f)
                src = ysum if f < 4 else ogsum
                pe.wait_ge(S("odd_rows"), 1 if f < 4 else 2)
                for c in range(TILES):
                    ins = nc.tensor.transpose(b[:, tok(c)], src[:, c, tok(f % 4)], ident)
                ready(ins)
            for f in range(8):
                pe.wait_ge(*taken("mT", f))
            project_out(1)
            norm(3)
            router(1)
            experts(1)
            norm(4)
            pe.wait_ge(S("h"), 5)
            for c in range(TILES):
                for half in range(2):
                    b = issue("fin", c, half)
                    for k in range(4):
                        ins = nc.tensor.transpose(b[:, tok(k)], hT[:, 4 * half + k, tok(c)], ident)
                    ready(ins)
            assert at[0] == len(jobs)

        @block.scalar
        def _(act):
            done, take = every(act)
            fn = nc.scalar.activation
            act.wait_ge(S("small_in"), SMALL)
            done(fn(sil[:], cc[:], ACT.Silu), "silu_c")

            def norm(n):
                act.wait_ge(S("x"), n + 1)
                done(fn(mix[:], xT[:], ACT.Square), "squares")
                act.wait_ge(*computed("ss", n))
                take(fn(rB[:], bank("ss", n)[:, 0:T], ACT.Sqrt, scale=1.0 / D, bias=eps[:, 0:1]), "ss", n)

            act.wait_ge(S("eps"), 1)
            norm(0)
            for h in range(4):
                act.wait_ge(*computed("qT", h))
                take(fn(qT[:, h, :], bank("qT", h)[:, 0:T], ACT.Copy, scale=DK ** -0.5), "qT", h)
            for h in range(4):
                act.wait_ge(*computed("kT", h))
                take(fn(kT[:, h, :], bank("kT", h)[:, 0:T], ACT.Copy), "kT", h)
            for c in range(TILES):
                act.wait_ge(*computed("oN", c))
                take(fn(oS[:, c, :], bank("oN", c), ACT.Sigmoid), "oN", c)
            act.wait_ge(S("f_abs"), 1)
            done(fn(tf, tf, ACT.Exp, scale=-1.0), "act_own")
            done(fn(tf, tf, ACT.Ln, bias=1.0), "f_ln")
            for u, (d, c) in enumerate(units):
                act.wait_ge(S("mr_masked"), u + 1)
                for h in range(4):
                    ins = fn(ET[:, h * P:(h + 1) * P], mrt[:, h * P:(h + 1) * P], ACT.Exp, bias=rr[:, d, c, h:h + 1])
                ins.then_inc(S("et"), 1)
                act.wait_ge(S("ml_small"), u + 1)
                fn(aexp, mx, ACT.Exp)
                fn(emq, emq, ACT.Exp)
                fn(dec, dec, ACT.Exp)
                fn(wk, wk, ACT.Exp).then_inc(S("ml_exps"), 1)
            act.wait_ge(S("hm_ms"), 1)
            done(fn(ms12, ms12, ACT.Sqrt, scale=1.0 / DK, bias=eps[:, 0:1]), "hm_rt")
            for h in range(4):
                act.wait_ge(*computed("hmT", h))
                take(fn(mix[:, h, :], bank("hmT", h)[:, 0:T], ACT.Copy), "hmT", h)
            act.wait_ge(S("mla_ms"), 1)
            fn(ms3, ms3, ACT.Sqrt, scale=1.0 / Q_RANK, bias=eps[:, 0:1])
            done(fn(ms6, ms6, ACT.Sqrt, scale=1.0 / KV_RANK, bias=eps[:, 0:1]), "mla_rt")
            for k in range(3):
                act.wait_ge(*computed("cqT", k))
                take(fn(cqT[:, k, :], bank("cqT", k)[:, 0:T], ACT.Copy), "cqT", k)
            for k in range(2):
                act.wait_ge(*computed("kvT", k))
                take(fn(kvT[:, k, :], bank("kvT", k), ACT.Copy), "kvT", k)
            act.wait_ge(*computed("kpT"))
            take(fn(kpe[NOPE:QK_DIM, :], bank("kpT")[NOPE:QK_DIM, :], ACT.Copy), "kpT")
            for h in range(MLA_H):
                act.wait_ge(*computed("qf", h))
                take(fn(qfT[0:QK_DIM, h, :], bank("qf", h)[0:QK_DIM, 0:T], ACT.Copy), "qf", h)
            for h in range(MLA_H):
                act.wait_ge(*computed("kn", h))
                take(fn(kfT[0:NOPE, h, :], bank("kn", h)[0:NOPE, :], ACT.Copy), "kn", h)
            act.wait_ge(S("k_rot"), 1)
            done(fn(kfT[NOPE:QK_DIM, :, :], bc(kpe[NOPE:QK_DIM, :], 1, [ROPE, MLA_H, KEYS]), ACT.Copy), "keys")
            scale = QK_DIM ** -0.5
            for c in range(TILES):
                nk = P if c == 0 else 3 * P
                for h in range(MLA_H):
                    n = c * MLA_H + h
                    act.wait_ge(S("score_max"), n + 1)
                    if n >= 2:
                        act.wait_ge(*computed("pT", (n - 2) // MLA_H, (n - 2) % MLA_H))
                    take(fn(pr[:, n % 2, 0:nk], bank("sc", c, h)[:, 0:nk], ACT.Exp, scale=scale,
                            bias=nb[:, n % 2:n % 2 + 1], accum_out=rs[:, n % 2:n % 2 + 1]), "sc", c, h)
                    act.wait_ge(*computed("pT", c, h))
                    take(fn(prT[:, n % 2, 0:nk], bank("pT", c, h)[:, 0:nk], ACT.Copy), "pT", c, h)
                    if h % 2:
                        act.wait_ge(*computed("pv", c, h // 2))
                        take(fn(mix[:, 4 + h // 2, c * P:(c + 1) * P], bank("pv", c, h // 2)[:, 0:P], ACT.Copy),
                             "pv", c, h // 2)

            def router(l):
                act.wait_ge(S("g_shift"), l + 1)
                done(fn(route[:, 3, :, 0:GROUPS], route[:, 3, :, 0:GROUPS], ACT.Exp), "g_exp")
                act.wait_ge(S("top_gap"), l + 1)
                done(fn(route[:, 10, :, 2:3], route[:, 10, :, 2:3], ACT.Exp), "top_exp")

            def experts(l):
                with act.Fori(0, EXPERTS // 2) as i:
                    for u in range(2):
                        e = i * 2 + u
                        for j in range(2):
                            act.wait_ge(S("gu_computed"), e * 2 + (j + 1 + 2 * EXPERTS * l))
                            fn(sg[:, j, :], psum[:, 2 * j, 0:T], ACT.Silu).then_inc(S("silu_done"), 1)

            norm(1)
            router(0)
            experts(0)
            norm(2)
            for c in range(TILES):
                act.wait_ge(*computed("zs", c))
                take(fn(zs[:, c, :], bank("zs", c), ACT.Silu), "zs", c)
            act.wait_ge(S("pads"), 1)
            for i in range(CONV_TILES):
                act.wait_ge(*computed("xb", i))
                fn(cin[:, i, PAD:PAD + PROMPT], bank("xb", i)[:, 0:PROMPT], ACT.Copy)
                take(fn(cin[:, i, 3 * PAD + PROMPT:3 * PAD + T], bank("xb", i)[:, PROMPT:T], ACT.Copy), "xb", i)
            for c in range(TILES):
                act.wait_ge(*computed("zg", c))
                take(fn(zg[:, c, :], bank("zg", c), ACT.Silu), "zg", c)
            act.wait_ge(*computed("dg"))
            take(fn(dg.rearrange("p c n -> p (c n)"), bank("dg")[:, 0:TILES * 32], ACT.Copy), "dg")
            for i in range(CONV_TILES):
                act.wait_ge(S("conv_tile"), i + 1)
                done(fn(conv[:, i, :], conv[:, i, :], ACT.Silu), "conv_act")
            act.wait_ge(S("conv_done"), 1)
            done(fn(l2, conv[:, 8:16, :], ACT.Square), "l2_squares")
            for i in range(8):
                act.wait_ge(*computed("l2", i))
                take(fn(l2[:, i, :], bank("l2", i)[:, 0:COUT], ACT.Sqrt, bias=eps[:, 0:1]), "l2", i)
            act.wait_ge(S("sp_in"), 1)
            done(fn(sp, sp, ACT.Exp, scale=-1.0), "act_own")
            done(fn(sp, sp, ACT.Ln, bias=1.0), "sp_ln")
            fn(wA, alog[:].rearrange("p d h -> p (d h)"), ACT.Exp).then_inc(S("wA"), 1)
            for d in range(2):
                src = dg[:, :, 28 + 4 * d - 4:32 + 4 * d - 4]
                ins = fn(beta[:, d], src, ACT.Sigmoid)
            ins.then_inc(S("beta"), 1)
            act.wait_ge(S("odd_cum"), 1)
            fn(ecb, cb, ACT.Exp)
            fn(etot, tot, ACT.Exp)
            fn(edif, edif, ACT.Exp).then_inc(S("odd_exps"), 1)
            for u, (d, c) in enumerate(units):
                for g in range(2):
                    act.wait_ge(S("e_masked"), 3 * u + g + 1)
                    for h in range(4):
                        ins = fn(E1[:, h * P:(h + 1) * P], E1[:, h * P:(h + 1) * P], ACT.Exp,
                                 bias=ncb[:, d, c, 4 * g + h:4 * g + h + 1])
                    ins.then_inc(S("e_done"), 1)
                act.wait_ge(S("e_masked"), 3 * u + 3)
                for h in range(4):
                    ins = fn(EB[:, h * P:(h + 1) * P], EB[:, h * P:(h + 1) * P], ACT.Exp,
                             bias=ncb[:, d, c, 8 + h:9 + h])
                ins.then_inc(S("e_done"), 1)
                act.wait_ge(*computed("X0", u))
                take(fn(X, bank("X0", u), ACT.Copy), "X0", u)
                for n in range(1, 7):
                    act.wait_ge(*computed("T1", u, n))
                    take(fn(TT, bank("T1", u, n), ACT.Copy), "T1", u, n)
                act.wait_ge(*computed("U", u))
                take(fn(U, bank("U", u), ACT.Copy), "U", u)
                if c == 0:
                    act.wait_ge(*computed("hT", d))
                    take(fn(hsO[:, d, :], bank("hT", d), ACT.Copy), "hT", d)
            act.wait_ge(S("odd_ms"), 1)
            fn(ms3, ms3, ACT.Sqrt, scale=1.0 / 512, bias=eps[:, 0:1])
            done(fn(ms12, ms12, ACT.Sqrt, scale=1.0 / DK, bias=eps[:, 0:1]), "odd_rt")
            for f in range(8):
                act.wait_ge(*computed("mT", f))
                take(fn(mix[:, f, :], bank("mT", f)[:, 0:T], ACT.Copy), "mT", f)
            norm(3)
            router(1)
            experts(1)
            norm(4)
            for c in range(TILES):
                for half in range(2):
                    act.wait_ge(*computed("fin", c, half))
                    dst = mix[:].rearrange("p k t -> p (k t)")[:, c * D:(c + 1) * D]\
                        .rearrange("p (q k) -> p k q", k=KD)[:, 4 * half:4 * half + 4, :]
                    fn(dst, heads(bank("fin", c, half), 4), ACT.Copy).then_inc(S("y_rows"), 1)

        @block.vector
        def _(dve):
            done, take = every(dve)
            v = nc.vector
            tt, ts, stt = v.tensor_tensor, v.tensor_scalar, v.scalar_tensor_tensor
            own = "dve_own"

            def o_(ins):
                done(ins, own)

            done(v.memset(eps[:], EPS), "eps")
            o_(v.memset(kpin[:, 0:NOPE], 0.0))
            for k in range(KD):
                dve.wait_ge(*computed("xt", k))
                take(v.tensor_copy(xT[:, k, :], bank("xt", k)[:, 0:T]), "xt", k)
            done(v.memset(ms3, 0.0), "x")
            dve.wait_ge(*computed("cols"))
            take(v.tensor_copy(colsT[:], bank("cols")[:, 0:P]), "cols")
            done(v.tensor_copy(mln[:, 1].rearrange("p d h -> p (d h)"), colsT[:, 120:128]), "n_start")
            for l in range(2):
                for i in range(6):
                    dve.wait_ge(*computed("mod", l, i))
                    take(tt(modT[:, l, i], bank("mod", l, i)[:, 0:16].rearrange("p (m j) -> p m j", j=2),
                            bc(adab[:, l, i, :], 2, [P, KD, 2]), ALU.add), "mod", l, i)
                for w in range(2):
                    o_(stt(amp[:, l, w], modT[:, l, 1 + 3 * w], 1.0, bc(gains[:, 2 * w + l, :], 2, [P, KD, 2]),
                           ALU.add, ALU.mult))

            def norm(n):
                dve.wait_ge(*taken("ss", n))
                o_(v.reciprocal(rB[:], rB[:]))
                o_(tt(hT[:], xT[:], bc(rB[:], 1, [P, KD, T]), ALU.mult))
                if n == 4:
                    done(tt(hT[:], hT[:], bc(gains[:, 4, :], 2, [P, KD, T]), ALU.mult), "h")
                    return
                l, w = n // 2, n % 2
                for j, t0, t1 in SEGS:
                    o_(tt(hT[:, :, t0:t1], hT[:, :, t0:t1], bc(amp[:, l, w, :, j], 2, [P, KD, t1 - t0]), ALU.mult))
                for j, t0, t1 in SEGS:
                    ins = tt(hT[:, :, t0:t1], hT[:, :, t0:t1], bc(modT[:, l, 3 * w, :, j], 2, [P, KD, t1 - t0]), ALU.add)
                    o_(ins) if j == 0 else done(ins, "h")

            def b4(ap):
                return bc(ap, 2, [P, 4, P])

            norm(0)
            for name, dst in (("kN", kN), ("vN", vN)):
                for c in range(TILES):
                    dve.wait_ge(*computed(name, c))
                    take(v.tensor_copy(dst[:, c, :], bank(name, c)), name, c)
            for c in range(TILES):
                dve.wait_ge(*computed("ta", c))
                take(v.tensor_copy(tail[:, c, 0:512], bank("ta", c)), "ta", c)
            for c in range(TILES):
                dve.wait_ge(*computed("tb", c))
                take(v.tensor_copy(tail[:, c, 512:TAIL], bank("tb", c)[:, 0:TAIL - 512]), "tb", c)
            for d in range(2):
                o_(tt(li[:, d], tail[:, :, 4 * d:4 * d + 4], bc(bias_e[:, 4 * d:4 * d + 4], 1, [P, TILES, 4]), ALU.add))
                o_(tt(lf[:, d], tail[:, :, 8 + 4 * d:12 + 4 * d], bc(bias_e[:, 8 + 4 * d:12 + 4 * d], 1, [P, TILES, 4]), ALU.add))
            done(stt(tf, lf, -1.0, lf, ALU.mult, ALU.max), "f_abs")
            o_(ts(lf, lf, 0.0, None, ALU.min))
            dve.wait_ge(S("f_ln"), 1)
            done(tt(lf, lf, tf, ALU.subtract), "log_decay")
            dve.wait_ge(*computed("cum", 0))
            take(v.tensor_copy(sm(72, 48), bank("cum", 0)[:, 0:48]), "cum", 0)
            o_(v.tensor_copy(mst[:, 1].rearrange("p d h -> p (d h)"), mprev0[:]))
            o_(v.memset(mst[:, 0], 0.0))
            done(tt(rr, li, bcum, ALU.subtract), "r")

            for u, (d, c) in enumerate(units):
                s = int(c > 0)
                m = mst[:, s, d]
                dve.wait_ge(*computed("R", u))
                if u:
                    dve.wait_ge(S("ml_exps"), u)
                o_(v.tensor_reduce(mxa, heads(bank("R", u), 4), AX, ALU.max))
                take(tt(heads(Rm, 4), heads(bank("R", u), 4), bc(neg_ts[d], 1, [P, 4, P]), ALU.add), "R", u)
                o_(v.tensor_reduce(mx, heads(Rm, 4), AX, ALU.max))
                o_(tt(mx, mx, m, ALU.max))
                done(ts(nmr, mx, -1.0, None, ALU.mult), "neg_m")
                o_(tt(mxa, mxa, m, ALU.max))
                o_(tt(emq, nmr, bcum[:, d, c], ALU.subtract))
                o_(tt(dec, m, mxa, ALU.subtract))
                o_(tt(mx, m, mx, ALU.subtract))
                o_(tt(m, mxa, btot[:, d, c], ALU.add))
                done(tt(wk, rr[:, d, c], mxa, ALU.subtract), "ml_small")
                dve.wait_ge(*computed("MR", u))
                if u:
                    dve.wait_ge(S("et"), u)
                ins = tt(heads(mrt, 4), heads(bank("MR", u), 4), bc(neg_st[d], 1, [P, 4, P]), ALU.add)
                take(ins, "MR", u)
                done(v.memset(ms3, 0.0), "mr_masked")
                dve.wait_ge(*computed("SK", u))
                dve.wait_ge(S("et"), u + 1)
                take(tt(ST, ET, bank("SK", u), ALU.mult), "SK", u)
                done(v.memset(ms3, 0.0), "st")
                dve.wait_ge(S("ml_exps"), u + 1)
                if c == 0 or first_chunk(d, c):
                    done(tt(heads(kw, 4), heads(kN[:, c, :], 4), b4(wk), ALU.mult), "kw")
                dve.wait_ge(*computed("N1", u))
                take(v.tensor_copy(num, bank("N1", u)), "N1", u)
                dve.wait_ge(*computed("DN", u))
                if c:
                    o_(tt(den, aexp, bank("DN", u)[:, 4:8], ALU.mult))
                    take(tt(den, den, bank("DN", u)[:, 0:4], ALU.add), "DN", u)
                    dve.wait_ge(*computed("N2", u))
                    take(tt(heads(t512, 4), heads(bank("N2", u), 4), b4(aexp), ALU.mult), "N2", u)
                    o_(tt(num, num, t512, ALU.add))
                else:
                    take(v.tensor_copy(den, bank("DN", u)[:, 0:4]), "DN", u)
                o_(stt(den, den, -1.0, den, ALU.mult, ALU.max))
                o_(tt(den, den, emq, ALU.max))
                o_(v.reciprocal(den2, den))
                first = (d, c) in ((0, 0), (0, 1), (1, 2))
                if first:
                    o_(tt(heads(hsum[:, c, :], 4), heads(num, 4), b4(den2), ALU.mult))
                else:
                    o_(tt(heads(num, 4), heads(num, 4), b4(den2), ALU.mult))
                    o_(tt(hsum[:, c, :], hsum[:, c, :], num, ALU.add))
                if c == 0:
                    dve.wait_ge(*computed("CU", u))
                    take(v.tensor_copy(mlC[:, 0, d, :], bank("CU", u)), "CU", u)
                    dve.wait_ge(*computed("NU", u))
                    take(v.tensor_copy(mln[:, 0, d, :], bank("NU", u)[:, 0:4]), "NU", u)
                    done(v.memset(ms3, 0.0), "ml_states")
                elif first_chunk(d, c):
                    dve.wait_ge(*computed("CU", u))
                    o_(tt(heads(mlC[:, 1, d, :], 4), heads(mlC[:, 1, d, :], 4), b4(dec), ALU.mult))
                    take(tt(mlC[:, 1, d, :], mlC[:, 1, d, :], bank("CU", u), ALU.add), "CU", u)
                    o_(tt(mln[:, 1, d, :], mln[:, 1, d, :], dec, ALU.mult))
                    dve.wait_ge(*computed("NU", u))
                    take(tt(mln[:, 1, d, :], mln[:, 1, d, :], bank("NU", u)[:, 0:4], ALU.add), "NU", u)
                    done(v.memset(ms3, 0.0), "ml_updated")

            h12 = hsum.rearrange("p c (h n) -> p (c h) n", h=4)
            for c in range(TILES):
                o_(tt(t512, hsum[:, c, :], hsum[:, c, :], ALU.mult))
                o_(v.tensor_reduce(ms12[:, 4 * c:4 * c + 4], heads(t512, 4), AX, ALU.add))
            done(v.memset(ms3, 0.0), "hm_ms")
            dve.wait_ge(S("hm_rt"), 1)
            o_(v.reciprocal(ms12, ms12))
            o_(tt(h12, h12, bc(ms12, 2, [P, 12, P]), ALU.mult))
            o_(tt(hsum, hsum, bc(gml, 1, [P, TILES, 512]), ALU.mult))
            dve.wait_ge(*taken("oN", 2))
            done(tt(hsum, hsum, oS, ALU.mult), "hm")

            dve.wait_ge(*computed("hmT", 3))
            dve.wait_ge(S("ml_out"), 80)
            cq, ck = tail[:, :, CQ0:CQ0 + Q_RANK], tail[:, :, CKV0:CKV0 + KV_RANK]
            sq3 = sqt.rearrange("p (c n) -> p c n", c=TILES)
            o_(tt(sq3, cq, cq, ALU.mult))
            o_(v.tensor_reduce(ms3, sq3, AX, ALU.add))
            o_(tt(ckn, ck, ck, ALU.mult))
            done(v.tensor_reduce(ms6, ckn, AX, ALU.add), "mla_ms")
            dve.wait_ge(S("mla_rt"), 1)
            o_(v.reciprocal(ms3, ms3))
            o_(v.reciprocal(ms6, ms6))
            o_(tt(ckn, ck, bc(ms6, 2, [P, TILES, KV_RANK]), ALU.mult))
            done(tt(ckn, ckn, bc(gkv, 1, [P, TILES, KV_RANK]), ALU.mult), "kv_norm")
            o_(tt(cqn, cq, bc(ms3, 2, [P, TILES, Q_RANK]), ALU.mult))
            done(tt(cqn, cqn, bc(gq, 1, [P, TILES, Q_RANK]), ALU.mult), "mla_norm")
            r = slice(NOPE, QK_DIM)
            dve.wait_ge(*computed("kpR"))
            dve.wait_ge(*taken("kpT"))
            take(tt(rtmp[r, 0:SAMPLE], sinT[r], bank("kpR")[r, 0:SAMPLE], ALU.mult), "kpR")
            o_(tt(kpe[r, 2 * P:4 * P], kpe[r, 2 * P:4 * P], cosT[r], ALU.mult))
            done(tt(kpe[r, 2 * P:4 * P], kpe[r, 2 * P:4 * P], rtmp[r, 0:SAMPLE], ALU.add), "k_rot")
            for i in range(4):
                q = qfT[r, 2 * i:2 * i + 2, PROMPT:T]
                dve.wait_ge(*computed("qR", i))
                tmp = rtmp[r, :].rearrange("p (h t) -> p h t", h=2)
                take(tt(tmp, bc(sinT[r], 1, [ROPE, 2, SAMPLE]), bank("qR", i)[r, :].rearrange("p (h t) -> p h t", h=2),
                        ALU.mult), "qR", i)
                o_(tt(q, q, bc(cosT[r], 1, [ROPE, 2, SAMPLE]), ALU.mult))
                o_(tt(q, q, tmp, ALU.add))
            done(v.memset(ms3, 0.0), "q_rot")
            for n in range(4):
                dve.wait_ge(*computed("vv", n))
                take(v.tensor_copy(vv[:, n, :], bank("vv", n)), "vv", n)
            scale = QK_DIM ** -0.5
            for c in range(TILES):
                nk = P if c == 0 else 3 * P
                for h in range(MLA_H):
                    n = c * MLA_H + h
                    k = n % 2
                    dve.wait_ge(*computed("sc", c, h))
                    o_(v.tensor_reduce(nbm[:, k:k + 1], bank("sc", c, h)[:, 0:nk], AX, ALU.max))
                    done(ts(nb[:, k:k + 1], nbm[:, k:k + 1], -scale, None, ALU.mult), "score_max")
                    dve.wait_ge(*taken("sc", c, h))
                    o_(v.reciprocal(rsi[:, k:k + 1], rs[:, k:k + 1]))
                    done(ts(pr[:, k, 0:nk], pr[:, k, 0:nk], rsi[:, k:k + 1], None, ALU.mult), "probs")

            def residual(name, l, part):
                for m in range(KD):
                    dve.wait_ge(*computed(name, l, m))
                    for j, t0, t1 in SEGS:
                        ins = stt(xT[:, m, t0:t1], bank(name, l, m)[:, t0:t1], modT[:, l, part, m, j:j + 1],
                                  xT[:, m, t0:t1], ALU.mult, ALU.add)
                    take(ins, name, l, m)
                done(v.memset(ms3, 0.0), "x")

            def router(l):
                R = [route[:, n] for n in range(12)]
                sh = [P, TILES, GROUPS]

                def col(n, k=0):
                    return R[10][:, :, n:n + 1] if k == 0 else R[10][:, :, n:n + 1].to_broadcast([P, TILES, k])

                dve.wait_ge(*computed("rt", l))
                take(tt(R[0], bank("rt", l)[:, 0:TILES * ROUTES].rearrange("p (c n) -> p c n", c=TILES),
                        bc(br[:, l, :], 1, [P, TILES, ROUTES]), ALU.add), "rt", l)
                g, el = R[0][:, :, 0:GROUPS], R[0][:, :, GROUPS:ROUTES]

                def first_max(dst, top, src, n, sc):
                    rk = rank[:, EXPERTS - n:EXPERTS]
                    o_(v.tensor_reduce(col(top), src, AX, ALU.max))
                    o_(tt(dst, src, col(top, n), ALU.is_equal))
                    o_(tt(dst, dst, bc(rk, 1, [P, TILES, n]), ALU.mult))
                    o_(v.tensor_reduce(col(sc), dst, AX, ALU.max))
                    o_(tt(dst, dst, col(sc, n), ALU.is_equal))

                gs = R[1][:, :, 0:GROUPS]
                first_max(gs, 0, g, GROUPS, 9)
                done(tt(R[3][:, :, 0:GROUPS], g, col(0, GROUPS), ALU.subtract), "g_shift")
                pen = R[2][:, :, 0:GROUPS]
                o_(ts(pen, gs, -NEG, NEG, ALU.mult, ALU.add))
                em = R[4][:, :, 0:EXPERTS]

                def by_group(x):
                    return x.rearrange("p c (g e) -> p c g e", g=GROUPS)

                full4 = [P, TILES, GROUPS, EXPERTS // GROUPS]
                o_(tt(by_group(em), by_group(el), bc(gs, 3, full4), ALU.mult))
                o_(tt(by_group(em), by_group(em), bc(pen, 3, full4), ALU.add))
                o1, o2 = R[5][:, :, 0:EXPERTS], R[6][:, :, 0:EXPERTS]
                first_max(o1, 3, em, EXPERTS, 9)
                o_(stt(em, o1, 2 * NEG, em, ALU.mult, ALU.add))
                first_max(o2, 4, em, EXPERTS, 9)
                done(tt(col(2), col(4), col(3), ALU.subtract), "top_gap")
                dve.wait_ge(S("g_exp"), l + 1)
                o_(v.tensor_reduce(col(5), R[3][:, :, 0:GROUPS], AX, ALU.add))
                dve.wait_ge(S("top_exp"), l + 1)
                o_(ts(col(6), col(2), 1.0, None, ALU.add))
                o_(tt(col(6), col(6), col(5), ALU.mult))
                o_(v.reciprocal(col(7), col(6)))
                o_(tt(col(8), col(7), col(2), ALU.mult))
                o_(tt(o1, o1, col(7, EXPERTS), ALU.mult))
                o_(tt(o2, o2, col(8, EXPERTS), ALU.mult))
                o_(tt(comb[:], o1, o2, ALU.add))

            def experts(l):
                ins = v.memset(mix[:], 0.0)
                o_(ins)
                done(v.memset(ms3, 0.0), "zeroed")
                v.memset(ms3, 0.0).then_inc(S("act_ready"), 2)
                v.memset(ms6, 0.0).then_inc(S("y_taken"), 4)
                dve.wait_ge(S("y_taken"), (6 * EXPERTS + 4) * l + 4)
                dve.wait_ge(S("act_ready"), (2 * EXPERTS + 2) * l + 2)
                with dve.Fori(0, EXPERTS // 2) as i:
                    for u in range(2):
                        e = i * 2 + u
                        for j in range(2):
                            dve.wait_ge(S("silu_done"), e * 2 + (j + 1 + 2 * EXPERTS * l))
                            tt(actT[u][:, j, :], sg[:, j, :], psum[:, 2 * j + 1, 0:T], ALU.mult)\
                                .then_inc(S("act_ready"), 1)
                        for q in range(6):
                            c, half = q // 2, slice(q % 2 * 512, q % 2 * 512 + 512)
                            dve.wait_ge(S("y_computed"), e * 6 + (q + 1 + 6 * EXPERTS * l))
                            stt(yacc[:, c, half], psum[:, 4 + (6 * u + q) % 4, :], comb[:, c, bass.ds(e, 1)],
                                yacc[:, c, half], ALU.mult, ALU.add).then_inc(S("y_taken"), 1)
                        dve.wait_ge(S("y_taken"), e * 6 + (10 + (6 * EXPERTS + 4) * l))

            residual("o", 0, 2)
            norm(1)
            router(0)
            experts(0)
            residual("yt", 0, 5)
            done(v.memset(cin, 0.0), "pads")
            norm(2)

            for i in range(CONV_TILES):
                if i < 8:
                    wcol = [colsT[:, w * 8 + i:w * 8 + i + 1] for w in range(CONV_W)]
                    bcol = colsT[:, 100 + i:101 + i]
                else:
                    wcol = [colsT[:, 40 + w * 12 + i - 8:41 + w * 12 + i - 8] for w in range(CONV_W)]
                    bcol = colsT[:, 108 + i - 8:109 + i - 8]
                dve.wait_ge(*taken("xb", i))
                o_(ts(conv[:, i, :], cin[:, i, 0:COUT], wcol[0], bcol, ALU.mult, ALU.add))
                for w in range(1, CONV_W):
                    ins = stt(conv[:, i, :], cin[:, i, w:w + COUT], wcol[w], conv[:, i, :], ALU.mult, ALU.add)
                    o_(ins) if w < CONV_W - 1 else done(ins, "conv_tile")
            dve.wait_ge(S("conv_act"), CONV_TILES)
            done(v.memset(ms3, 0.0), "conv_done")

            for i in range(8):
                dve.wait_ge(*taken("l2", i))
                o_(v.reciprocal(l2[:, i, :], l2[:, i, :]))
            o_(stt(conv[:, 8:12, :], conv[:, 8:12, :], DK ** -0.5, l2[:, 0:4, :], ALU.mult, ALU.mult))
            done(tt(conv[:, 12:16, :], conv[:, 12:16, :], l2[:, 4:8, :], ALU.mult), "l2_done")

            for c in range(TILES):
                for name, dst, n in (("tx", xN, 512), ("tB", BN, 256), ("tk", gk, 512), ("tv", gv, 512)):
                    dve.wait_ge(*computed(name, c))
                    take(v.tensor_copy(dst[:, c, :], bank(name, c)[:, 0:n]), name, c)
            dve.wait_ge(*taken("dg"))
            for d in range(2):
                for lo, n, src in ((0, 8, dg[:, :, 8 * d:8 * d + 8]), (8, 4, dg[:, :, 16 + 4 * d:20 + 4 * d])):
                    o_(tt(spin[:, d, :, lo:lo + n], src, bc(bias_o[:, d, lo:lo + n], 1, [P, TILES, n]), ALU.add))
            done(stt(sp, spin, -1.0, spin, ALU.mult, ALU.max), "sp_in")
            o_(ts(spin, spin, 0.0, None, ALU.max))
            dve.wait_ge(S("sp_ln"), 1)
            o_(tt(sp, sp, spin, ALU.add))
            dve.wait_ge(S("wA"), 1)
            o_(ts(wA, wA, -1.0, None, ALU.mult))
            for d in range(2):
                ins = tt(lg[:, d], sp[:, d], bc(wA[:, 12 * d:12 * d + 12], 1, [P, TILES, 12]), ALU.mult)
                o_(ins) if d == 0 else done(ins, "log_decay2")
            done(v.memset(ms3, 0.0), "log_decay")
            dve.wait_ge(*computed("cum", 1))
            o_(v.tensor_copy(cb.rearrange("p d c h -> p (d c h)"), bank("cum", 1)[:, 0:72]))
            take(v.tensor_copy(tot.rearrange("p d c h -> p (d c h)"), bank("cum", 1)[:, 72:144]), "cum", 1)
            o_(tt(edif, tot, cb, ALU.subtract))
            done(ts(ncb, cb, -1.0, None, ALU.mult), "odd_cum")
            dve.wait_ge(S("odd_exps"), 1)
            dve.wait_ge(S("beta"), 1)
            done(tt(edb, edif[:, :, :, 8:12], beta, ALU.mult), "odd_gates")
            for d in range(2):
                dve.wait_ge(*computed("h0T", d))
                take(v.tensor_copy(hsT[:, 1, d, :], bank("h0T", d)), "h0T", d)
            dve.wait_ge(S("gdn_in"), 32)

            for u, (d, c) in enumerate(units):
                s = int(c > 0)
                first = (d, c) in ((0, 0), (0, 1), (1, 2))
                update = c == 0 or first_chunk(d, c)

                def b8(ap):
                    return bc(ap, 2, [P, 8, SSD_P])

                if u:
                    dve.wait_ge(*computed("Y1", u - 1))
                for g in range(2):
                    dve.wait_ge(*computed("Es", u, g))
                    take(tt(heads(E1, 4), heads(bank("Es", u, g), 4), bc(neg_st[d], 1, [P, 4, P]), ALU.add), "Es", u, g)
                    done(v.memset(ms3, 0.0), "e_masked")
                    dve.wait_ge(S("e_done"), 3 * u + g + 1)
                    dve.wait_ge(*computed("GB", u, g))
                    take(tt(heads(G[:, g * 512:(g + 1) * 512], 4), heads(E1, 4),
                            bc(bank("GB", u, g)[:, 0:P], 1, [P, 4, P]), ALU.mult), "GB", u, g)
                o_(tt(heads(xdt, 8), heads(xN[:, c, :], 8), b8(sp[:, d, c, 0:8]), ALU.mult))
                o_(tt(heads(xw, 8), heads(xdt, 8), b8(edif[:, d, c, 0:8]), ALU.mult))
                done(v.memset(ms3, 0.0), "ssd_in")
                dve.wait_ge(*computed("Y1", u))
                ys = ysum[:, c, :]
                if first:
                    take(v.tensor_copy(ys, bank("Y1", u)), "Y1", u)
                else:
                    take(tt(ys, ys, bank("Y1", u), ALU.add), "Y1", u)
                if c:
                    dve.wait_ge(*computed("Y2", u))
                    take(tt(heads(y2, 8), heads(bank("Y2", u), 8), b8(ecb[:, d, c, 0:8]), ALU.mult), "Y2", u)
                    o_(tt(ys, ys, y2, ALU.add))
                hs = hsT[:, s, d, :]
                if update:
                    dve.wait_ge(*computed("HU", u))
                    if c:
                        o_(tt(heads(hs, 8), heads(hs, 8), b8(etot[:, d, c, 0:8]), ALU.mult))
                        take(tt(hs, hs, bank("HU", u), ALU.add), "HU", u)
                    else:
                        take(v.tensor_copy(hs, bank("HU", u)), "HU", u)
                    done(v.memset(ms3, 0.0), "ssd_updated")

                dve.wait_ge(*computed("Eg", u))
                take(tt(heads(EB, 4), heads(bank("Eg", u), 4), bc(neg_st[d], 1, [P, 4, P]), ALU.add), "Eg", u)
                done(v.memset(ms3, 0.0), "e_masked")
                dve.wait_ge(S("e_done"), 3 * u + 3)
                o_(tt(heads(EB, 4), heads(EB, 4), b4(beta[:, d, c]), ALU.mult))
                dve.wait_ge(*computed("KK", u))
                take(tt(AT, EB, bank("KK", u), ALU.mult), "KK", u)
                dve.wait_ge(*computed("KQ", u))
                take(tt(PT, EB, bank("KQ", u), ALU.mult), "KQ", u)
                o_(tt(heads(LT, 4), heads(AT, 4), bc(lvl[0], 1, [P, 4, P]), ALU.mult))
                done(tt(heads(XT, 4), bc(ident, 1, [P, 4, P]), heads(LT, 4), ALU.subtract), "xt_new")
                for n in range(1, 7):
                    if n > 1:
                        dve.wait_ge(*computed("T1", u, n - 1))
                    done(tt(heads(LT, 4), heads(AT, 4), bc(lvl[n], 1, [P, 4, P]), ALU.mult), "lt")
                    dve.wait_ge(*computed("XT", u, n))
                    if n < 6:
                        dve.wait_ge(*computed("XX", u, n))
                    take(tt(XT, XT, bank("XT", u, n), ALU.subtract), "XT", u, n)
                    done(v.memset(ms3, 0.0), "xt_new")
                    if n < 6:
                        dve.wait_ge(*taken("X0", u))
                        take(tt(X, X, bank("XX", u, n), ALU.subtract), "XX", u, n)
                if c:
                    dve.wait_ge(*computed("KS", u))
                    take(tt(heads(Rg, 4), heads(bank("KS", u), 4), b4(ecb[:, d, c, 8:12]), ALU.mult), "KS", u)
                    done(tt(Rg, gv[:, c, :], Rg, ALU.subtract), "rhs")
                og = ogsum[:, c, :]
                dve.wait_ge(*taken("U", u))
                if update:
                    done(tt(heads(Uw, 4), heads(U, 4), b4(edb[:, d, c]), ALU.mult), "uw")
                dve.wait_ge(*computed("O1", u))
                if first:
                    take(v.tensor_copy(og, bank("O1", u)), "O1", u)
                else:
                    take(tt(og, og, bank("O1", u), ALU.add), "O1", u)
                if c:
                    dve.wait_ge(*computed("O2", u))
                    take(tt(heads(y2, 4), heads(bank("O2", u), 4), b4(ecb[:, d, c, 8:12]), ALU.mult), "O2", u)
                    o_(tt(og, og, y2, ALU.add))
                sg_ = Sg[:, s, d, :]
                if update:
                    dve.wait_ge(*computed("SU", u))
                    if c:
                        o_(tt(heads(sg_, 4), heads(sg_, 4), b4(etot[:, d, c, 8:12]), ALU.mult))
                        take(tt(sg_, sg_, bank("SU", u), ALU.add), "SU", u)
                    else:
                        take(v.tensor_copy(sg_, bank("SU", u)), "SU", u)
                        done(v.memset(ms3, 0.0), "gdn_state")
                    done(v.memset(ms3, 0.0), "gdn_updated")

            dve.wait_ge(S("odd_in"), 64)
            scr = G[:, 0:512]
            for c in range(TILES):
                o_(tt(heads(y2, 8), heads(xN[:, c, :], 8), bc(dskip[:], 2, [P, 8, SSD_P]), ALU.mult))
                o_(tt(ysum[:, c, :], ysum[:, c, :], y2, ALU.add))
                o_(tt(ysum[:, c, :], ysum[:, c, :], zs[:, c, :], ALU.mult))
                o_(tt(y2, ysum[:, c, :], ysum[:, c, :], ALU.mult))
                o_(v.tensor_reduce(ms3[:, c:c + 1], y2, AX, ALU.add))
                o_(tt(scr, ogsum[:, c, :], ogsum[:, c, :], ALU.mult))
                o_(v.tensor_reduce(ms12[:, 4 * c:4 * c + 4], heads(scr, 4), AX, ALU.add))
            done(v.memset(ms6, 0.0), "odd_ms")
            dve.wait_ge(S("odd_rt"), 1)
            o_(v.reciprocal(ms3, ms3))
            o_(v.reciprocal(ms12, ms12))
            o_(tt(ysum, ysum, bc(ms3, 2, [P, TILES, 512]), ALU.mult))
            done(tt(ysum, ysum, bc(gssd, 1, [P, TILES, 512]), ALU.mult), "odd_rows")
            og12 = ogsum.rearrange("p c (h n) -> p (c h) n", h=4)
            o_(tt(og12, og12, bc(ms12, 2, [P, 12, P]), ALU.mult))
            o_(tt(og12, og12, bc(ggdn, 1, [P, 12, P]), ALU.mult))
            done(tt(ogsum, ogsum, zg, ALU.mult), "odd_rows")
            residual("o", 1, 2)
            norm(3)
            router(1)
            experts(1)
            residual("yt", 1, 5)
            norm(4)
        build.free_words = room - used[1]


_INS = ['x_prompt', 'x_sample', 'c', 'cache_mla_kv', 'cache_mla_krope', 'state_mlstm_C', 'state_mlstm_n',
        'state_mlstm_m', 'state_ssd', 'state_gdn', 'c_ctx', 'ada_w', 'ada_b', 'norm_mix', 'norm_ffn',
        'w_in_even', 'ml_i_bias', 'ml_f_bias', 'ml_norm', 'mla_q_norm', 'mla_w_uq', 'mla_kv_norm', 'mla_w_ukv',
        'w_out_even', 'w_in_odd', 'ssd_conv_w', 'ssd_conv_b', 'ssd_dt_bias', 'ssd_A_log', 'ssd_D', 'ssd_norm',
        'gdn_conv_w', 'gdn_conv_b', 'gdn_dt_bias', 'gdn_A_log', 'gdn_norm', 'w_out_odd',
        'moe_w_group', 'moe_b_group', 'moe_w_expert', 'moe_b_expert', 'moe_w_gate', 'moe_w_up', 'moe_w_down',
        'norm_final']
_OUTS = [("yp", (1, PROMPT, D)), ("ys", (1, SAMPLE, D)), ("kv", (1, 1, PROMPT, KV_RANK)),
         ("krope", (1, 1, PROMPT, ROPE)), ("C", (1, 1, 2, ML_H, DK, DK)), ("n", (1, 1, 2, ML_H, DK)),
         ("m", (1, 1, 2, ML_H)), ("ssd", (1, 1, 2, SSD_H, SSD_P, SSD_N)), ("gdn", (1, 1, 2, GDN_H, DK, DK))]


def kernel(**inputs):
    import concourse.bacc as _bacc
    from concourse.bass_utils import run_bass_kernel_spmd as _run

    nc = _bacc.Bacc("TRN2", target_bir_lowering=False, num_devices=1)
    arrays, a, o = {}, {}, {}
    for name in _INS:
        x = np.ascontiguousarray(inputs[name])
        arrays[f"in_{name}"] = x
        a[name] = nc.dram_tensor(f"in_{name}", x.shape, mybir.dt.from_np(x.dtype), kind="ExternalInput").ap()
    arrays["in_consts"] = const_table()
    a["consts"] = nc.dram_tensor("in_consts", (P, C_ALL), F32, kind="ExternalInput").ap()
    for name, shape in _OUTS:
        o[name] = nc.dram_tensor(f"out_{name}", shape, F32, kind="ExternalOutput").ap()
    build(nc, a, o)
    r = _run(nc, [arrays], core_ids=[0])
    return tuple(r.results[0][f"out_{name}"] for name, _ in _OUTS)
```

```python
from contextlib import ExitStack

import numpy as np

import concourse.bass as bass
from concourse import mybir

F32 = mybir.dt.float32
I32 = mybir.dt.int32
U32 = mybir.dt.uint32
ALU = mybir.AluOpType
ACT = mybir.ActivationFunctionType
AX = mybir.AxisListType.X

P = 128
D = 1024
KD = D // P
PROMPT, SAMPLE = 128, 256
T = PROMPT + SAMPLE
TILES = T // P
SEGS = ((0, 0, PROMPT), (1, PROMPT, T))
EPS = 1e-6
NEG = -1e30

ML_H, DK = 4, 128
Q_RANK, KV_RANK, NOPE, ROPE, V_DIM, MLA_H = 384, 256, 64, 32, 64, 8
QK_DIM = NOPE + ROPE
PAST = 128
KEYS = PROMPT + PAST + SAMPLE
EVEN_TAIL = 2048
IN_EVEN = EVEN_TAIL + 16 + Q_RANK + KV_RANK + ROPE
TAIL = IN_EVEN - EVEN_TAIL
CQ0, CKV0, KPE0 = 16, 16 + Q_RANK, 16 + Q_RANK + KV_RANK

SSD_H, SSD_P, SSD_N = 8, 64, 128
GDN_H = 4
SSD_CH, GDN_CH, CONV_W = 1024, 1536, 5
Z_S, XBC, DT, QKV, Z_G, GA = 0, 512, 1536, 1552, 3088, 3600
IN_ODD = 3616
CONV_TILES = (SSD_CH + GDN_CH) // P
PAD = CONV_W // 2
CIN = PROMPT + SAMPLE + 4 * PAD
COUT = CIN - 2 * PAD
CO = (0, PROMPT + 2 * PAD, PROMPT + 2 * PAD + P)

GROUPS, EXPERTS, FF = 4, 32, 256
ROUTES = GROUPS + EXPERTS
CAP = 80
OOB = 1 << 20

BANKS = 8
RING = 3
SLOT = 4096

C_ID, C_ONE, C_UP, C_LO, C_NUP, C_NLO = (i * P for i in range(6))
C_LVL = 6 * P
C_RANK = C_LVL + 7 * P
C_COS = C_RANK + EXPERTS
C_SIN = C_COS + SAMPLE
C_ROT = C_SIN + SAMPLE
C_ALL = C_ROT + ROPE


def const_table():
    c = np.zeros((P, C_ALL), np.float32)
    row, col = np.arange(P)[:, None], np.arange(P)[None, :]
    c[:, C_ID:C_ID + P] = row == col
    c[:, C_ONE:C_ONE + P] = 1.0
    c[:, C_UP:C_UP + P] = col >= row
    c[:, C_LO:C_LO + P] = col <= row
    c[:, C_NUP:C_NUP + P] = np.where(col >= row, 0.0, NEG)
    c[:, C_NLO:C_NLO + P] = np.where(col <= row, 0.0, NEG)
    for n in range(7):
        b = 1 << n
        c[:, C_LVL + n * P:C_LVL + (n + 1) * P] = (row // (2 * b) == col // (2 * b)) & (row // b != col // b)
    c[:, C_RANK:C_RANK + EXPERTS] = EXPERTS - np.arange(EXPERTS)
    half, nf = ROPE // 2, ROPE // 4
    inv = np.float32(10000.0) ** (-np.arange(nf, dtype=np.float32) / np.float32(nf))
    t = np.arange(SAMPLE)
    for part, pos in ((0, t // 64), (1, t % 64)):
        ang = (pos.astype(np.float32)[None, :] * inv[:, None]).astype(np.float32)
        for two in range(2):
            r = NOPE + part * half + two * nf
            c[r:r + nf, C_COS:C_COS + SAMPLE] = np.cos(ang)
            c[r:r + nf, C_SIN:C_SIN + SAMPLE] = np.sin(ang)
        for f in range(nf):
            a, b = part * half + f, part * half + nf + f
            c[NOPE + b, C_ROT + a] = -1.0
            c[NOPE + a, C_ROT + b] = 1.0
    return c


def row_id_table():
    token = np.arange(P)[:, None, None] + P * np.arange(TILES)[None, None, :] + np.zeros((1, 2, 1), np.int64)
    return np.stack([token, 2 * token + np.arange(2)[None, :, None]], -1).astype(np.int32)


def scan_units():
    return [(0, 0), (1, 0), (0, 1), (1, 2), (0, 2), (1, 1)]


def first_chunk(d, c):
    return (d, c) in ((0, 1), (1, 2))


def plan_jobs():
    jobs = [("xt", k) for k in range(KD)] + [("cols",)]
    jobs += [("mod", l, i) for l in range(2) for i in range(6)]

    def norm(n):
        return [("ss", n)]

    jobs += norm(0)
    jobs += [("qT", h) for h in range(4)] + [("kT", h) for h in range(4)]
    jobs += [(n, c) for n in ("kN", "vN", "oN", "ta", "tb") for c in range(TILES)]
    jobs += [("cum", 0)]
    for u, (d, c) in enumerate(scan_units()):
        jobs += [(n, u) for n in ("R", "MR", "SK", "N1", "DN")]
        if c:
            jobs += [("N2", u)]
        if c == 0 or first_chunk(d, c):
            jobs += [("CU", u), ("NU", u)]
    jobs += [("hmT", h) for h in range(4)]
    jobs += [("cqT", k) for k in range(3)] + [("kvT", k) for k in range(2)] + [("kpT",), ("kpR",)]
    jobs += [("qf", h) for h in range(MLA_H)] + [("qR", i) for i in range(4)]
    jobs += [("kn", h) for h in range(MLA_H)] + [("vv", k) for k in range(4)]
    for c in range(TILES):
        for h in range(MLA_H):
            jobs += [("sc", c, h), ("pT", c, h)]
            if h % 2:
                jobs += [("pv", c, h // 2)]
    jobs += [("o", 0, m) for m in range(KD)]
    def experts(l):
        return [("rt", l), ("rk", l)] + [("hr", l, c, half) for c in range(TILES) for half in range(2)] +\
            [("yt", l, m) for m in range(KD)]

    jobs += norm(1) + experts(0)
    jobs += norm(2)
    jobs += [("zs", c) for c in range(TILES)] + [("xb", i) for i in range(CONV_TILES)]
    jobs += [("zg", c) for c in range(TILES)] + [("dg",)]
    jobs += [("l2", i) for i in range(8)]
    jobs += [(n, c) for c in range(TILES) for n in ("tx", "tB", "tk", "tv")]
    jobs += [("cum", 1)] + [("h0T", d) for d in range(2)]
    for u, (d, c) in enumerate(scan_units()):
        for g in range(2):
            jobs += [("Es", u, g), ("GB", u, g)]
        jobs += [("Y1", u)]
        if c:
            jobs += [("Y2", u)]
        if c == 0 or first_chunk(d, c):
            jobs += [("HU", u)]
        jobs += [("Eg", u), ("KK", u), ("KQ", u), ("X0", u)]
        for n in range(1, 7):
            jobs += [("T1", u, n), ("XT", u, n)] + [("XX", u, n)] * (n < 6)
        if c:
            jobs += [("KS", u)]
        jobs += [("U", u), ("O1", u)]
        if c:
            jobs += [("O2", u)]
        if c == 0 or first_chunk(d, c):
            jobs += [("SU", u)]
        if c == 0:
            jobs += [("hT", d)]
    jobs += [("mT", f) for f in range(8)]
    jobs += [("o", 1, m) for m in range(KD)]
    jobs += norm(3) + experts(1)
    jobs += norm(4) + [("fin", c, k // 4) for c in range(TILES) for k in range(0, KD, 4)]
    return jobs


def plan_weights():
    items = []
    for l in range(2):
        for i in range(6):
            items += [("ada", (l, i, half), ("mod", l, i)) for half in range(2)]
    last = [("qT", 3), ("kN", 2), ("vN", 2), ("oN", 2), ("ta", 2), ("tb", 2)]
    items += [("even", n, last[n]) for n in range(6)]
    items += [("out", (0, half), ("o", 0, KD - 1)) for half in range(2)]
    last = [("zs", 2), ("xb", 3), ("xb", 7), ("xb", 11), ("xb", 15), ("xb", 19), ("zg", 2), ("dg",)]
    items += [("odd", n, last[n]) for n in range(8)]
    items += [("out", (1, half), ("o", 1, KD - 1)) for half in range(2)]
    return items


ODD_COLS = [(Z_S, 512), (XBC, 512), (XBC + 512, 512), (QKV, 512), (QKV + 512, 512), (QKV + 1024, 512),
            (Z_G, 512)]


def build(nc, a, o):
    jobs = plan_jobs()
    job_at = {j: n for n, j in enumerate(jobs)}
    assert len(job_at) == len(jobs)
    weights = plan_weights()
    weight_at = {(w, what): n for n, (w, what, _) in enumerate(weights)}
    units = scan_units()
    es = ExitStack()
    with es:
        sems = {}

        def S(name):
            if name not in sems:
                sems[name] = es.enter_context(nc.semaphore(name))
            return sems[name]

        def sb(name, shape, dt=F32):
            return es.enter_context(nc.sbuf_tensor(name, shape, dt))

        h_dram = nc.dram_tensor("h_rows", (T, D), F32).ap()
        y_dram = nc.dram_tensor("y_rows", (2 * T, D), F32).ap()
        tab_dram = [nc.dram_tensor(f"slot_table{l}", (EXPERTS * CAP, 2), I32).ap() for l in range(2)]

        psum = es.enter_context(nc.psum_tensor("psum", [P, BANKS, 512], F32))
        full = [S(f"bank{b}_full") for b in range(BANKS)]
        free = [S(f"bank{b}_read") for b in range(BANKS)]

        def bank(*job):
            return psum[:, job_at[job] % BANKS, :]

        def computed(*job):
            n = job_at[job]
            return full[n % BANKS], n // BANKS + 1

        def taken(*job):
            n = job_at[job]
            return free[n % BANKS], n // BANKS + 1

        def x_ready(n):
            return taken(*(("xt", KD - 1), ("o", 0, KD - 1), ("yt", 0, KD - 1), ("o", 1, KD - 1), ("yt", 1, KD - 1))[n])

        def bc(ap, axis, shape):
            return ap.unsqueeze(axis).to_broadcast(shape)

        def heads(ap, h):
            return ap.rearrange("p (h n) -> p h n", h=h)

        cst = sb("cst", [P, C_ALL])
        ident, ones = cst[:, C_ID:C_ID + P], cst[:, C_ONE:C_ONE + P]
        cum01 = (cst[:, C_UP:C_UP + P], cst[:, C_LO:C_LO + P])
        neg_st = (cst[:, C_NUP:C_NUP + P], cst[:, C_NLO:C_NLO + P])
        neg_ts = (neg_st[1], neg_st[0])
        lvl = [cst[:, C_LVL + n * P:C_LVL + (n + 1) * P] for n in range(7)]
        rank = cst[:, C_RANK:C_RANK + EXPERTS]
        cosT, sinT = cst[:, C_COS:C_COS + SAMPLE], cst[:, C_SIN:C_SIN + SAMPLE]
        rot = cst[:, C_ROT:C_ROT + ROPE]

        xT = sb("xT", [P, KD, T])
        hT = sb("hT", [P, KD, T])
        mix = sb("mix", [P, KD, T])
        rB = sb("rB", [P, T])
        ring = sb("ring", [P, RING, SLOT])
        cc = sb("cc", [P, 2, KD])
        sil = sb("sil", [P, 2, KD])
        adab = sb("adab", [P, 2, 6, KD])
        gains = sb("gains", [P, 5, KD])
        modT = sb("modT", [P, 2, 6, KD, 2])
        amp = sb("amp", [P, 2, 2, KD, 2])
        rows = sb("rows", [P, P])
        colsT = sb("colsT", [P, P])
        wr = sb("wr", [P, 2, KD, ROUTES])
        br = sb("br", [P, 2, ROUTES])
        route = sb("route", [P, 12, TILES, ROUTES])
        comb = sb("comb", [P, TILES, EXPERTS])
        slots_f = sb("slots_f", [P, 6, 2, TILES])
        slots_i = sb("slots_i", [P, 2, TILES], I32)
        row_ids = sb("row_ids", [P, 2, TILES, 2], I32)
        table = sb("table", [P, EXPERTS, 2], I32)
        index = sb("index", [P, 2, 2], I32)
        sindex = [sb(f"sindex{u}", [P, 1], I32) for u in range(2)]
        unused = sb("unused", [P, EXPERTS * CAP * 2 // P], I32)
        flag = sb("flag", [1, 2], I32)
        carrier = sb("carrier", [1, 2, 2, EXPERTS], I32)
        small = sb("small", [P, 256])
        bias_e = sb("bias_e", [P, 16])
        bias_o = sb("bias_o", [P, 2, 12])
        alog = sb("alog", [P, 2, 12])
        dskip = sb("dskip", [P, SSD_H])
        mprev0 = sb("mprev0", [P, 8])
        eps = sb("eps", [P, 1])
        gain_row = sb("gain_row", [P, 1152])
        gml, gq, gkv = gain_row[:, 0:512], gain_row[:, 512:896], gain_row[:, 896:1152]
        gssd, ggdn = gain_row[:, 0:512], gain_row[:, 512:640]

        room = (nc.sbuf_usable_end - nc.sbuf_base) // 4 - 64
        arena = sb("arena", [P, room])
        used = [0, 0]

        def carve(n, at=None):
            if at is None:
                at = used[0]
                used[0] += n
            assert at + n <= room, (at, n, room)
            used[1] = max(used[1], at + n)
            return arena[:, at:at + n]

        gu = [carve(2 * KD * FF).rearrange("p (w k f) -> p w k f", w=2, k=KD) for _ in range(2)]
        dn = [carve(2 * D).rearrange("p (j d) -> p j d", j=2) for _ in range(2)]
        base = used[0]
        sg = carve(2 * T).rearrange("p (j t) -> p j t", j=2)
        actT = [carve(2 * T).rearrange("p (j t) -> p j t", j=2) for _ in range(2)]
        used[0] = base
        hrow = [carve(D) for _ in range(2)]
        hg = [carve(KD * CAP).rearrange("p (k s) -> p k s", k=KD) for _ in range(2)]
        sgs = carve(2 * CAP).rearrange("p (j s) -> p j s", j=2)
        act_s = [carve(2 * CAP).rearrange("p (j s) -> p j s", j=2) for _ in range(2)]
        yrow = [carve(D) for _ in range(2)]
        ysel = arena[:, 0:TILES * 2 * D].rearrange("p (c w d) -> p c w d", c=TILES, w=2)
        hrows = mix[:].rearrange("p k t -> p (k t)").rearrange("p (c n) -> p c n", c=TILES)
        yacc = mix[:].rearrange("p k t -> p (k t)").rearrange("p (c d) -> p c d", c=TILES)

        used[0] = 0
        tail = carve(TILES * TAIL).rearrange("p (c n) -> p c n", c=TILES)
        w_ukv = carve(2 * 1024).rearrange("p (k n) -> p k n", k=2)
        w_uq = carve(3 * 768).rearrange("p (k n) -> p k n", k=3)
        kpin = carve(QK_DIM)
        kvpast = carve(KV_RANK)
        base = used[0]
        qT = carve(4 * T).rearrange("p (h t) -> p h t", h=4)
        kT = carve(4 * T).rearrange("p (h t) -> p h t", h=4)
        kN = carve(TILES * 512).rearrange("p (c n) -> p c n", c=TILES)
        vN = carve(TILES * 512).rearrange("p (c n) -> p c n", c=TILES)
        oS = carve(TILES * 512).rearrange("p (c n) -> p c n", c=TILES)
        hsum = carve(TILES * 512).rearrange("p (c n) -> p c n", c=TILES)
        mlC = carve(4 * 512).rearrange("p (s d n) -> p s d n", s=2, d=2)
        mln = carve(16).rearrange("p (s d n) -> p s d n", s=2, d=2)
        Rm, mrt, ET, ST, num, kw, t512 = (carve(512) for _ in range(7))
        used[0] = base
        cqn = carve(TILES * Q_RANK).rearrange("p (c n) -> p c n", c=TILES)
        ckn = carve(TILES * KV_RANK).rearrange("p (c n) -> p c n", c=TILES)
        sqt = carve(TILES * Q_RANK)
        cqT = carve(3 * T).rearrange("p (k t) -> p k t", k=3)
        kvT = carve(2 * KEYS).rearrange("p (k t) -> p k t", k=2)
        qfT = carve(MLA_H * T).rearrange("p (h t) -> p h t", h=MLA_H)
        kfT = carve(MLA_H * KEYS).rearrange("p (h t) -> p h t", h=MLA_H)
        vv = carve(4 * 512).rearrange("p (k n) -> p k n", k=4)
        kpe = carve(KEYS)
        rtmp = carve(512)
        pr = carve(2 * T).rearrange("p (b t) -> p b t", b=2)
        prT = carve(2 * T).rearrange("p (b t) -> p b t", b=2)

        used[0] = 0
        conv = carve(CONV_TILES * COUT).rearrange("p (i t) -> p i t", i=CONV_TILES)
        zs = carve(TILES * 512).rearrange("p (c n) -> p c n", c=TILES)
        zg = carve(TILES * 512).rearrange("p (c n) -> p c n", c=TILES)
        dg = carve(TILES * 32).rearrange("p (c n) -> p c n", c=TILES)
        spin, sp, lg, cb, tot, ecb, etot, edif, ncb = (
            carve(72).rearrange("p (d c h) -> p d c h", d=2, c=TILES) for _ in range(9))
        beta, edb = (carve(24).rearrange("p (d c h) -> p d c h", d=2, c=TILES) for _ in range(2))
        wA = carve(24)
        base = used[0]
        cin = carve(CONV_TILES * CIN).rearrange("p (i t) -> p i t", i=CONV_TILES)
        used[0] = base
        l2 = carve(8 * COUT).rearrange("p (i t) -> p i t", i=8)
        used[0] = base
        xN = carve(TILES * 512).rearrange("p (c n) -> p c n", c=TILES)
        BN = carve(TILES * 256).rearrange("p (c n) -> p c n", c=TILES)
        hsT = carve(4 * 512).rearrange("p (s d n) -> p s d n", s=2, d=2)
        hsO = carve(2 * 512).rearrange("p (d n) -> p d n", d=2)
        Sg = carve(4 * 512).rearrange("p (s d n) -> p s d n", s=2, d=2)
        G = carve(1024)
        h0 = G.rearrange("p (d i n) -> p d i n", d=2, i=4)
        E1, xdt, xw, y2, EB, PT = (carve(512) for _ in range(6))
        AT, XT, X, LT, TT, Rg, U, Uw = (ring[:, 0, 512 * n:512 * n + 512] for n in range(8))
        hflat = hT[:].rearrange("p k t -> p (k t)")
        gk = hflat[:, 0:1536].rearrange("p (c n) -> p c n", c=TILES)
        gv = hflat[:, 1536:3072].rearrange("p (c n) -> p c n", c=TILES)
        ysum = conv[:, 0:4, :].rearrange("p i t -> p (i t)")[:, 0:1536].rearrange("p (c n) -> p c n", c=TILES)
        ogsum = conv[:, 16:20, :].rearrange("p i t -> p (i t)")[:, 0:1536].rearrange("p (c n) -> p c n", c=TILES)

        def sm(at, n):
            return small[:, at:at + n]

        li = sm(0, 24).rearrange("p (d c h) -> p d c h", d=2, c=TILES)
        lf = sm(24, 24).rearrange("p (d c h) -> p d c h", d=2, c=TILES)
        tf = sm(48, 24).rearrange("p (d c h) -> p d c h", d=2, c=TILES)
        bcum = sm(72, 24).rearrange("p (d c h) -> p d c h", d=2, c=TILES)
        btot = sm(96, 24).rearrange("p (d c h) -> p d c h", d=2, c=TILES)
        rr = sm(120, 24).rearrange("p (d c h) -> p d c h", d=2, c=TILES)
        mst = sm(144, 16).rearrange("p (s d h) -> p s d h", s=2, d=2)
        mx, mxa, nmr, aexp, emq, dec, wk, den = (sm(160 + 4 * n, 4) for n in range(8))
        den2 = sm(192, 4)
        nmall = sm(196, 4)
        ms12 = sm(200, 12)
        ms3 = sm(212, 3)
        ms6 = sm(216, 3)
        nb = sm(220, 2)
        rs = sm(222, 2)
        rsi = sm(224, 2)
        nbm = sm(226, 2)

        block = es.enter_context(nc.Block())

        def every(eng):
            count = {}

            def done(ins, name):
                count[name] = count.get(name, 0) + 1
                ins.then_inc(S(name), 1)
                eng.wait_ge(S(name), count[name])

            def take(ins, *job):
                sem, n = taken(*job)
                ins.then_inc(sem, 1)
                eng.wait_ge(sem, n)

            return done, take

        def overflow(eng, l):
            eng.wait_ge(S("flag"), l + 1)
            return eng.If(eng.value_load(flag[0:1, l:l + 1], min_val=0, max_val=1))

        @block.sync
        def _(sp):
            for c in range(TILES):
                src = a["x_prompt"][0] if c == 0 else a["x_sample"][0, (c - 1) * P:c * P, :]
                sp.dma_start(ring[:, 2, c * D:(c + 1) * D], src).then_inc(S("x_in"), 16)
            ring_full = [S(f"ring{n}_full") for n in range(RING)]

            def load(n):
                kind, what, _ = weights[n]
                slot = ring[:, n % RING, :]
                if n >= RING:
                    sp.wait_ge(*computed(*weights[n - RING][2]))
                elif n == 2:
                    sp.wait_ge(*taken("xt", KD - 1))
                if kind == "ada":
                    l, i, half = what
                    src = a["ada_w"][l].rearrange("(p k) n -> p k n", k=KD)[:, 4 * half:4 * half + 4, i * D:(i + 1) * D]
                    dst = slot.rearrange("p (k n) -> p k n", k=4)
                elif kind == "out":
                    l, half = what
                    w = a["w_out_even" if l == 0 else "w_out_odd"][0]
                    src = w.rearrange("(k p) n -> p k n", p=P)[:, 4 * half:4 * half + 4, :]
                    dst = slot.rearrange("p (k n) -> p k n", k=4)
                elif kind == "even":
                    w = a["w_in_even"][0].rearrange("(p k) n -> p k n", k=KD)
                    n0, n1 = what * 512, min(what * 512 + 512, IN_EVEN)
                    src = w[:, :, n0:n1]
                    dst = slot.rearrange("p (k n) -> p k n", k=KD)[:, :, 0:n1 - n0]
                else:
                    w = a["w_in_odd"][0].rearrange("(p k) n -> p k n", k=KD)
                    dst = slot.rearrange("p (k n) -> p k n", k=KD)
                    if what < 7:
                        n0, width = ODD_COLS[what]
                        src = w[:, :, n0:n0 + width]
                    else:
                        sp.dma_start(dst[:, :, 0:16], w[:, :, DT:DT + 16]).then_inc(ring_full[n % RING], 16)
                        src, dst = w[:, :, GA:GA + 16], dst[:, :, 16:32]
                sp.dma_start(dst, src).then_inc(ring_full[n % RING], 16)

            def h_rows_out(l):
                for c in range(TILES):
                    for half in range(2):
                        sp.wait_ge(*taken("hr", l, c, half))
                    sp.dma_start(h_dram[c * P:(c + 1) * P, :], hrows[:, c, :]).then_inc(S("h_rows_out"), 16)

            def experts(l, dense):
                wg, wu, wd = (a[n][l] for n in ("moe_w_gate", "moe_w_up", "moe_w_down"))
                kind = f"{'dense' if dense else 'gathered'}{l}_"
                per_gu, per_y = (2, 6) if dense else (2, 2)

                def load_expert(e, u):
                    for w, m in ((0, wg), (1, wu)):
                        sp.dma_start(gu[u][:, w], m[bass.ds(e, 1)].rearrange("e (p k) f -> p (e k) f", k=KD))\
                          .then_inc(S(f"{kind}gu{u}_in"), 16)
                    return lambda: sp.dma_start(dn[u], wd[bass.ds(e, 1)].rearrange("e (p j) d -> p (e j) d", j=2))\
                        .then_inc(S(f"{kind}dn{u}_in"), 16)

                for u in range(2):
                    load_expert(u, u)()
                with sp.Fori(1, EXPERTS // 2) as i:
                    for u in range(2):
                        e = i * 2 + u
                        sp.wait_ge(S(f"{kind}gu_computed"), e * per_gu - per_gu)
                        down = load_expert(e, u)
                        sp.wait_ge(S(f"{kind}y_computed"), e * per_y - per_y)
                        down()

            def moe(l):
                sp.wait_ge(*x_ready(2 * l + 1))
                if l == 0:
                    sp.wait_ge(S("even_out"), 32)
                else:
                    sp.wait_ge(S("odd_out"), 64)
                h_rows_out(l)
                experts(l, dense=False)
                with overflow(sp, l):
                    sp.wait_ge(S("y_combined"), TILES * (l + 1))
                    experts(l, dense=True)

            n_even = weight_at[("out", (0, 1))] + 1
            for n in range(n_even):
                load(n)
            moe(0)
            for n in range(n_even, len(weights)):
                load(n)
            moe(1)

        @block.gpsimd
        def _(pool):
            count = [0]

            def small_load(dst, src):
                pool.dma_start(dst, src).then_inc(S("small_in"), 16)
                count[0] += 1

            def along(v):
                return v.partition_broadcast(P)

            with nc.allow_non_contiguous_dma(reason="small vectors"):
                small_load(cst[:], a["consts"])
                small_load(row_ids[:], a["row_ids"])
                small_load(cc[:, 0, :], a["c_ctx"].rearrange("(p k) -> p k", k=KD))
                small_load(cc[:, 1, :], a["c"][0].rearrange("(p k) -> p k", k=KD))
                for l in range(2):
                    small_load(adab[:, l], a["ada_b"][l].rearrange("(i p k) -> p i k", i=6, k=KD))
                    small_load(gains[:, l, :], a["norm_mix"][l].rearrange("(p k) -> p k", k=KD))
                    small_load(gains[:, 2 + l, :], a["norm_ffn"][l].rearrange("(p k) -> p k", k=KD))
                    small_load(wr[:, l, :, 0:GROUPS], a["moe_w_group"][l].rearrange("(p k) n -> p k n", k=KD))
                    small_load(wr[:, l, :, GROUPS:ROUTES], a["moe_w_expert"][l].rearrange("(p k) n -> p k n", k=KD))
                    small_load(br[:, l, 0:GROUPS], along(a["moe_b_group"][l]))
                    small_load(br[:, l, GROUPS:ROUTES], along(a["moe_b_expert"][l]))
                small_load(gains[:, 4, :], a["norm_final"].rearrange("(p k) -> p k", k=KD))
                small_load(rows[0:40, :], a["ssd_conv_w"][0].rearrange("w (i p) -> (w i) p", p=P))
                small_load(rows[40:100, :], a["gdn_conv_w"][0].rearrange("w (i p) -> (w i) p", p=P))
                small_load(rows[100:108, :], a["ssd_conv_b"][0].rearrange("(i p) -> i p", p=P))
                small_load(rows[108:120, :], a["gdn_conv_b"][0].rearrange("(i p) -> i p", p=P))
                small_load(rows[120:128, :], a["state_mlstm_n"][0, 0].rearrange("d h k -> (d h) k"))
                small_load(bias_e[:, 0:8], along(a["ml_i_bias"][0].rearrange("d h -> (d h)")))
                small_load(bias_e[:, 8:16], along(a["ml_f_bias"][0].rearrange("d h -> (d h)")))
                for d in range(2):
                    small_load(bias_o[:, d, 0:8], along(a["ssd_dt_bias"][0, d]))
                    small_load(bias_o[:, d, 8:12], along(a["gdn_dt_bias"][0, d]))
                    small_load(alog[:, d, 0:8], along(a["ssd_A_log"][0, d]))
                    small_load(alog[:, d, 8:12], along(a["gdn_A_log"][0, d]))
                small_load(dskip[:], along(a["ssd_D"][0]))
                small_load(mprev0[:], along(a["state_mlstm_m"][0, 0].rearrange("d h -> (d h)")))
                small_load(gml, along(a["ml_norm"][0].rearrange("h v -> (h v)")))
                small_load(gq, along(a["mla_q_norm"][0]))
                small_load(gkv, along(a["mla_kv_norm"][0]))
                small_load(w_uq, a["mla_w_uq"][0].rearrange("(k p) n -> p k n", p=P))
                small_load(w_ukv, a["mla_w_ukv"][0].rearrange("(k p) n -> p k n", p=P))
                small_load(kvpast, a["cache_mla_kv"][0, 0])
                pool.dma_start(kpin[:, NOPE:QK_DIM], a["cache_mla_krope"][0, 0]).then_inc(S("small_in"), 16)
                count[0] += 1
                for d in range(2):
                    small_load(mlC[:, 1, d, :].rearrange("p (h v) -> p h v", h=4),
                               a["state_mlstm_C"][0, 0, d].rearrange("h k v -> k h v"))
                build.n_small = count[0]
                zero_row = mix[:].rearrange("p k t -> p (k t)")[:, 0:D]
                last_slot, last_token, last_choice = (pool.to_reg(n - 1) for n in (EXPERTS * CAP, T, 2 * T))
                pool.wait_ge(S("zeroed"), 1)
                for l in range(2):
                    pool.dma_start(tab_dram[l].rearrange("(p n) w -> p (n w)", p=P), unused[:]).then_inc(S("tables_empty"), 16)
                pool.dma_start(y_dram.rearrange("(p n) d -> p n d", p=P), bc(zero_row, 1, [P, 2 * T // P, D]))\
                    .then_inc(S("rows_zero"), 16)

                def gathered(l):
                    def carry(e, n, *waits):
                        for sem, value in waits:
                            pool.wait_ge(sem, value)
                        nc.gpsimd.tensor_copy(carrier[:, l, n, bass.ds(e, 1)], row_ids[0:1, 0, 0, 0:1])

                    pool.wait_ge(S("tables_empty"), 32)
                    pool.wait_ge(S("rows_zero"), 16)
                    pool.wait_ge(S("slots"), l + 1)
                    for w in range(2):
                        for c in range(TILES):
                            pool.indirect_dma_start(
                                out=tab_dram[l], out_offset=bass.IndirectOffsetOnAxis(ap=slots_i[:, w, c:c + 1].bitcast(U32), axis=0),
                                in_=row_ids[:, w, c, :], in_offset=None, bounds_check=last_slot,
                                oob_is_err=False).then_inc(S("table_set"), 16)
                    pool.wait_ge(S("table_set"), 96 * (l + 1))
                    pool.dma_start(table[0:CAP], tab_dram[l].rearrange("(e s) w -> s e w", s=CAP)).then_inc(S("table_in"), 16)
                    pool.wait_ge(S("table_in"), 16 * (l + 1))
                    pool.wait_ge(S("h_rows_out"), 16 * TILES * (l + 1))
                    pool.wait_ge(S("rows_clear"), l + 1)

                    def gather(e, u):
                        nc.gpsimd.tensor_copy(index[0:CAP, u, :], table[0:CAP, bass.ds(e, 1), :].rearrange("p e w -> p (e w)"))\
                            .then_inc(S(f"gathered{l}_index"), 1)
                        carry(e, 0, (S(f"gathered{l}_index"), e + 1))
                        pool.indirect_dma_start(
                            out=hrow[u][0:CAP, :], out_offset=None, in_=h_dram,
                            in_offset=bass.IndirectOffsetOnAxis(ap=index[0:CAP, u, 0:1].bitcast(U32), axis=0),
                            bounds_check=last_token, oob_is_err=False).then_inc(S(f"gathered{l}_hrow{u}_in"), 16)

                    def scatter(e, u):
                        carry(e, 1, (S(f"gathered{l}_sindex"), e + 1), (S(f"gathered{l}_ya"), e + 1),
                              (S(f"gathered{l}_yb"), e + 1))
                        pool.indirect_dma_start(
                            out=y_dram, out_offset=bass.IndirectOffsetOnAxis(ap=sindex[u][0:CAP, :].bitcast(U32), axis=0),
                            in_=yrow[u][0:CAP, :], in_offset=None, bounds_check=last_choice,
                            oob_is_err=False).then_inc(S(f"gathered{l}_yrow{u}_out"), 16)

                    def scatter_index(e, u):
                        nc.gpsimd.tensor_copy(sindex[u][0:CAP, :], table[0:CAP, bass.ds(e, 1), 1:2].rearrange("p e w -> p (e w)"))\
                            .then_inc(S(f"gathered{l}_sindex"), 1)

                    for u in range(2):
                        gather(u, u)
                    for u in range(2):
                        pool.wait_ge(S(f"gathered{l}_turned"), u + 1)
                        gather(u + 2, u)
                        scatter_index(u, u)
                        scatter(u, u)
                    with pool.Fori(1, EXPERTS // 2 - 1) as i:
                        for u in range(2):
                            e = i * 2 + u
                            pool.wait_ge(S(f"gathered{l}_turned"), e + 1)
                            gather(e + 2, u)
                            pool.wait_ge(S(f"gathered{l}_yrow{u}_out"), i * 16)
                            scatter_index(e, u)
                            scatter(e, u)
                    for u in range(2):
                        e = EXPERTS - 2 + u
                        pool.wait_ge(S(f"gathered{l}_yrow{u}_out"), 16 * (EXPERTS // 2 - 1))
                        scatter_index(e, u)
                        scatter(e, u)
                    for u in range(2):
                        pool.wait_ge(S(f"gathered{l}_yrow{u}_out"), 16 * EXPERTS // 2)
                    pool.dma_start(ysel, y_dram.rearrange("(c p w) d -> p c w d", c=TILES, w=2)).then_inc(S("chosen_in"), 16)

                pool.wait_ge(*taken("tb", 0))
                pool.dma_start(o["krope"][0, 0], tail[:, 0, KPE0:KPE0 + ROPE]).then_inc(S("even_out"), 16)
                for u in range(2):
                    pool.wait_ge(*taken("NU", u))
                for d in range(2):
                    pool.dma_start(o["C"][0, 0, d].rearrange("h k v -> k h v"),
                                   mlC[:, 0, d, :].rearrange("p (h v) -> p h v", h=4)).then_inc(S("ml_out"), 16)
                    pool.dma_start(o["n"][0, 0, d].rearrange("h k -> k h"), mln[:, 0, d, :]).then_inc(S("ml_out"), 16)
                pool.dma_start(o["m"][0, 0].rearrange("d h -> (d h)").unsqueeze(0),
                               mst[0:1, 0, :, :].rearrange("p d h -> p (d h)")).then_inc(S("ml_out"), 16)

                pool.wait_ge(S("kv_norm"), 1)
                pool.dma_start(o["kv"][0, 0], ckn[:, 0, :]).then_inc(S("even_out"), 16)

                gathered(0)

                pool.wait_ge(*x_ready(2))
                pool.dma_start(gssd, along(a["ssd_norm"][0])).then_inc(S("odd_in"), 16)
                pool.dma_start(ggdn, along(a["gdn_norm"][0])).then_inc(S("odd_in"), 16)
                pool.wait_ge(S("conv_tile"), CONV_TILES)
                for d in range(2):
                    pool.dma_start(h0[:, d], a["state_ssd"][0, 0, d].rearrange("(i g) q n -> (g q) i n", g=2))\
                        .then_inc(S("odd_in"), 16)
                for d in range(2):
                    pool.dma_start(Sg[:, 1, d, :].rearrange("p (h v) -> p h v", h=4),
                                   a["state_gdn"][0, 0, d].rearrange("h k v -> k h v")).then_inc(S("gdn_in"), 16)
                for d in range(2):
                    pool.wait_ge(*taken("SU", d))
                    pool.dma_start(o["gdn"][0, 0, d].rearrange("h k v -> k h v"),
                                   Sg[:, 0, d, :].rearrange("p (h v) -> p h v", h=4)).then_inc(S("odd_out"), 16)
                    pool.wait_ge(*taken("hT", d))
                    pool.dma_start(o["ssd"][0, 0, d].rearrange("(i g) q n -> (g q) i n", g=2),
                                   hsO[:, d, :].rearrange("p (i n) -> p i n", i=4)).then_inc(S("odd_out"), 16)
                gathered(1)
                for c in range(TILES):
                    pool.wait_ge(S("y_rows"), 2 * (c + 1))
                    dst = o["yp"][0] if c == 0 else o["ys"][0, (c - 1) * P:c * P, :]
                    pool.dma_start(dst, mix[:].rearrange("p k t -> p (k t)")[:, c * D:(c + 1) * D]).then_inc(S("out"), 16)
                pool.wait_ge(S("odd_out"), 64)
                pool.wait_ge(S("out"), 16 * TILES)
                pool.wait_ge(S("even_out"), 32)
                pool.wait_ge(S("ml_out"), 80)

        SMALL = 16 * build.n_small

        @block.tensor
        def _(pe):
            at = [0]
            mm = nc.tensor.matmul

            def issue(*job):
                assert jobs[at[0]] == job, (jobs[at[0]], job)
                n = at[0]
                at[0] += 1
                if n >= BANKS:
                    pe.wait_ge(free[n % BANKS], n // BANKS)
                return psum[:, n % BANKS, :]

            def ready(ins):
                n = at[0] - 1
                ins.then_inc(full[n % BANKS], 1)

            ring_count = [0] * RING
            ring_at = [0]

            def weight(kind, what):
                n = ring_at[0]
                assert weights[n][0:2] == (kind, what), (weights[n], kind, what)
                ring_at[0] += 1
                ring_count[n % RING] += 32 if (kind, what) == ("odd", 7) else 16
                pe.wait_ge(S(f"ring{n % RING}_full"), ring_count[n % RING])
                return ring[:, n % RING, :]

            def wview(slot):
                return slot.rearrange("p (k n) -> p k n", k=KD)

            def contract(out, lhs, rhs, n):
                for k in range(n):
                    ins = mm(out, lhs(k), rhs(k), start=(k == 0), stop=(k == n - 1))
                return ins

            def tok(c):
                return slice(c * P, (c + 1) * P)

            pe.wait_ge(S("small_in"), SMALL)
            pe.wait_ge(S("x_in"), 16 * TILES)
            for k in range(KD):
                b = issue("xt", k)
                for c in range(TILES):
                    ins = nc.tensor.transpose(b[:, tok(c)], ring[:, 2, c * D + k:(c + 1) * D:KD], ident)
                ready(ins)
            b = issue("cols")
            ready(nc.tensor.transpose(b[:, 0:P], rows[:], ident))

            pe.wait_ge(S("silu_c"), 1)
            for l in range(2):
                for i in range(6):
                    w = [weight("ada", (l, i, half)).rearrange("p (k n) -> p k n", k=4) for half in range(2)]
                    b = issue("mod", l, i)
                    for m in range(KD):
                        ins = contract(b[:, 2 * m:2 * m + 2], lambda k: w[k // 4][:, k % 4, m::KD],
                                       lambda k: sil[:, :, k], KD)
                    ready(ins)

            def norm(n):
                pe.wait_ge(S("squares"), n + 1)
                b = issue("ss", n)
                ready(contract(b[:, 0:T], lambda k: ones, lambda k: mix[:, k, :], KD))

            norm(0)
            pe.wait_ge(S("h"), 1)
            for n, name in ((0, "qT"), (1, "kT")):
                w = wview(weight("even", n))
                for h in range(4):
                    b = issue(name, h)
                    ready(contract(b[:, 0:T], lambda k: w[:, k, h * P:(h + 1) * P], lambda k: hT[:, k, :], KD))
            for n, name in ((1, "kN"), (2, "vN"), (3, "oN"), (4, "ta"), (5, "tb")):
                if n > 1:
                    w = wview(weight("even", n))
                width = 512 if n < 5 else IN_EVEN - 5 * 512
                for c in range(TILES):
                    b = issue(name, c)
                    ready(contract(b[:, 0:width], lambda k: hT[:, k, tok(c)], lambda k: w[:, k, 0:width], KD))

            def cumulate(n, lf_, tri, width):
                pe.wait_ge(S("log_decay"), n + 1)
                b = issue("cum", n)
                for d in range(2):
                    mm(b[:, d * width:(d + 1) * width], tri[d], lf_[:, d].rearrange("p c h -> p (c h)"),
                       start=True, stop=True)
                ready(mm(b[:, 2 * width:4 * width], ones, lf_.rearrange("p d c h -> p (d c h)"), start=True, stop=True))

            cumulate(0, lf, cum01, 12)

            def spread(b, col):
                for h in range(4):
                    ins = mm(b[:, tok(h)], col(h).to_broadcast([P, P]), ident, start=True, stop=True)
                ready(ins)

            def four(b, lhs, rhs, width=P):
                for h in range(4):
                    ins = mm(b[:, h * width:(h + 1) * width], lhs(h), rhs(h), start=True, stop=True)
                ready(ins)

            pe.wait_ge(S("r"), 1)
            for u, (d, c) in enumerate(units):
                s = int(c > 0)
                spread(issue("R", u), lambda h: rr[:, d, c, h:h + 1])
                b = issue("MR", u)
                pe.wait_ge(S("neg_m"), u + 1)
                spread(b, lambda h: nmr[:, h:h + 1])
                pe.wait_ge(*taken("kT", 3))
                four(issue("SK", u), lambda h: kT[:, h, tok(c)], lambda h: qT[:, h, tok(c)])
                b = issue("N1", u)
                pe.wait_ge(*taken("SK", u))
                pe.wait_ge(*taken("vN", 2))
                four(b, lambda h: ST[:, tok(h)], lambda h: vN[:, c, tok(h)])
                b = issue("DN", u)
                for h in range(4):
                    ins = mm(b[:, h:h + 1], ST[:, tok(h)], ones[:, 0:1], start=True, stop=True)
                if c:
                    if first_chunk(d, c):
                        pe.wait_ge(S("n_start"), 1)
                    else:
                        pe.wait_ge(*taken("NU", u - 2))
                    for h in range(4):
                        ins = mm(b[:, 4 + h:5 + h], qT[:, h, tok(c)], mln[:, 1, d, h:h + 1], start=True, stop=True)
                ready(ins)
                if c:
                    four(issue("N2", u), lambda h: qT[:, h, tok(c)], lambda h: mlC[:, 1, d, tok(h)])
                if c == 0 or first_chunk(d, c):
                    b = issue("CU", u)
                    pe.wait_ge(S("kw"), u + 1)
                    four(b, lambda h: kw[:, tok(h)], lambda h: vN[:, c, tok(h)])
                    four(issue("NU", u), lambda h: kw[:, tok(h)], lambda h: ones[:, 0:1], width=1)

            pe.wait_ge(S("hm"), 1)
            for h in range(4):
                b = issue("hmT", h)
                for c in range(TILES):
                    ins = nc.tensor.transpose(b[:, tok(c)], hsum[:, c, tok(h)], ident)
                ready(ins)

            pe.wait_ge(S("mla_norm"), 1)
            for k in range(3):
                b = issue("cqT", k)
                for c in range(TILES):
                    ins = nc.tensor.transpose(b[:, tok(c)], cqn[:, c, tok(k)], ident)
                ready(ins)
            for k in range(2):
                b = issue("kvT", k)
                for n, src in enumerate((ckn[:, 0], kvpast, ckn[:, 1], ckn[:, 2])):
                    ins = nc.tensor.transpose(b[:, tok(n)], src[:, tok(k)], ident)
                ready(ins)
            b = issue("kpT")
            for n, src in enumerate((tail[:, 0], None, tail[:, 1], tail[:, 2])):
                src = kpin[:, 0:QK_DIM] if src is None else src[:, KPE0 - NOPE:KPE0 + ROPE]
                ins = nc.tensor.transpose(b[0:QK_DIM, tok(n)], src, ident)
            ready(ins)
            b = issue("kpR")
            pe.wait_ge(*taken("kpT"))
            ready(mm(b[NOPE:QK_DIM, 0:SAMPLE], rot[NOPE:QK_DIM, :], kpe[NOPE:QK_DIM, 2 * P:4 * P], start=True, stop=True))
            for h in range(MLA_H):
                b = issue("qf", h)
                pe.wait_ge(*taken("cqT", 2))
                ready(contract(b[0:QK_DIM, 0:T], lambda k: w_uq[:, k, h * QK_DIM:(h + 1) * QK_DIM],
                               lambda k: cqT[:, k, :], 3))
            for i in range(4):
                b = issue("qR", i)
                pe.wait_ge(*taken("qf", 2 * i + 1))
                ready(mm(b[NOPE:QK_DIM, :].rearrange("p (h t) -> p h t", h=2), rot[NOPE:QK_DIM, :],
                         qfT[NOPE:QK_DIM, 2 * i:2 * i + 2, PROMPT:T], start=True, stop=True))
            for h in range(MLA_H):
                b = issue("kn", h)
                pe.wait_ge(*taken("kvT", 1))
                ready(contract(b[0:NOPE, :], lambda k: w_ukv[:, k, h * P:h * P + NOPE], lambda k: kvT[:, k, :], 2))
            for n in range(4):
                b = issue("vv", n)
                ready(contract(b[:, :].rearrange("p (h v) -> p h v", h=MLA_H), lambda k: kvT[:, k, tok(n)],
                               lambda k: w_ukv[:, k, :].rearrange("p (h v) -> p h v", h=MLA_H)[:, :, NOPE:P], 2))
            pe.wait_ge(*taken("vv", 3))
            pe.wait_ge(*taken("kn", 7))
            pe.wait_ge(S("keys"), 1)
            pe.wait_ge(S("q_rot"), 4)
            for c in range(TILES):
                tiles = [0] if c == 0 else [1, 2, 3]
                nk = len(tiles) * P
                for h in range(MLA_H):
                    n = c * MLA_H + h
                    b = issue("sc", c, h)
                    ready(mm(b[:, 0:nk], qfT[0:QK_DIM, h, tok(c)], kfT[0:QK_DIM, h, tiles[0] * P:tiles[0] * P + nk],
                             start=True, stop=True))
                    b = issue("pT", c, h)
                    pe.wait_ge(S("probs"), n + 1)
                    for t in range(len(tiles)):
                        ins = nc.tensor.transpose(b[:, tok(t)], pr[:, n % 2, tok(t)], ident)
                    ready(ins)
                    if h % 2:
                        b = issue("pv", c, h // 2)
                        for g in range(2):
                            hh = h - 1 + g
                            pe.wait_ge(*taken("pT", c, hh))
                            for t, kt in enumerate(tiles):
                                ins = mm(b[64 * g:64 * g + 64, 0:P], vv[:, kt, hh * 64:hh * 64 + 64],
                                         prT[:, (n - 1 + g) % 2, tok(t)], start=(t == 0), stop=(t == len(tiles) - 1))
                        ready(ins)

            def project_out(l):
                w = [weight("out", (l, half)).rearrange("p (k n) -> p k n", k=4) for half in range(2)]
                for m in range(KD):
                    b = issue("o", l, m)
                    ready(contract(b[:, 0:T], lambda k: w[k // 4][:, k % 4, m::KD], lambda k: mix[:, k, :], KD))

            def router(l):
                pe.wait_ge(S("h"), 2 * l + 2)
                b = issue("rt", l)
                for c in range(TILES):
                    ins = contract(b[:, c * ROUTES:(c + 1) * ROUTES], lambda k: hT[:, k, tok(c)],
                                   lambda k: wr[:, l, k, :], KD)
                ready(ins)

            def ranks(l):
                b = issue("rk", l)
                pe.wait_ge(S("chosen"), l + 1)
                for c in range(TILES):
                    for k in range(c + 1):
                        ins = mm(b[:, c * EXPERTS:(c + 1) * EXPERTS], cum01[0] if k == c else ones, comb[:, k, :],
                                 start=(k == 0), stop=(k == c))
                for k in range(TILES):
                    ins = mm(b[:, TILES * EXPERTS:(TILES + 1) * EXPERTS], ones, comb[:, k, :], start=(k == 0), stop=(k == TILES - 1))
                ready(ins)

            def rows_out(l):
                for c in range(TILES):
                    for half in range(2):
                        b = issue("hr", l, c, half)
                        for k in range(4):
                            ins = nc.tensor.transpose(b[:, tok(k)], hT[:, 4 * half + k, tok(c)], ident)
                        ready(ins)

            def clear_banks():
                for n in range(at[0] - BANKS, at[0]):
                    pe.wait_ge(free[n % BANKS], n // BANKS + 1)

            def gathered(l):
                clear_banks()
                kind = f"gathered{l}_"

                def turn(e, u, i):
                    pe.wait_ge(S(f"{kind}hrow{u}_in"), i * 16 + 16)
                    if not (isinstance(e, int) and e == 0):
                        pe.wait_ge(S(f"{kind}hg"), e)
                    for k in range(KD):
                        ins = nc.tensor.transpose(psum[:, k // 4, k % 4 * CAP:(k % 4 + 1) * CAP],
                                                  hrow[u][0:CAP, k * P:(k + 1) * P], ident[0:CAP, 0:CAP])
                    ins.then_inc(S(f"{kind}turned"), 1)

                def expert(e, u, i, more):
                    pe.wait_ge(S(f"{kind}hg"), e + 1)
                    pe.wait_ge(S(f"{kind}gu{u}_in"), i * 32 + 32)
                    for j in range(2):
                        for w in range(2):
                            ins = contract(psum[:, 2 + j, w * CAP:(w + 1) * CAP], lambda k: gu[u][:, w, k, j::2],
                                           lambda k: hg[u][:, k, :], KD)
                        ins.then_inc(S(f"{kind}gu_computed"), 1)
                    if more:
                        turn(e + 1, 1 - u, i + u)
                    pe.wait_ge(S(f"{kind}act"), e * 2 + 2)
                    pe.wait_ge(S(f"{kind}dn{u}_in"), i * 16 + 16)
                    for half in range(2):
                        ins = contract(psum[0:CAP, 4 + 2 * u + half, :], lambda j: act_s[u][:, j, :],
                                       lambda j: dn[u][:, j, half * 512:half * 512 + 512], 2)
                        ins.then_inc(S(f"{kind}y_computed"), 1)

                turn(0, 0, 0)
                with pe.Fori(0, EXPERTS // 2 - 1) as i:
                    for u in range(2):
                        expert(i * 2 + u, u, i, True)
                for u in range(2):
                    expert(EXPERTS - 2 + u, u, EXPERTS // 2 - 1, u == 0)

            def dense(l):
                kind = f"dense{l}_"
                with pe.Fori(0, EXPERTS // 2) as i:
                    for u in range(2):
                        e = i * 2 + u
                        pe.wait_ge(S(f"{kind}gu{u}_in"), i * 32 + 32)
                        for j in range(2):
                            pe.wait_ge(S(f"{kind}act"), e * 2 + (j + 1))
                            for w in range(2):
                                ins = contract(psum[:, 2 * j + w, 0:T], lambda k: gu[u][:, w, k, j::2],
                                               lambda k: hT[:, k, :], KD)
                            ins.then_inc(S(f"{kind}gu_computed"), 1)
                        pe.wait_ge(S(f"{kind}dn{u}_in"), i * 16 + 16)
                        pe.wait_ge(S(f"{kind}act"), e * 2 + 4)
                        for q in range(6):
                            c, half = q // 2, q % 2
                            pe.wait_ge(S(f"{kind}y_taken"), e * 6 + (q + 1))
                            ins = contract(psum[:, 4 + (6 * u + q) % 4, :], lambda j: actT[u][:, j, tok(c)],
                                           lambda j: dn[u][:, j, half * 512:half * 512 + 512], 2)
                            ins.then_inc(S(f"{kind}y_computed"), 1)
                pe.wait_ge(S(f"{kind}y_taken"), 6 * EXPERTS + 4)

            def moe(l):
                router(l)
                ranks(l)
                rows_out(l)
                gathered(l)
                with overflow(pe, l):
                    dense(l)
                pe.wait_ge(S("y_combined"), TILES * (l + 1))
                for m in range(KD):
                    b = issue("yt", l, m)
                    for c in range(TILES):
                        ins = nc.tensor.transpose(b[:, tok(c)], yacc[:, c, m::KD], ident)
                    ready(ins)

            for m in range(4):
                pe.wait_ge(*taken("hmT", m))
                pe.wait_ge(*taken("pv", 2, m))
            project_out(0)
            norm(1)
            moe(0)
            norm(2)

            pe.wait_ge(S("h"), 3)
            w = wview(weight("odd", 0))
            for c in range(TILES):
                b = issue("zs", c)
                ready(contract(b, lambda k: hT[:, k, tok(c)], lambda k: w[:, k, :], KD))
            for i in range(CONV_TILES):
                if i % 4 == 0:
                    w = wview(weight("odd", 1 + i // 4))
                b = issue("xb", i)
                ready(contract(b[:, 0:T], lambda k: w[:, k, tok(i % 4)], lambda k: hT[:, k, :], KD))
            w = wview(weight("odd", 6))
            for c in range(TILES):
                b = issue("zg", c)
                ready(contract(b, lambda k: hT[:, k, tok(c)], lambda k: w[:, k, :], KD))
            w = wview(weight("odd", 7))
            b = issue("dg")
            for c in range(TILES):
                ins = contract(b[:, c * 32:c * 32 + 32], lambda k: hT[:, k, tok(c)], lambda k: w[:, k, 0:32], KD)
            ready(ins)

            pe.wait_ge(S("l2_squares"), 1)
            for i in range(8):
                b = issue("l2", i)
                ready(mm(b[:, 0:COUT], ones, l2[:, i, :], start=True, stop=True))
            pe.wait_ge(S("l2_done"), 1)
            for c in range(TILES):
                for name, i0, n in (("tx", 0, 4), ("tB", 4, 2), ("tk", 12, 4), ("tv", 16, 4)):
                    b = issue(name, c)
                    for i in range(n):
                        ins = nc.tensor.transpose(b[:, tok(i)], conv[:, i0 + i, CO[c]:CO[c] + P], ident)
                    ready(ins)
            cumulate(1, lg, cum01, 36)
            pe.wait_ge(S("odd_in"), 64)
            for d in range(2):
                b = issue("h0T", d)
                for i in range(4):
                    ins = nc.tensor.transpose(b[:, tok(i)], h0[:, d, i, :], ident)
                ready(ins)

            pe.wait_ge(S("odd_gates"), 1)
            pe.wait_ge(*taken("tv", 2))
            pe.wait_ge(*taken("tk", 2))
            pe.wait_ge(*taken("h0T", 1))
            pe.wait_ge(S("gdn_in"), 32)
            for u, (d, c) in enumerate(units):
                s = int(c > 0)
                t = slice(CO[c], CO[c] + P)
                for g in range(2):
                    spread(issue("Es", u, g), lambda h: cb[:, d, c, 4 * g + h:4 * g + h + 1])
                    ready(mm(issue("GB", u, g)[:, 0:P], conv[:, 4 + g, t], conv[:, 6 + g, t], start=True, stop=True))
                b = issue("Y1", u)
                pe.wait_ge(S("ssd_in"), u + 1)
                for h in range(SSD_H):
                    ins = mm(b[:, h * SSD_P:(h + 1) * SSD_P], G[:, tok(h)], xdt[:, h * SSD_P:(h + 1) * SSD_P],
                             start=True, stop=True)
                ready(ins)
                if c:
                    b = issue("Y2", u)
                    if not first_chunk(d, c):
                        pe.wait_ge(*taken("HU", u - 2))
                    for g in range(2):
                        ins = mm(b[:, g * 256:(g + 1) * 256], conv[:, 6 + g, t], hsT[:, 1, d, g * 256:(g + 1) * 256],
                                 start=True, stop=True)
                    ready(ins)
                if c == 0 or first_chunk(d, c):
                    b = issue("HU", u)
                    for g in range(2):
                        ins = mm(b[:, g * 256:(g + 1) * 256], BN[:, c, tok(g)], xw[:, g * 256:(g + 1) * 256],
                                 start=True, stop=True)
                    ready(ins)
                spread(issue("Eg", u), lambda h: cb[:, d, c, 8 + h:9 + h])
                four(issue("KK", u), lambda h: conv[:, 12 + h, t], lambda h: conv[:, 12 + h, t])
                four(issue("KQ", u), lambda h: conv[:, 12 + h, t], lambda h: conv[:, 8 + h, t])
                b = issue("X0", u)
                pe.wait_ge(S("xt_first"), u + 1)
                for h in range(4):
                    ins = nc.tensor.transpose(b[:, tok(h)], XT[:, tok(h)], ident)
                ready(ins)
                for n in range(1, 7):
                    b = issue("T1", u, n)
                    if n == 1:
                        pe.wait_ge(*taken("X0", u))
                    else:
                        pe.wait_ge(*taken("XX", u, n - 1))
                    pe.wait_ge(S("lt"), 6 * u + n)
                    four(b, lambda h: LT[:, tok(h)], lambda h: X[:, tok(h)])
                    b = issue("XT", u, n)
                    pe.wait_ge(*taken("T1", u, n))
                    four(b, lambda h: TT[:, tok(h)], lambda h: XT[:, tok(h)])
                    if n < 6:
                        four(issue("XX", u, n), lambda h: XT[:, tok(h)], lambda h: TT[:, tok(h)])
                if c:
                    if not first_chunk(d, c):
                        pe.wait_ge(*taken("SU", u - 2))
                    four(issue("KS", u), lambda h: conv[:, 12 + h, t], lambda h: Sg[:, 1, d, tok(h)])
                b = issue("U", u)
                pe.wait_ge(*taken("XT", u, 6))
                if c:
                    pe.wait_ge(S("rhs"), 1 + [j for j, v in enumerate(units) if v[1]].index(u))
                    four(b, lambda h: XT[:, tok(h)], lambda h: Rg[:, tok(h)])
                else:
                    four(b, lambda h: XT[:, tok(h)], lambda h: gv[:, c, tok(h)])
                b = issue("O1", u)
                pe.wait_ge(*taken("U", u))
                four(b, lambda h: PT[:, tok(h)], lambda h: U[:, tok(h)])
                if c:
                    four(issue("O2", u), lambda h: conv[:, 8 + h, t], lambda h: Sg[:, 1, d, tok(h)])
                if c == 0 or first_chunk(d, c):
                    b = issue("SU", u)
                    pe.wait_ge(S("uw"), u + 1)
                    four(b, lambda h: gk[:, c, tok(h)], lambda h: Uw[:, tok(h)])
                if c == 0:
                    b = issue("hT", d)
                    pe.wait_ge(*taken("HU", u))
                    for i in range(4):
                        ins = nc.tensor.transpose(b[:, tok(i)], hsT[:, 0, d, tok(i)], ident)
                    ready(ins)

            for f in range(8):
                b = issue("mT", f)
                src = ysum if f < 4 else ogsum
                pe.wait_ge(S("odd_rows"), 1 if f < 4 else 2)
                for c in range(TILES):
                    ins = nc.tensor.transpose(b[:, tok(c)], src[:, c, tok(f % 4)], ident)
                ready(ins)
            for f in range(8):
                pe.wait_ge(*taken("mT", f))
            project_out(1)
            norm(3)
            moe(1)
            norm(4)
            pe.wait_ge(S("h"), 5)
            for c in range(TILES):
                for half in range(2):
                    b = issue("fin", c, half)
                    for k in range(4):
                        ins = nc.tensor.transpose(b[:, tok(k)], hT[:, 4 * half + k, tok(c)], ident)
                    ready(ins)
            assert at[0] == len(jobs)

        @block.scalar
        def _(act):
            done, take = every(act)
            fn = nc.scalar.activation
            act.wait_ge(S("small_in"), SMALL)
            done(fn(sil[:], cc[:], ACT.Silu), "silu_c")

            def norm(n):
                act.wait_ge(*x_ready(n))
                if n == 0:
                    act.wait_ge(S("rows_zero"), 16)
                done(fn(mix[:], xT[:], ACT.Square), "squares")
                act.wait_ge(*computed("ss", n))
                take(fn(rB[:], bank("ss", n)[:, 0:T], ACT.Sqrt, scale=1.0 / D, bias=eps[:, 0:1]), "ss", n)

            act.wait_ge(S("eps"), 1)
            norm(0)
            for h in range(4):
                act.wait_ge(*computed("qT", h))
                take(fn(qT[:, h, :], bank("qT", h)[:, 0:T], ACT.Copy, scale=DK ** -0.5), "qT", h)
            for h in range(4):
                act.wait_ge(*computed("kT", h))
                take(fn(kT[:, h, :], bank("kT", h)[:, 0:T], ACT.Copy), "kT", h)
            for c in range(TILES):
                act.wait_ge(*computed("oN", c))
                take(fn(oS[:, c, :], bank("oN", c), ACT.Sigmoid), "oN", c)
            act.wait_ge(S("f_abs"), 1)
            done(fn(tf, tf, ACT.Exp, scale=-1.0), "act_own")
            done(fn(tf, tf, ACT.Ln, bias=1.0), "f_ln")
            for u, (d, c) in enumerate(units):
                act.wait_ge(*taken("MR", u))
                for h in range(4):
                    ins = fn(ET[:, h * P:(h + 1) * P], mrt[:, h * P:(h + 1) * P], ACT.Exp, bias=rr[:, d, c, h:h + 1])
                ins.then_inc(S("et"), 1)
                act.wait_ge(S("ml_small"), u + 1)
                fn(aexp, mx, ACT.Exp)
                fn(emq, emq, ACT.Exp)
                fn(dec, dec, ACT.Exp)
                fn(wk, wk, ACT.Exp).then_inc(S("ml_exps"), 1)
            act.wait_ge(S("hm_ms"), TILES)
            done(fn(ms12, ms12, ACT.Sqrt, scale=1.0 / DK, bias=eps[:, 0:1]), "hm_rt")
            for h in range(4):
                act.wait_ge(*computed("hmT", h))
                take(fn(mix[:, h, :], bank("hmT", h)[:, 0:T], ACT.Copy), "hmT", h)
            act.wait_ge(S("mla_ms"), 1)
            fn(ms3, ms3, ACT.Sqrt, scale=1.0 / Q_RANK, bias=eps[:, 0:1])
            done(fn(ms6, ms6, ACT.Sqrt, scale=1.0 / KV_RANK, bias=eps[:, 0:1]), "mla_rt")
            for k in range(3):
                act.wait_ge(*computed("cqT", k))
                take(fn(cqT[:, k, :], bank("cqT", k)[:, 0:T], ACT.Copy), "cqT", k)
            for k in range(2):
                act.wait_ge(*computed("kvT", k))
                take(fn(kvT[:, k, :], bank("kvT", k), ACT.Copy), "kvT", k)
            act.wait_ge(*computed("kpT"))
            take(fn(kpe[NOPE:QK_DIM, :], bank("kpT")[NOPE:QK_DIM, :], ACT.Copy), "kpT")
            for h in range(MLA_H):
                act.wait_ge(*computed("qf", h))
                take(fn(qfT[0:QK_DIM, h, :], bank("qf", h)[0:QK_DIM, 0:T], ACT.Copy), "qf", h)
            for h in range(MLA_H):
                act.wait_ge(*computed("kn", h))
                take(fn(kfT[0:NOPE, h, :], bank("kn", h)[0:NOPE, :], ACT.Copy), "kn", h)
            act.wait_ge(S("k_rot"), 1)
            done(fn(kfT[NOPE:QK_DIM, :, :], bc(kpe[NOPE:QK_DIM, :], 1, [ROPE, MLA_H, KEYS]), ACT.Copy), "keys")
            scale = QK_DIM ** -0.5
            for c in range(TILES):
                nk = P if c == 0 else 3 * P
                for h in range(MLA_H):
                    n = c * MLA_H + h
                    act.wait_ge(S("score_max"), n + 1)
                    if n >= 2:
                        act.wait_ge(*computed("pT", (n - 2) // MLA_H, (n - 2) % MLA_H))
                    take(fn(pr[:, n % 2, 0:nk], bank("sc", c, h)[:, 0:nk], ACT.Exp, scale=scale,
                            bias=nb[:, n % 2:n % 2 + 1], accum_out=rs[:, n % 2:n % 2 + 1]), "sc", c, h)
                    act.wait_ge(*computed("pT", c, h))
                    take(fn(prT[:, n % 2, 0:nk], bank("pT", c, h)[:, 0:nk], ACT.Copy), "pT", c, h)
                    if h % 2:
                        act.wait_ge(*computed("pv", c, h // 2))
                        take(fn(mix[:, 4 + h // 2, c * P:(c + 1) * P], bank("pv", c, h // 2)[:, 0:P], ACT.Copy),
                             "pv", c, h // 2)

            def router(l):
                act.wait_ge(S("g_shift"), l + 1)
                done(fn(route[:, 3, :, 0:GROUPS], route[:, 3, :, 0:GROUPS], ACT.Exp), "g_exp")
                act.wait_ge(S("top_gap"), l + 1)
                done(fn(route[:, 10, :, 2:3], route[:, 10, :, 2:3], ACT.Exp), "top_exp")

            def rows_out(l):
                for c in range(TILES):
                    for half in range(2):
                        act.wait_ge(*computed("hr", l, c, half))
                        if c == 0 and half == 0:
                            act.wait_ge(*computed("ss", 2 * l + 1))
                        take(fn(hrows[:, c, 512 * half:512 * half + 512], bank("hr", l, c, half), ACT.Copy), "hr", l, c, half)

            def gathered(l):
                kind = f"gathered{l}_"

                def copy_turned(e, u):
                    act.wait_ge(S(f"{kind}turned"), e + 1)
                    fn(hg[u].rearrange("p (w k) s -> p w (k s)", w=2), psum[:, 0:2, 0:4 * CAP], ACT.Copy)\
                        .then_inc(S(f"{kind}hg"), 1)

                def expert(e, u, i, more, first):
                    for j in range(2):
                        act.wait_ge(S(f"{kind}gu_computed"), e * 2 + (j + 1))
                        fn(sgs[:, j, :], psum[:, 2 + j, 0:CAP], ACT.Silu).then_inc(S(f"{kind}silu"), 1)
                    if more:
                        copy_turned(e + 1, 1 - u)
                    act.wait_ge(S(f"{kind}y_computed"), e * 2 + 1)
                    if not first:
                        act.wait_ge(S(f"{kind}yrow{u}_out"), i * 16)
                    fn(yrow[u][0:CAP, 0:512], psum[0:CAP, 4 + 2 * u, :], ACT.Copy).then_inc(S(f"{kind}ya"), 1)

                copy_turned(0, 0)
                for u in range(2):
                    expert(u, u, 0, True, True)
                with act.Fori(1, EXPERTS // 2 - 1) as i:
                    for u in range(2):
                        expert(i * 2 + u, u, i, True, False)
                for u in range(2):
                    expert(EXPERTS - 2 + u, u, EXPERTS // 2 - 1, u == 0, False)

            def dense(l):
                with act.Fori(0, EXPERTS // 2) as i:
                    for u in range(2):
                        e = i * 2 + u
                        for j in range(2):
                            act.wait_ge(S(f"dense{l}_gu_computed"), e * 2 + (j + 1))
                            fn(sg[:, j, :], psum[:, 2 * j, 0:T], ACT.Silu).then_inc(S(f"dense{l}_silu"), 1)

            def moe(l):
                router(l)
                rows_out(l)
                gathered(l)
                with overflow(act, l):
                    dense(l)

            norm(1)
            moe(0)
            norm(2)
            for c in range(TILES):
                act.wait_ge(*computed("zs", c))
                take(fn(zs[:, c, :], bank("zs", c), ACT.Silu), "zs", c)
            act.wait_ge(S("pads"), 1)
            for i in range(CONV_TILES):
                act.wait_ge(*computed("xb", i))
                fn(cin[:, i, PAD:PAD + PROMPT], bank("xb", i)[:, 0:PROMPT], ACT.Copy)
                take(fn(cin[:, i, 3 * PAD + PROMPT:3 * PAD + T], bank("xb", i)[:, PROMPT:T], ACT.Copy), "xb", i)
            for c in range(TILES):
                act.wait_ge(*computed("zg", c))
                take(fn(zg[:, c, :], bank("zg", c), ACT.Silu), "zg", c)
            act.wait_ge(*computed("dg"))
            take(fn(dg.rearrange("p c n -> p (c n)"), bank("dg")[:, 0:TILES * 32], ACT.Copy), "dg")
            for i in range(CONV_TILES):
                act.wait_ge(S("conv_tile"), i + 1)
                done(fn(conv[:, i, :], conv[:, i, :], ACT.Silu), "conv_act")
            act.wait_ge(S("conv_tile"), CONV_TILES)
            done(fn(l2, conv[:, 8:16, :], ACT.Square), "l2_squares")
            for i in range(8):
                act.wait_ge(*computed("l2", i))
                take(fn(l2[:, i, :], bank("l2", i)[:, 0:COUT], ACT.Sqrt, bias=eps[:, 0:1]), "l2", i)
            act.wait_ge(S("sp_in"), 1)
            done(fn(sp, sp, ACT.Exp, scale=-1.0), "act_own")
            done(fn(sp, sp, ACT.Ln, bias=1.0), "sp_ln")
            fn(wA, alog[:].rearrange("p d h -> p (d h)"), ACT.Exp).then_inc(S("wA"), 1)
            for d in range(2):
                src = dg[:, :, 28 + 4 * d - 4:32 + 4 * d - 4]
                ins = fn(beta[:, d], src, ACT.Sigmoid)
            ins.then_inc(S("beta"), 1)
            act.wait_ge(S("odd_cum"), 1)
            fn(ecb, cb, ACT.Exp)
            fn(etot, tot, ACT.Exp)
            fn(edif, edif, ACT.Exp).then_inc(S("odd_exps"), 1)
            for u, (d, c) in enumerate(units):
                for g in range(2):
                    act.wait_ge(*taken("Es", u, g))
                    for h in range(4):
                        ins = fn(E1[:, h * P:(h + 1) * P], E1[:, h * P:(h + 1) * P], ACT.Exp,
                                 bias=ncb[:, d, c, 4 * g + h:4 * g + h + 1])
                    ins.then_inc(S("e_done"), 1)
                act.wait_ge(*taken("Eg", u))
                for h in range(4):
                    ins = fn(EB[:, h * P:(h + 1) * P], EB[:, h * P:(h + 1) * P], ACT.Exp,
                             bias=ncb[:, d, c, 8 + h:9 + h])
                ins.then_inc(S("e_done"), 1)
                act.wait_ge(*computed("X0", u))
                take(fn(X, bank("X0", u), ACT.Copy), "X0", u)
                for n in range(1, 7):
                    act.wait_ge(*computed("T1", u, n))
                    take(fn(TT, bank("T1", u, n), ACT.Copy), "T1", u, n)
                act.wait_ge(*computed("U", u))
                take(fn(U, bank("U", u), ACT.Copy), "U", u)
                if c == 0:
                    act.wait_ge(*computed("hT", d))
                    take(fn(hsO[:, d, :], bank("hT", d), ACT.Copy), "hT", d)
            act.wait_ge(S("odd_ms"), TILES)
            fn(ms3, ms3, ACT.Sqrt, scale=1.0 / 512, bias=eps[:, 0:1])
            done(fn(ms12, ms12, ACT.Sqrt, scale=1.0 / DK, bias=eps[:, 0:1]), "odd_rt")
            for f in range(8):
                act.wait_ge(*computed("mT", f))
                take(fn(mix[:, f, :], bank("mT", f)[:, 0:T], ACT.Copy), "mT", f)
            norm(3)
            moe(1)
            norm(4)
            for c in range(TILES):
                for half in range(2):
                    act.wait_ge(*computed("fin", c, half))
                    dst = mix[:].rearrange("p k t -> p (k t)")[:, c * D:(c + 1) * D]\
                        .rearrange("p (q k) -> p k q", k=KD)[:, 4 * half:4 * half + 4, :]
                    fn(dst, heads(bank("fin", c, half), 4), ACT.Copy).then_inc(S("y_rows"), 1)

        @block.vector
        def _(dve):
            done, take = every(dve)
            v = nc.vector
            tt, ts, stt = v.tensor_tensor, v.tensor_scalar, v.scalar_tensor_tensor
            own = "dve_own"

            def o_(ins):
                done(ins, own)

            done(v.memset(eps[:], EPS), "eps")
            o_(v.memset(unused[:], OOB))
            zero_row = mix[:].rearrange("p k t -> p (k t)")[:, 0:D]
            done(v.memset(zero_row, 0.0), "zeroed")
            o_(v.memset(kpin[:, 0:NOPE], 0.0))
            for k in range(KD):
                dve.wait_ge(*computed("xt", k))
                take(v.tensor_copy(xT[:, k, :], bank("xt", k)[:, 0:T]), "xt", k)
            dve.wait_ge(*computed("cols"))
            take(v.tensor_copy(colsT[:], bank("cols")[:, 0:P]), "cols")
            done(v.tensor_copy(mln[:, 1].rearrange("p d h -> p (d h)"), colsT[:, 120:128]), "n_start")
            for l in range(2):
                for i in range(6):
                    dve.wait_ge(*computed("mod", l, i))
                    take(tt(modT[:, l, i], bank("mod", l, i)[:, 0:16].rearrange("p (m j) -> p m j", j=2),
                            bc(adab[:, l, i, :], 2, [P, KD, 2]), ALU.add), "mod", l, i)
                for w in range(2):
                    o_(stt(amp[:, l, w], modT[:, l, 1 + 3 * w], 1.0, bc(gains[:, 2 * w + l, :], 2, [P, KD, 2]),
                           ALU.add, ALU.mult))

            def norm(n):
                dve.wait_ge(*taken("ss", n))
                o_(v.reciprocal(rB[:], rB[:]))
                o_(tt(hT[:], xT[:], bc(rB[:], 1, [P, KD, T]), ALU.mult))
                if n == 4:
                    done(tt(hT[:], hT[:], bc(gains[:, 4, :], 2, [P, KD, T]), ALU.mult), "h")
                    return
                l, w = n // 2, n % 2
                for j, t0, t1 in SEGS:
                    o_(tt(hT[:, :, t0:t1], hT[:, :, t0:t1], bc(amp[:, l, w, :, j], 2, [P, KD, t1 - t0]), ALU.mult))
                for j, t0, t1 in SEGS:
                    ins = tt(hT[:, :, t0:t1], hT[:, :, t0:t1], bc(modT[:, l, 3 * w, :, j], 2, [P, KD, t1 - t0]), ALU.add)
                    o_(ins) if j == 0 else done(ins, "h")

            def b4(ap):
                return bc(ap, 2, [P, 4, P])

            norm(0)
            for name, dst in (("kN", kN), ("vN", vN)):
                for c in range(TILES):
                    dve.wait_ge(*computed(name, c))
                    take(v.tensor_copy(dst[:, c, :], bank(name, c)), name, c)
            for c in range(TILES):
                dve.wait_ge(*computed("ta", c))
                take(v.tensor_copy(tail[:, c, 0:512], bank("ta", c)), "ta", c)
            for c in range(TILES):
                dve.wait_ge(*computed("tb", c))
                take(v.tensor_copy(tail[:, c, 512:TAIL], bank("tb", c)[:, 0:TAIL - 512]), "tb", c)
            for d in range(2):
                o_(tt(li[:, d], tail[:, :, 4 * d:4 * d + 4], bc(bias_e[:, 4 * d:4 * d + 4], 1, [P, TILES, 4]), ALU.add))
                o_(tt(lf[:, d], tail[:, :, 8 + 4 * d:12 + 4 * d], bc(bias_e[:, 8 + 4 * d:12 + 4 * d], 1, [P, TILES, 4]), ALU.add))
            done(stt(tf, lf, -1.0, lf, ALU.mult, ALU.max), "f_abs")
            o_(ts(lf, lf, 0.0, None, ALU.min))
            dve.wait_ge(S("f_ln"), 1)
            done(tt(lf, lf, tf, ALU.subtract), "log_decay")
            dve.wait_ge(*computed("cum", 0))
            take(v.tensor_copy(sm(72, 48), bank("cum", 0)[:, 0:48]), "cum", 0)
            o_(v.tensor_copy(mst[:, 1].rearrange("p d h -> p (d h)"), mprev0[:]))
            o_(v.memset(mst[:, 0], 0.0))
            done(tt(rr, li, bcum, ALU.subtract), "r")

            for u, (d, c) in enumerate(units):
                s = int(c > 0)
                m = mst[:, s, d]
                dve.wait_ge(*computed("R", u))
                if u:
                    dve.wait_ge(S("ml_exps"), u)
                o_(v.tensor_reduce(mxa, heads(bank("R", u), 4), AX, ALU.max))
                take(tt(heads(Rm, 4), heads(bank("R", u), 4), bc(neg_ts[d], 1, [P, 4, P]), ALU.add), "R", u)
                o_(v.tensor_reduce(mx, heads(Rm, 4), AX, ALU.max))
                o_(tt(mx, mx, m, ALU.max))
                done(ts(nmr, mx, -1.0, None, ALU.mult), "neg_m")
                o_(tt(mxa, mxa, m, ALU.max))
                o_(tt(emq, nmr, bcum[:, d, c], ALU.subtract))
                o_(tt(dec, m, mxa, ALU.subtract))
                o_(tt(mx, m, mx, ALU.subtract))
                o_(tt(m, mxa, btot[:, d, c], ALU.add))
                done(tt(wk, rr[:, d, c], mxa, ALU.subtract), "ml_small")
                dve.wait_ge(*computed("MR", u))
                if u:
                    dve.wait_ge(S("et"), u)
                ins = tt(heads(mrt, 4), heads(bank("MR", u), 4), bc(neg_st[d], 1, [P, 4, P]), ALU.add)
                take(ins, "MR", u)
                dve.wait_ge(*computed("SK", u))
                dve.wait_ge(S("et"), u + 1)
                take(tt(ST, ET, bank("SK", u), ALU.mult), "SK", u)
                dve.wait_ge(S("ml_exps"), u + 1)
                if c == 0 or first_chunk(d, c):
                    done(tt(heads(kw, 4), heads(kN[:, c, :], 4), b4(wk), ALU.mult), "kw")
                dve.wait_ge(*computed("N1", u))
                take(v.tensor_copy(num, bank("N1", u)), "N1", u)
                dve.wait_ge(*computed("DN", u))
                if c:
                    o_(tt(den, aexp, bank("DN", u)[:, 4:8], ALU.mult))
                    take(tt(den, den, bank("DN", u)[:, 0:4], ALU.add), "DN", u)
                    dve.wait_ge(*computed("N2", u))
                    take(tt(heads(t512, 4), heads(bank("N2", u), 4), b4(aexp), ALU.mult), "N2", u)
                    o_(tt(num, num, t512, ALU.add))
                else:
                    take(v.tensor_copy(den, bank("DN", u)[:, 0:4]), "DN", u)
                o_(stt(den, den, -1.0, den, ALU.mult, ALU.max))
                o_(tt(den, den, emq, ALU.max))
                o_(v.reciprocal(den2, den))
                first = (d, c) in ((0, 0), (0, 1), (1, 2))
                if first:
                    o_(tt(heads(hsum[:, c, :], 4), heads(num, 4), b4(den2), ALU.mult))
                else:
                    o_(tt(heads(num, 4), heads(num, 4), b4(den2), ALU.mult))
                    o_(tt(hsum[:, c, :], hsum[:, c, :], num, ALU.add))
                if c == 0:
                    dve.wait_ge(*computed("CU", u))
                    take(v.tensor_copy(mlC[:, 0, d, :], bank("CU", u)), "CU", u)
                    dve.wait_ge(*computed("NU", u))
                    take(v.tensor_copy(mln[:, 0, d, :], bank("NU", u)[:, 0:4]), "NU", u)
                elif first_chunk(d, c):
                    dve.wait_ge(*computed("CU", u))
                    o_(tt(heads(mlC[:, 1, d, :], 4), heads(mlC[:, 1, d, :], 4), b4(dec), ALU.mult))
                    take(tt(mlC[:, 1, d, :], mlC[:, 1, d, :], bank("CU", u), ALU.add), "CU", u)
                    o_(tt(mln[:, 1, d, :], mln[:, 1, d, :], dec, ALU.mult))
                    dve.wait_ge(*computed("NU", u))
                    take(tt(mln[:, 1, d, :], mln[:, 1, d, :], bank("NU", u)[:, 0:4], ALU.add), "NU", u)

            h12 = hsum.rearrange("p c (h n) -> p (c h) n", h=4)
            for c in range(TILES):
                o_(tt(t512, hsum[:, c, :], hsum[:, c, :], ALU.mult))
                done(v.tensor_reduce(ms12[:, 4 * c:4 * c + 4], heads(t512, 4), AX, ALU.add), "hm_ms")
            dve.wait_ge(S("hm_rt"), 1)
            o_(v.reciprocal(ms12, ms12))
            o_(tt(h12, h12, bc(ms12, 2, [P, 12, P]), ALU.mult))
            o_(tt(hsum, hsum, bc(gml, 1, [P, TILES, 512]), ALU.mult))
            dve.wait_ge(*taken("oN", 2))
            done(tt(hsum, hsum, oS, ALU.mult), "hm")

            dve.wait_ge(*computed("hmT", 3))
            dve.wait_ge(S("ml_out"), 80)
            cq, ck = tail[:, :, CQ0:CQ0 + Q_RANK], tail[:, :, CKV0:CKV0 + KV_RANK]
            sq3 = sqt.rearrange("p (c n) -> p c n", c=TILES)
            o_(tt(sq3, cq, cq, ALU.mult))
            o_(v.tensor_reduce(ms3, sq3, AX, ALU.add))
            o_(tt(ckn, ck, ck, ALU.mult))
            done(v.tensor_reduce(ms6, ckn, AX, ALU.add), "mla_ms")
            dve.wait_ge(S("mla_rt"), 1)
            o_(v.reciprocal(ms3, ms3))
            o_(v.reciprocal(ms6, ms6))
            o_(tt(ckn, ck, bc(ms6, 2, [P, TILES, KV_RANK]), ALU.mult))
            done(tt(ckn, ckn, bc(gkv, 1, [P, TILES, KV_RANK]), ALU.mult), "kv_norm")
            o_(tt(cqn, cq, bc(ms3, 2, [P, TILES, Q_RANK]), ALU.mult))
            done(tt(cqn, cqn, bc(gq, 1, [P, TILES, Q_RANK]), ALU.mult), "mla_norm")
            r = slice(NOPE, QK_DIM)
            dve.wait_ge(*computed("kpR"))
            dve.wait_ge(*taken("kpT"))
            take(tt(rtmp[r, 0:SAMPLE], sinT[r], bank("kpR")[r, 0:SAMPLE], ALU.mult), "kpR")
            o_(tt(kpe[r, 2 * P:4 * P], kpe[r, 2 * P:4 * P], cosT[r], ALU.mult))
            done(tt(kpe[r, 2 * P:4 * P], kpe[r, 2 * P:4 * P], rtmp[r, 0:SAMPLE], ALU.add), "k_rot")
            for i in range(4):
                q = qfT[r, 2 * i:2 * i + 2, PROMPT:T]
                dve.wait_ge(*computed("qR", i))
                tmp = rtmp[r, :].rearrange("p (h t) -> p h t", h=2)
                take(tt(tmp, bc(sinT[r], 1, [ROPE, 2, SAMPLE]), bank("qR", i)[r, :].rearrange("p (h t) -> p h t", h=2),
                        ALU.mult), "qR", i)
                o_(tt(q, q, bc(cosT[r], 1, [ROPE, 2, SAMPLE]), ALU.mult))
                done(tt(q, q, tmp, ALU.add), "q_rot")
            for n in range(4):
                dve.wait_ge(*computed("vv", n))
                take(v.tensor_copy(vv[:, n, :], bank("vv", n)), "vv", n)
            scale = QK_DIM ** -0.5
            for c in range(TILES):
                nk = P if c == 0 else 3 * P
                for h in range(MLA_H):
                    n = c * MLA_H + h
                    k = n % 2
                    dve.wait_ge(*computed("sc", c, h))
                    o_(v.tensor_reduce(nbm[:, k:k + 1], bank("sc", c, h)[:, 0:nk], AX, ALU.max))
                    done(ts(nb[:, k:k + 1], nbm[:, k:k + 1], -scale, None, ALU.mult), "score_max")
                    dve.wait_ge(*taken("sc", c, h))
                    o_(v.reciprocal(rsi[:, k:k + 1], rs[:, k:k + 1]))
                    done(ts(pr[:, k, 0:nk], pr[:, k, 0:nk], rsi[:, k:k + 1], None, ALU.mult), "probs")

            def residual(name, l, part):
                for m in range(KD):
                    dve.wait_ge(*computed(name, l, m))
                    for j, t0, t1 in SEGS:
                        ins = stt(xT[:, m, t0:t1], bank(name, l, m)[:, t0:t1], modT[:, l, part, m, j:j + 1],
                                  xT[:, m, t0:t1], ALU.mult, ALU.add)
                    take(ins, name, l, m)

            def router(l):
                R = [route[:, n] for n in range(12)]
                sh = [P, TILES, GROUPS]

                def col(n, k=0):
                    return R[10][:, :, n:n + 1] if k == 0 else R[10][:, :, n:n + 1].to_broadcast([P, TILES, k])

                dve.wait_ge(*computed("rt", l))
                take(tt(R[0], bank("rt", l)[:, 0:TILES * ROUTES].rearrange("p (c n) -> p c n", c=TILES),
                        bc(br[:, l, :], 1, [P, TILES, ROUTES]), ALU.add), "rt", l)
                g, el = R[0][:, :, 0:GROUPS], R[0][:, :, GROUPS:ROUTES]

                def first_max(dst, top, src, n, sc):
                    rk = rank[:, EXPERTS - n:EXPERTS]
                    o_(v.tensor_reduce(col(top), src, AX, ALU.max))
                    o_(tt(dst, src, col(top, n), ALU.is_equal))
                    o_(tt(dst, dst, bc(rk, 1, [P, TILES, n]), ALU.mult))
                    o_(v.tensor_reduce(col(sc), dst, AX, ALU.max))
                    o_(tt(dst, dst, col(sc, n), ALU.is_equal))

                gs = R[1][:, :, 0:GROUPS]
                first_max(gs, 0, g, GROUPS, 9)
                done(tt(R[3][:, :, 0:GROUPS], g, col(0, GROUPS), ALU.subtract), "g_shift")
                pen = R[2][:, :, 0:GROUPS]
                o_(ts(pen, gs, -NEG, NEG, ALU.mult, ALU.add))
                em = R[4][:, :, 0:EXPERTS]

                def by_group(x):
                    return x.rearrange("p c (g e) -> p c g e", g=GROUPS)

                full4 = [P, TILES, GROUPS, EXPERTS // GROUPS]
                o_(tt(by_group(em), by_group(el), bc(gs, 3, full4), ALU.mult))
                o_(tt(by_group(em), by_group(em), bc(pen, 3, full4), ALU.add))
                o1, o2 = R[5][:, :, 0:EXPERTS], R[6][:, :, 0:EXPERTS]
                first_max(o1, 3, em, EXPERTS, 9)
                o_(stt(em, o1, 2 * NEG, em, ALU.mult, ALU.add))
                first_max(o2, 4, em, EXPERTS, 9)
                done(tt(col(2), col(4), col(3), ALU.subtract), "top_gap")
                done(tt(comb[:], o1, o2, ALU.add), "chosen")
                oh = [o1, o2]
                rk, ex, keep, slot, wt = (slots_f[:, n] for n in range(5))
                prod = R[7][:, :, 0:EXPERTS]
                for w in range(2):
                    o_(tt(prod, oh[w], bc(rank, 1, [P, TILES, EXPERTS]), ALU.mult))
                    o_(v.tensor_reduce(ex[:, w, :], prod, AX, ALU.max))
                dve.wait_ge(*computed("rk", l))
                for w in range(2):
                    o_(tt(prod, oh[w], bank("rk", l)[:, 0:TILES * EXPERTS].rearrange("p (c e) -> p c e", c=TILES), ALU.mult))
                    o_(v.tensor_reduce(rk[:, w, :], prod, AX, ALU.max))
                inc = R[8][:, :, 0:EXPERTS]
                o_(ts(inc, bank("rk", l)[:, 0:TILES * EXPERTS].rearrange("p (c e) -> p c e", c=TILES), CAP + 0.5, None, ALU.is_gt))
                take(v.tensor_reduce(slots_f[:, 5, 0, 0:1], bank("rk", l)[:, TILES * EXPERTS:(TILES + 1) * EXPERTS], AX, ALU.max), "rk", l)
                done(ts(flag[0:1, l:l + 1], slots_f[0:1, 5, 0, 0:1], CAP + 0.5, None, ALU.is_gt), "flag")
                o_(ts(keep, rk, CAP + 0.5, None, ALU.is_le))
                o_(stt(slot, ex, -float(CAP), rk, ALU.mult, ALU.add))
                o_(ts(slot, slot, float(EXPERTS * CAP - 1 - OOB), None, ALU.add))
                o_(tt(slot, slot, keep, ALU.mult))
                o_(ts(slot, slot, float(OOB), None, ALU.add))
                done(v.tensor_copy(slots_i[:], slot), "slots")
                dve.wait_ge(S("g_exp"), l + 1)
                o_(v.tensor_reduce(col(5), R[3][:, :, 0:GROUPS], AX, ALU.add))
                dve.wait_ge(S("top_exp"), l + 1)
                o_(ts(col(6), col(2), 1.0, None, ALU.add))
                o_(tt(col(6), col(6), col(5), ALU.mult))
                o_(v.reciprocal(col(7), col(6)))
                o_(tt(col(8), col(7), col(2), ALU.mult))
                for w in range(2):
                    o_(tt(wt[:, w, :], col(7 + w).rearrange("p c n -> p (c n)"), keep[:, w, :], ALU.mult))
                o_(tt(o1, o1, col(7, EXPERTS), ALU.mult))
                o_(tt(o2, o2, col(8, EXPERTS), ALU.mult))
                o_(tt(comb[:], o1, o2, ALU.add))
                o_(tt(comb[:], comb[:], inc, ALU.mult))

            def gathered(l):
                kind = f"gathered{l}_"

                def expert(e, u, i, first):
                    for j in range(2):
                        dve.wait_ge(S(f"{kind}silu"), e * 2 + (j + 1))
                        tt(act_s[u][:, j, :], sgs[:, j, :], psum[:, 2 + j, CAP:2 * CAP], ALU.mult).then_inc(S(f"{kind}act"), 1)
                    dve.wait_ge(S(f"{kind}y_computed"), e * 2 + 2)
                    if not first:
                        dve.wait_ge(S(f"{kind}yrow{u}_out"), i * 16)
                    v.tensor_copy(yrow[u][0:CAP, 512:D], psum[0:CAP, 5 + 2 * u, :]).then_inc(S(f"{kind}yb"), 1)

                for u in range(2):
                    expert(u, u, 0, True)
                with dve.Fori(1, EXPERTS // 2) as i:
                    for u in range(2):
                        expert(i * 2 + u, u, i, False)
                dve.wait_ge(S("chosen_in"), 16 * (l + 1))
                wt = slots_f[:, 4]
                for c in range(TILES):
                    o_(ts(ysel[:, c, 0, :], ysel[:, c, 0, :], wt[:, 0, c:c + 1], None, ALU.mult))
                    done(stt(yacc[:, c, :], ysel[:, c, 1, :], wt[:, 1, c:c + 1], ysel[:, c, 0, :], ALU.mult, ALU.add), "y_combined")

            def dense(l):
                kind = f"dense{l}_"
                v.memset(ms3, 0.0).then_inc(S(f"{kind}act"), 2)
                v.memset(ms6, 0.0).then_inc(S(f"{kind}y_taken"), 4)
                with dve.Fori(0, EXPERTS // 2) as i:
                    for u in range(2):
                        e = i * 2 + u
                        for j in range(2):
                            dve.wait_ge(S(f"{kind}silu"), e * 2 + (j + 1))
                            tt(actT[u][:, j, :], sg[:, j, :], psum[:, 2 * j + 1, 0:T], ALU.mult)\
                                .then_inc(S(f"{kind}act"), 1)
                        for q in range(6):
                            c, half = q // 2, slice(q % 2 * 512, q % 2 * 512 + 512)
                            dve.wait_ge(S(f"{kind}y_computed"), e * 6 + (q + 1))
                            stt(yacc[:, c, half], psum[:, 4 + (6 * u + q) % 4, :], comb[:, c, bass.ds(e, 1)],
                                yacc[:, c, half], ALU.mult, ALU.add).then_inc(S(f"{kind}y_taken"), 1)
                        dve.wait_ge(S(f"{kind}y_taken"), e * 6 + 10)

            def moe(l):
                if l == 0:
                    dve.wait_ge(S("even_out"), 32)
                else:
                    dve.wait_ge(S("odd_out"), 64)
                o_(v.memset(hrow[0], 0.0))
                done(v.memset(hrow[1], 0.0), "rows_clear")
                router(l)
                gathered(l)
                with overflow(dve, l):
                    dense(l)

            residual("o", 0, 2)
            norm(1)
            moe(0)
            residual("yt", 0, 5)
            done(v.memset(cin, 0.0), "pads")
            norm(2)

            for i in range(CONV_TILES):
                if i < 8:
                    wcol = [colsT[:, w * 8 + i:w * 8 + i + 1] for w in range(CONV_W)]
                    bcol = colsT[:, 100 + i:101 + i]
                else:
                    wcol = [colsT[:, 40 + w * 12 + i - 8:41 + w * 12 + i - 8] for w in range(CONV_W)]
                    bcol = colsT[:, 108 + i - 8:109 + i - 8]
                dve.wait_ge(*taken("xb", i))
                o_(ts(conv[:, i, :], cin[:, i, 0:COUT], wcol[0], bcol, ALU.mult, ALU.add))
                for w in range(1, CONV_W):
                    ins = stt(conv[:, i, :], cin[:, i, w:w + COUT], wcol[w], conv[:, i, :], ALU.mult, ALU.add)
                    o_(ins) if w < CONV_W - 1 else done(ins, "conv_tile")

            for i in range(8):
                dve.wait_ge(*taken("l2", i))
                o_(v.reciprocal(l2[:, i, :], l2[:, i, :]))
            o_(stt(conv[:, 8:12, :], conv[:, 8:12, :], DK ** -0.5, l2[:, 0:4, :], ALU.mult, ALU.mult))
            done(tt(conv[:, 12:16, :], conv[:, 12:16, :], l2[:, 4:8, :], ALU.mult), "l2_done")

            for c in range(TILES):
                for name, dst, n in (("tx", xN, 512), ("tB", BN, 256), ("tk", gk, 512), ("tv", gv, 512)):
                    dve.wait_ge(*computed(name, c))
                    take(v.tensor_copy(dst[:, c, :], bank(name, c)[:, 0:n]), name, c)
            dve.wait_ge(*taken("dg"))
            for d in range(2):
                for lo, n, src in ((0, 8, dg[:, :, 8 * d:8 * d + 8]), (8, 4, dg[:, :, 16 + 4 * d:20 + 4 * d])):
                    o_(tt(spin[:, d, :, lo:lo + n], src, bc(bias_o[:, d, lo:lo + n], 1, [P, TILES, n]), ALU.add))
            done(stt(sp, spin, -1.0, spin, ALU.mult, ALU.max), "sp_in")
            o_(ts(spin, spin, 0.0, None, ALU.max))
            dve.wait_ge(S("sp_ln"), 1)
            o_(tt(sp, sp, spin, ALU.add))
            dve.wait_ge(S("wA"), 1)
            o_(ts(wA, wA, -1.0, None, ALU.mult))
            for d in range(2):
                ins = tt(lg[:, d], sp[:, d], bc(wA[:, 12 * d:12 * d + 12], 1, [P, TILES, 12]), ALU.mult)
                o_(ins) if d == 0 else done(ins, "log_decay")
            dve.wait_ge(*computed("cum", 1))
            o_(v.tensor_copy(cb.rearrange("p d c h -> p (d c h)"), bank("cum", 1)[:, 0:72]))
            take(v.tensor_copy(tot.rearrange("p d c h -> p (d c h)"), bank("cum", 1)[:, 72:144]), "cum", 1)
            o_(tt(edif, tot, cb, ALU.subtract))
            done(ts(ncb, cb, -1.0, None, ALU.mult), "odd_cum")
            dve.wait_ge(S("odd_exps"), 1)
            dve.wait_ge(S("beta"), 1)
            done(tt(edb, edif[:, :, :, 8:12], beta, ALU.mult), "odd_gates")
            for d in range(2):
                dve.wait_ge(*computed("h0T", d))
                take(v.tensor_copy(hsT[:, 1, d, :], bank("h0T", d)), "h0T", d)
            dve.wait_ge(S("gdn_in"), 32)

            for u, (d, c) in enumerate(units):
                s = int(c > 0)
                first = (d, c) in ((0, 0), (0, 1), (1, 2))
                update = c == 0 or first_chunk(d, c)

                def b8(ap):
                    return bc(ap, 2, [P, 8, SSD_P])

                if u:
                    dve.wait_ge(*computed("Y1", u - 1))
                for g in range(2):
                    dve.wait_ge(*computed("Es", u, g))
                    take(tt(heads(E1, 4), heads(bank("Es", u, g), 4), bc(neg_st[d], 1, [P, 4, P]), ALU.add), "Es", u, g)
                    dve.wait_ge(S("e_done"), 3 * u + g + 1)
                    dve.wait_ge(*computed("GB", u, g))
                    take(tt(heads(G[:, g * 512:(g + 1) * 512], 4), heads(E1, 4),
                            bc(bank("GB", u, g)[:, 0:P], 1, [P, 4, P]), ALU.mult), "GB", u, g)
                o_(tt(heads(xdt, 8), heads(xN[:, c, :], 8), b8(sp[:, d, c, 0:8]), ALU.mult))
                done(tt(heads(xw, 8), heads(xdt, 8), b8(edif[:, d, c, 0:8]), ALU.mult), "ssd_in")
                dve.wait_ge(*computed("Y1", u))
                ys = ysum[:, c, :]
                if first:
                    take(v.tensor_copy(ys, bank("Y1", u)), "Y1", u)
                else:
                    take(tt(ys, ys, bank("Y1", u), ALU.add), "Y1", u)
                if c:
                    dve.wait_ge(*computed("Y2", u))
                    take(tt(heads(y2, 8), heads(bank("Y2", u), 8), b8(ecb[:, d, c, 0:8]), ALU.mult), "Y2", u)
                    o_(tt(ys, ys, y2, ALU.add))
                hs = hsT[:, s, d, :]
                if update:
                    dve.wait_ge(*computed("HU", u))
                    if c:
                        o_(tt(heads(hs, 8), heads(hs, 8), b8(etot[:, d, c, 0:8]), ALU.mult))
                        take(tt(hs, hs, bank("HU", u), ALU.add), "HU", u)
                    else:
                        take(v.tensor_copy(hs, bank("HU", u)), "HU", u)

                dve.wait_ge(*computed("Eg", u))
                take(tt(heads(EB, 4), heads(bank("Eg", u), 4), bc(neg_st[d], 1, [P, 4, P]), ALU.add), "Eg", u)
                dve.wait_ge(S("e_done"), 3 * u + 3)
                o_(tt(heads(EB, 4), heads(EB, 4), b4(beta[:, d, c]), ALU.mult))
                dve.wait_ge(*computed("KK", u))
                take(tt(AT, EB, bank("KK", u), ALU.mult), "KK", u)
                dve.wait_ge(*computed("KQ", u))
                take(tt(PT, EB, bank("KQ", u), ALU.mult), "KQ", u)
                o_(tt(heads(LT, 4), heads(AT, 4), bc(lvl[0], 1, [P, 4, P]), ALU.mult))
                done(tt(heads(XT, 4), bc(ident, 1, [P, 4, P]), heads(LT, 4), ALU.subtract), "xt_first")
                for n in range(1, 7):
                    if n > 1:
                        dve.wait_ge(*computed("T1", u, n - 1))
                    done(tt(heads(LT, 4), heads(AT, 4), bc(lvl[n], 1, [P, 4, P]), ALU.mult), "lt")
                    dve.wait_ge(*computed("XT", u, n))
                    if n < 6:
                        dve.wait_ge(*computed("XX", u, n))
                    take(tt(XT, XT, bank("XT", u, n), ALU.subtract), "XT", u, n)
                    if n < 6:
                        dve.wait_ge(*taken("X0", u))
                        take(tt(X, X, bank("XX", u, n), ALU.subtract), "XX", u, n)
                if c:
                    dve.wait_ge(*computed("KS", u))
                    take(tt(heads(Rg, 4), heads(bank("KS", u), 4), b4(ecb[:, d, c, 8:12]), ALU.mult), "KS", u)
                    done(tt(Rg, gv[:, c, :], Rg, ALU.subtract), "rhs")
                og = ogsum[:, c, :]
                dve.wait_ge(*taken("U", u))
                if update:
                    done(tt(heads(Uw, 4), heads(U, 4), b4(edb[:, d, c]), ALU.mult), "uw")
                dve.wait_ge(*computed("O1", u))
                if first:
                    take(v.tensor_copy(og, bank("O1", u)), "O1", u)
                else:
                    take(tt(og, og, bank("O1", u), ALU.add), "O1", u)
                if c:
                    dve.wait_ge(*computed("O2", u))
                    take(tt(heads(y2, 4), heads(bank("O2", u), 4), b4(ecb[:, d, c, 8:12]), ALU.mult), "O2", u)
                    o_(tt(og, og, y2, ALU.add))
                sg_ = Sg[:, s, d, :]
                if update:
                    dve.wait_ge(*computed("SU", u))
                    if c:
                        o_(tt(heads(sg_, 4), heads(sg_, 4), b4(etot[:, d, c, 8:12]), ALU.mult))
                        take(tt(sg_, sg_, bank("SU", u), ALU.add), "SU", u)
                    else:
                        take(v.tensor_copy(sg_, bank("SU", u)), "SU", u)

            dve.wait_ge(S("odd_in"), 64)
            scr = G[:, 0:512]
            for c in range(TILES):
                o_(tt(heads(y2, 8), heads(xN[:, c, :], 8), bc(dskip[:], 2, [P, 8, SSD_P]), ALU.mult))
                o_(tt(ysum[:, c, :], ysum[:, c, :], y2, ALU.add))
                o_(tt(ysum[:, c, :], ysum[:, c, :], zs[:, c, :], ALU.mult))
                o_(tt(y2, ysum[:, c, :], ysum[:, c, :], ALU.mult))
                o_(v.tensor_reduce(ms3[:, c:c + 1], y2, AX, ALU.add))
                o_(tt(scr, ogsum[:, c, :], ogsum[:, c, :], ALU.mult))
                done(v.tensor_reduce(ms12[:, 4 * c:4 * c + 4], heads(scr, 4), AX, ALU.add), "odd_ms")
            dve.wait_ge(S("odd_rt"), 1)
            o_(v.reciprocal(ms3, ms3))
            o_(v.reciprocal(ms12, ms12))
            o_(tt(ysum, ysum, bc(ms3, 2, [P, TILES, 512]), ALU.mult))
            done(tt(ysum, ysum, bc(gssd, 1, [P, TILES, 512]), ALU.mult), "odd_rows")
            og12 = ogsum.rearrange("p c (h n) -> p (c h) n", h=4)
            o_(tt(og12, og12, bc(ms12, 2, [P, 12, P]), ALU.mult))
            o_(tt(og12, og12, bc(ggdn, 1, [P, 12, P]), ALU.mult))
            done(tt(ogsum, ogsum, zg, ALU.mult), "odd_rows")
            residual("o", 1, 2)
            norm(3)
            moe(1)
            residual("yt", 1, 5)
            norm(4)
        build.free_words = room - used[1]


_INS = ['x_prompt', 'x_sample', 'c', 'cache_mla_kv', 'cache_mla_krope', 'state_mlstm_C', 'state_mlstm_n',
        'state_mlstm_m', 'state_ssd', 'state_gdn', 'c_ctx', 'ada_w', 'ada_b', 'norm_mix', 'norm_ffn',
        'w_in_even', 'ml_i_bias', 'ml_f_bias', 'ml_norm', 'mla_q_norm', 'mla_w_uq', 'mla_kv_norm', 'mla_w_ukv',
        'w_out_even', 'w_in_odd', 'ssd_conv_w', 'ssd_conv_b', 'ssd_dt_bias', 'ssd_A_log', 'ssd_D', 'ssd_norm',
        'gdn_conv_w', 'gdn_conv_b', 'gdn_dt_bias', 'gdn_A_log', 'gdn_norm', 'w_out_odd',
        'moe_w_group', 'moe_b_group', 'moe_w_expert', 'moe_b_expert', 'moe_w_gate', 'moe_w_up', 'moe_w_down',
        'norm_final']
_OUTS = [("yp", (1, PROMPT, D)), ("ys", (1, SAMPLE, D)), ("kv", (1, 1, PROMPT, KV_RANK)),
         ("krope", (1, 1, PROMPT, ROPE)), ("C", (1, 1, 2, ML_H, DK, DK)), ("n", (1, 1, 2, ML_H, DK)),
         ("m", (1, 1, 2, ML_H)), ("ssd", (1, 1, 2, SSD_H, SSD_P, SSD_N)), ("gdn", (1, 1, 2, GDN_H, DK, DK))]


def kernel(**inputs):
    import concourse.bacc as _bacc
    from concourse.bass_utils import run_bass_kernel_spmd as _run

    nc = _bacc.Bacc("TRN2", target_bir_lowering=False, num_devices=1)
    arrays, a, o = {}, {}, {}
    for name in _INS:
        x = np.ascontiguousarray(inputs[name])
        arrays[f"in_{name}"] = x
        a[name] = nc.dram_tensor(f"in_{name}", x.shape, mybir.dt.from_np(x.dtype), kind="ExternalInput").ap()
    arrays["in_row_ids"] = row_id_table()
    a["row_ids"] = nc.dram_tensor("in_row_ids", (P, 2, TILES, 2), I32, kind="ExternalInput").ap()
    arrays["in_consts"] = const_table()
    a["consts"] = nc.dram_tensor("in_consts", (P, C_ALL), F32, kind="ExternalInput").ap()
    for name, shape in _OUTS:
        o[name] = nc.dram_tensor(f"out_{name}", shape, F32, kind="ExternalOutput").ap()
    build(nc, a, o)
    r = _run(nc, [arrays], core_ids=[0])
    return tuple(r.results[0][f"out_{name}"] for name, _ in _OUTS)
```

```python
from contextlib import ExitStack

import numpy as np

import concourse.bass as bass
from concourse import mybir

F32 = mybir.dt.float32
I32 = mybir.dt.int32
U32 = mybir.dt.uint32
ALU = mybir.AluOpType
ACT = mybir.ActivationFunctionType
AX = mybir.AxisListType.X

P = 128
D = 1024
KD = D // P
PROMPT, SAMPLE = 128, 256
T = PROMPT + SAMPLE
TILES = T // P
SEGS = ((0, 0, PROMPT), (1, PROMPT, T))
EPS = 1e-6
NEG = -1e30

ML_H, DK = 4, 128
Q_RANK, KV_RANK, NOPE, ROPE, MLA_H = 384, 256, 64, 32, 8
QK_DIM = NOPE + ROPE
PAST = 128
KEYS = PROMPT + PAST + SAMPLE
EVEN_TAIL = 2048
IN_EVEN = EVEN_TAIL + 16 + Q_RANK + KV_RANK + ROPE
TAIL = IN_EVEN - EVEN_TAIL
CQ0, CKV0, KPE0 = 16, 16 + Q_RANK, 16 + Q_RANK + KV_RANK

SSD_H, SSD_P, SSD_N = 8, 64, 128
GDN_H = 4
SSD_CH, GDN_CH, CONV_W = 1024, 1536, 5
Z_S, XBC, DT, QKV, Z_G, GA = 0, 512, 1536, 1552, 3088, 3600
CONV_TILES = (SSD_CH + GDN_CH) // P
CONV_ORDER = list(range(8, CONV_TILES)) + list(range(8))
PAD = CONV_W // 2
CIN = PROMPT + SAMPLE + 4 * PAD
COUT = CIN - 2 * PAD
CO = (0, PROMPT + 2 * PAD, PROMPT + 2 * PAD + P)

GROUPS, EXPERTS, FF = 4, 32, 256
ROUTES = GROUPS + EXPERTS
CAP = 80
OOB = 1 << 20

BANKS = 8
RING = 3
SLOT = 4096

C_ID, C_ONE, C_UP, C_LO, C_NUP, C_NLO = (i * P for i in range(6))
C_LVL = 6 * P
C_RANK = C_LVL + 7 * P
C_COS = C_RANK + EXPERTS
C_SIN = C_COS + SAMPLE
C_ROT = C_SIN + SAMPLE
C_SEL = C_ROT + ROPE
C_ALL = C_SEL + 4


def const_table():
    c = np.zeros((P, C_ALL), np.float32)
    row, col = np.arange(P)[:, None], np.arange(P)[None, :]
    c[:, C_ID:C_ID + P] = row == col
    c[:, C_ONE:C_ONE + P] = 1.0
    c[:, C_UP:C_UP + P] = col >= row
    c[:, C_LO:C_LO + P] = col <= row
    c[:, C_NUP:C_NUP + P] = np.where(col >= row, 0.0, NEG)
    c[:, C_NLO:C_NLO + P] = np.where(col <= row, 0.0, NEG)
    for n in range(7):
        b = 1 << n
        c[:, C_LVL + n * P:C_LVL + (n + 1) * P] = (row // (2 * b) == col // (2 * b)) & (row // b != col // b)
    c[:, C_RANK:C_RANK + EXPERTS] = EXPERTS - np.arange(EXPERTS)
    for parity in range(2):
        for half in range(2):
            for cond in range(2):
                c[32 * (2 * parity + half) + cond, C_SEL + 2 * parity + cond] = 1.0
    half, nf = ROPE // 2, ROPE // 4
    inv = np.float32(10000.0) ** (-np.arange(nf, dtype=np.float32) / np.float32(nf))
    t = np.arange(SAMPLE)
    for part, pos in ((0, t // 64), (1, t % 64)):
        ang = (pos.astype(np.float32)[None, :] * inv[:, None]).astype(np.float32)
        for two in range(2):
            r = NOPE + part * half + two * nf
            c[r:r + nf, C_COS:C_COS + SAMPLE] = np.cos(ang)
            c[r:r + nf, C_SIN:C_SIN + SAMPLE] = np.sin(ang)
        for f in range(nf):
            a, b = part * half + f, part * half + nf + f
            c[NOPE + b, C_ROT + a] = -1.0
            c[NOPE + a, C_ROT + b] = 1.0
    return c


def row_id_table():
    token = np.arange(P)[:, None, None] + P * np.arange(TILES)[None, None, :] + np.zeros((1, 2, 1), np.int64)
    return np.stack([token, 2 * token + np.arange(2)[None, :, None]], -1).astype(np.int32)


def scan_units():
    return [(0, 0), (1, 0), (0, 1), (1, 2), (0, 2), (1, 1)]


MOD_PARTS = [(l, i) for l in range(2) for i in range(6)]
MODS_FIRST = 2


def mods_beside():
    places = [("MR", 2 * pair) for pair in range(3)] + [("cqT", 0), ("hmT", 0)]
    places += [("pT", c, h) for c, h in ((0, 1), (0, 6), (1, 2), (1, 6), (2, 2), (2, 6))]
    parts = MOD_PARTS[MODS_FIRST:]
    assert len(places) == len(parts) + 1
    return {place: [("mod", *part) for part in parts[max(n - 1, 0):n]] + [("mod_rows", *part) for part in parts[n:n + 1]]
            for n, place in enumerate(places)}


def plan_jobs():
    jobs = [("xt", k) for k in range(KD)]
    jobs += [(name, l, i) for l, i in MOD_PARTS[:MODS_FIRST] for name in ("mod_rows", "mod")]

    def norm(n):
        return [("ss", n)]

    jobs += norm(0)
    jobs += [("qT", h) for h in range(4)] + [("kT", h) for h in range(4)]
    jobs += [(n, c) for n in ("kN", "vN", "oN", "ta", "tb") for c in range(TILES)]
    jobs += [("cols",), ("cum", 0)]
    for pair in range(3):
        two = (2 * pair, 2 * pair + 1)
        for name in ("R", "MR", "SK", "N1", "DN") + ("N2",) * (pair > 0) + ("CU", "NU") * (pair < 2):
            jobs += [(name, u) for u in two]
    jobs += [("cqT", k) for k in range(3)] + [("kvT", k) for k in range(2)] + [("kpT",), ("kpR",)]
    jobs += [("hmT", h) for h in range(4)]
    jobs += [("qf", h) for h in range(MLA_H)] + [("qR", i) for i in range(4)]
    jobs += [("kn", h) for h in range(MLA_H)] + [("vv", k) for k in range(4)]
    for c in range(TILES):
        jobs += [("sc", c, 0)]
        for h in range(MLA_H):
            jobs += [("sc", c, h + 1)] * (h + 1 < MLA_H) + [("pT", c, h)]
            if h % 2:
                jobs += [("pv", c, h // 2)]
    jobs += [("o", 0, m) for m in range(KD)]
    def experts(l):
        return [("rt", l)] + [("hr", l, c, half) for c in range(TILES) for half in range(2)] + [("rk", l)] +\
            [("yt", l, m) for m in range(KD)]

    jobs += norm(1) + experts(0)
    jobs += norm(2)
    jobs += [("xb", i) for i in CONV_ORDER[:8]] + [("dg",)] + [("xb", i) for i in CONV_ORDER[8:12]] + [("cum", 1)]
    jobs += [("l2", i) for i in range(8)] + [("xb", i) for i in CONV_ORDER[12:]]
    jobs += [(n, c) for n in ("zs", "zg") for c in range(TILES)]
    jobs += [(n, c) for c in range(TILES) for n in ("tk", "tv", "tx", "tB")]
    for pair in range(3):
        two = (2 * pair, 2 * pair + 1)
        c = scan_units()[two[0]][1]
        jobs += [(n, u) for u in two for n in ("Eg", "KK", "KQ")]
        jobs += [("X0", u) for u in two]
        for n in range(1, 7):
            jobs += [("T1", u, n) for u in two]
            if n <= 2:
                jobs += [(name, u, n - 1) for u in two for name in ("Es", "GB")]
            elif n == 3:
                jobs += [("Y1", u) for u in two]
            elif n == 4 and c:
                jobs += [("Y2", u) for u in two]
            elif n == 5 and pair < 2:
                jobs += [("HU", u) for u in two]
            elif n == 6 and c:
                jobs += [(name, u) for u in two for name in ("KS", "O2")]
            jobs += [(name, u, n) for u in two for name in (("XT", "XX") if n < 6 else ("XT",))]
        jobs += [("U", u) for u in two] + [("O1", u) for u in two]
        if pair < 2:
            jobs += [("SU", u) for u in two]
        if pair == 0:
            jobs += [(name, d) for name in ("hT", "h0T") for d in range(2)]
    jobs += [("mT", f) for f in range(8)]
    jobs += [("o", 1, m) for m in range(KD)]
    jobs += norm(3) + experts(1)
    jobs += norm(4) + [("fin", c, k // 4) for c in range(TILES) for k in range(0, KD, 4)]
    beside = mods_beside()
    return [one for job in jobs for one in beside.get(job, []) + [job]]


def plan_weights():
    def ada(parts):
        return [("ada", (l, i, half), ("mod_rows", l, i)) for l, i in parts for half in range(2)]

    items = ada(MOD_PARTS[:MODS_FIRST])
    last = [("qT", 3), ("kN", 2), ("vN", 2), ("oN", 2), ("ta", 2), ("tb", 2)]
    items += [("even", n, last[n]) for n in range(6)]
    items += ada(MOD_PARTS[MODS_FIRST:])
    items += [("out", (0, half), ("o", 0, KD - 1)) for half in range(2)]
    last = [("zs", 2), ("xb", 3), ("xb", 7), ("xb", 11), ("xb", 15), ("xb", 19), ("zg", 2), ("dg",)]
    items += [("odd", n, last[n]) for n in (3, 4, 7, 5, 1, 2, 0, 6)]
    items += [("out", (1, half), ("o", 1, KD - 1)) for half in range(2)]
    return items


ODD_COLS = [(Z_S, 512), (XBC, 512), (XBC + 512, 512), (QKV, 512), (QKV + 512, 512), (QKV + 1024, 512),
            (Z_G, 512)]


def build(nc, a, o):
    jobs = plan_jobs()
    job_at = {j: n for n, j in enumerate(jobs)}
    assert len(job_at) == len(jobs)
    weights = plan_weights()
    weight_at = {(w, what): n for n, (w, what, _) in enumerate(weights)}
    units = scan_units()
    es = ExitStack()
    with es:
        sems = {}

        def S(name):
            if name not in sems:
                sems[name] = es.enter_context(nc.semaphore(name))
            return sems[name]

        def sb(name, shape, dt=F32):
            return es.enter_context(nc.sbuf_tensor(name, shape, dt))

        h_dram = nc.dram_tensor("h_rows", (T, D), F32).ap()
        y_dram = nc.dram_tensor("y_rows", (2 * T, D), F32).ap()
        tab_dram = [nc.dram_tensor(f"slot_table{l}", (EXPERTS * CAP, 2), I32).ap() for l in range(2)]

        psum = es.enter_context(nc.psum_tensor("psum", [P, BANKS, 512], F32))
        full = [S(f"bank{b}_full") for b in range(BANKS)]
        free = [S(f"bank{b}_read") for b in range(BANKS)]

        def bank(*job):
            return psum[:, job_at[job] % BANKS, :]

        def computed(*job):
            n = job_at[job]
            return full[n % BANKS], n // BANKS + 1

        def taken(*job):
            n = job_at[job]
            return free[n % BANKS], n // BANKS + 1

        def x_ready(n, k=KD - 1):
            return taken(*(("xt", k), ("o", 0, k), ("yt", 0, k), ("o", 1, k), ("yt", 1, k))[n])

        def bc(ap, axis, shape):
            return ap.unsqueeze(axis).to_broadcast(shape)

        def heads(ap, h):
            return ap.rearrange("p (h n) -> p h n", h=h)

        cst = sb("cst", [P, C_ALL])
        ident, ones = cst[:, C_ID:C_ID + P], cst[:, C_ONE:C_ONE + P]
        cum01 = (cst[:, C_UP:C_UP + P], cst[:, C_LO:C_LO + P])
        neg_st = (cst[:, C_NUP:C_NUP + P], cst[:, C_NLO:C_NLO + P])
        neg_ts = (neg_st[1], neg_st[0])
        lvl = [cst[:, C_LVL + n * P:C_LVL + (n + 1) * P] for n in range(7)]
        rank = cst[:, C_RANK:C_RANK + EXPERTS]
        cosT, sinT = cst[:, C_COS:C_COS + SAMPLE], cst[:, C_SIN:C_SIN + SAMPLE]
        rot = cst[:, C_ROT:C_ROT + ROPE]
        pick = cst[:, C_SEL:C_SEL + 4]

        xT = sb("xT", [P, KD, T])
        hT = sb("hT", [P, KD, T])
        mix = sb("mix", [P, KD, T])
        rB = sb("rB", [P, T])
        ring = sb("ring", [P, RING, SLOT])
        cc = sb("cc", [P, 2, KD])
        sil = sb("sil", [P, KD, 32])
        mod_rows = sb("mod_rows", [P, 512])
        adab = sb("adab", [P, 2, 6, KD])
        gains = sb("gains", [P, 5, KD])
        modT = sb("modT", [P, 2, 6, KD, 2])
        amp = sb("amp", [P, 2, 2, KD, 2])
        rows = sb("rows", [P, P])
        colsT = sb("colsT", [P, P])
        wr = sb("wr", [P, 2, KD, ROUTES])
        br = sb("br", [P, 2, ROUTES])
        route = sb("route", [P, 12, TILES, ROUTES])
        comb = sb("comb", [P, TILES, EXPERTS])
        slots_f = sb("slots_f", [P, 6, 2, TILES])
        slots_i = sb("slots_i", [P, 2, TILES], I32)
        row_ids = sb("row_ids", [P, 2, TILES, 2], I32)
        table = sb("table", [P, EXPERTS, 2], I32)
        index = sb("index", [P, 2, 2], I32)
        sindex = [sb(f"sindex{u}", [P, 1], I32) for u in range(2)]
        unused = sb("unused", [P, EXPERTS * CAP * 2 // P], I32)
        flag = sb("flag", [1, 2], I32)
        carrier = sb("carrier", [1, 2, 2, EXPERTS], I32)
        small = sb("small", [P, 304])
        bias_e = sb("bias_e", [P, 16])
        bias_o = sb("bias_o", [P, 2, 12])
        alog = sb("alog", [P, 2, 12])
        dskip = sb("dskip", [P, SSD_H])
        mprev0 = sb("mprev0", [P, 8])
        eps = sb("eps", [P, 1])
        gain_row = sb("gain_row", [P, 1152])
        gml, gq, gkv = gain_row[:, 0:512], gain_row[:, 512:896], gain_row[:, 896:1152]
        gssd, ggdn = gain_row[:, 0:512], gain_row[:, 512:640]

        room = (nc.sbuf_usable_end - nc.sbuf_base) // 4 - 64
        arena = sb("arena", [P, room])
        used = [0, 0]

        def carve(n, at=None):
            if at is None:
                at = used[0]
                used[0] += n
            assert at + n <= room, (at, n, room)
            used[1] = max(used[1], at + n)
            return arena[:, at:at + n]

        gu = [carve(2 * KD * FF).rearrange("p (w k f) -> p w k f", w=2, k=KD) for _ in range(2)]
        dn = [carve(2 * D).rearrange("p (j d) -> p j d", j=2) for _ in range(2)]
        base = used[0]
        sg = carve(2 * T).rearrange("p (j t) -> p j t", j=2)
        actT = [carve(2 * T).rearrange("p (j t) -> p j t", j=2) for _ in range(2)]
        used[0] = base
        hrow = [carve(D) for _ in range(2)]
        hg = [carve(KD * CAP).rearrange("p (k s) -> p k s", k=KD) for _ in range(2)]
        sgs = carve(2 * CAP).rearrange("p (j s) -> p j s", j=2)
        act_s = [carve(2 * CAP).rearrange("p (j s) -> p j s", j=2) for _ in range(2)]
        yrow = [carve(D) for _ in range(2)]
        used[0] = base + 3 * 2 * T
        ysel = carve(TILES * 2 * D).rearrange("p (c w d) -> p c w d", c=TILES, w=2)
        diag = carve(TILES * 2 * P).rearrange("p (c w t) -> p c w t", c=TILES, w=2)
        hrows = mix[:].rearrange("p k t -> p (k t)").rearrange("p (c n) -> p c n", c=TILES)
        yacc = mix[:].rearrange("p k t -> p (k t)").rearrange("p (c d) -> p c d", c=TILES)

        used[0] = 0
        tail = carve(TILES * TAIL).rearrange("p (c n) -> p c n", c=TILES)
        w_ukv = carve(2 * 1024).rearrange("p (k n) -> p k n", k=2)
        w_uq = carve(3 * 768).rearrange("p (k n) -> p k n", k=3)
        kpin = carve(QK_DIM)
        kvpast = carve(KV_RANK)
        base = used[0]
        x_rows = arena[:, base:base + TILES * D].rearrange("p (c d) -> p c d", c=TILES)
        qT = carve(4 * T).rearrange("p (h t) -> p h t", h=4)
        kT = carve(4 * T).rearrange("p (h t) -> p h t", h=4)
        kN = carve(TILES * 512).rearrange("p (c n) -> p c n", c=TILES)
        vN = carve(TILES * 512).rearrange("p (c n) -> p c n", c=TILES)
        oS = carve(TILES * 512).rearrange("p (c n) -> p c n", c=TILES)
        hsum = carve(TILES * 512).rearrange("p (c n) -> p c n", c=TILES)
        mlC = carve(4 * 512).rearrange("p (s d n) -> p s d n", s=2, d=2)
        mln = carve(16).rearrange("p (s d n) -> p s d n", s=2, d=2)
        spare = hT[:].rearrange("p k t -> p (k t)")
        Rm, mrt, ET, ST, num, kw = ([carve(512), spare[:, 512 * n:512 * n + 512]] for n in range(6))
        carried = [carve(512) for _ in range(2)]
        used[0] = base
        cqT = carve(3 * T).rearrange("p (k t) -> p k t", k=3)
        kvT = carve(2 * KEYS).rearrange("p (k t) -> p k t", k=2)
        kpe = carve(KEYS)
        used[0] = base + 8 * T
        qfT = carve(MLA_H * T).rearrange("p (h t) -> p h t", h=MLA_H)
        kfT = carve(MLA_H * KEYS).rearrange("p (h t) -> p h t", h=MLA_H)
        vv = carve(4 * 512).rearrange("p (k n) -> p k n", k=4)
        rtmp = carve(512)
        pr = carve(2 * T).rearrange("p (b t) -> p b t", b=2)
        prT = carve(2 * T).rearrange("p (b t) -> p b t", b=2)
        flat = mix[:].rearrange("p k t -> p (k t)")
        cqn = flat[:, 0:TILES * Q_RANK].rearrange("p (c n) -> p c n", c=TILES)
        ckn = flat[:, TILES * Q_RANK:TILES * (Q_RANK + KV_RANK)].rearrange("p (c n) -> p c n", c=TILES)
        squares = flat[:, TILES * (Q_RANK + KV_RANK):TILES * (Q_RANK + KV_RANK) + 512]

        used[0] = 0
        conv = carve(CONV_TILES * COUT).rearrange("p (i t) -> p i t", i=CONV_TILES)
        zs = carve(TILES * 512).rearrange("p (c n) -> p c n", c=TILES)
        zg = carve(TILES * 512).rearrange("p (c n) -> p c n", c=TILES)
        dg = carve(TILES * 32).rearrange("p (c n) -> p c n", c=TILES)
        spin, sp, lg, cb, tot, ecb, etot, edif, ncb = (
            carve(72).rearrange("p (d c h) -> p d c h", d=2, c=TILES) for _ in range(9))
        beta, edb = (carve(24).rearrange("p (d c h) -> p d c h", d=2, c=TILES) for _ in range(2))
        wA = carve(24)
        base = used[0]
        cin = carve(CONV_TILES * CIN).rearrange("p (i t) -> p i t", i=CONV_TILES)
        l2 = mix
        l2_segs = ((0, PROMPT, 0), (PROMPT, T, 2 * PAD))
        used[0] = base
        xN = carve(TILES * 512).rearrange("p (c n) -> p c n", c=TILES)
        BN = carve(TILES * 256).rearrange("p (c n) -> p c n", c=TILES)
        hsT = carve(4 * 512).rearrange("p (s d n) -> p s d n", s=2, d=2)
        hsO = carve(2 * 512).rearrange("p (d n) -> p d n", d=2)
        Sg = carve(4 * 512).rearrange("p (s d n) -> p s d n", s=2, d=2)
        parts = (carve(4096), ring[:, 0, :], ring[:, 1, :], ring[:, 2, :])
        G = [parts[2 * w][:, 0:1024] for w in range(2)]
        E1, xdt, xw, y2, EB, PT = ([parts[2 * w][:, 512 * n:512 * n + 512] for w in range(2)] for n in range(2, 8))
        AT, XT, X, LT, TT, Rg, U, Uw = ([parts[2 * w + 1][:, 512 * n:512 * n + 512] for w in range(2)] for n in range(8))
        h0 = flat[:, TILES * 512:TILES * 512 + 1024].rearrange("p (d i n) -> p d i n", d=2, i=4)
        hflat = hT[:].rearrange("p k t -> p (k t)")
        gk = hflat[:, 0:1536].rearrange("p (c n) -> p c n", c=TILES)
        gv = hflat[:, 1536:3072].rearrange("p (c n) -> p c n", c=TILES)
        skip = flat[:, 0:TILES * 512].rearrange("p (c n) -> p c n", c=TILES)
        ysum = conv[:, 0:4, :].rearrange("p i t -> p (i t)")[:, 0:1536].rearrange("p (c n) -> p c n", c=TILES)
        ogsum = conv[:, 16:20, :].rearrange("p i t -> p (i t)")[:, 0:1536].rearrange("p (c n) -> p c n", c=TILES)

        def sm(at, n):
            return small[:, at:at + n]

        li = sm(0, 24).rearrange("p (d c h) -> p d c h", d=2, c=TILES)
        lf = sm(24, 24).rearrange("p (d c h) -> p d c h", d=2, c=TILES)
        tf = sm(48, 24).rearrange("p (d c h) -> p d c h", d=2, c=TILES)
        bcum = sm(72, 24).rearrange("p (d c h) -> p d c h", d=2, c=TILES)
        btot = sm(96, 24).rearrange("p (d c h) -> p d c h", d=2, c=TILES)
        rr = sm(120, 24).rearrange("p (d c h) -> p d c h", d=2, c=TILES)
        mst = sm(144, 16).rearrange("p (s d h) -> p s d h", s=2, d=2)
        mx, mxa, nmr, emq, dec, wk, den, den2, aexp = (
            sm(at_, 8).rearrange("p (d h) -> p d h", d=2) for at_ in range(232, 304, 8))
        ms12 = sm(200, 12)
        ms3 = sm(212, 3)
        ms6 = sm(216, 3)
        nb = sm(220, 2)
        rs = sm(222, 2)
        rsi = sm(224, 2)
        nbm = sm(226, 2)

        parts_at = mods_beside()

        block = es.enter_context(nc.Block())

        def every(eng):
            count = {}

            def done(ins, name):
                count[name] = count.get(name, 0) + 1
                ins.then_inc(S(name), 1)
                eng.wait_ge(S(name), count[name])

            def take(ins, *job):
                sem, n = taken(*job)
                ins.then_inc(sem, 1)
                eng.wait_ge(sem, n)

            return done, take

        def overflow(eng, l):
            eng.wait_ge(S("flag"), l + 1)
            return eng.If(eng.value_load(flag[0:1, l:l + 1], min_val=0, max_val=1))

        @block.sync
        def _(sp):
            sp.dma_start(cst[:], a["consts"]).then_inc(S("x_in"), 16)
            for c in range(TILES):
                src = a["x_prompt"][0] if c == 0 else a["x_sample"][0, (c - 1) * P:c * P, :]
                sp.dma_start(x_rows[:, c, :], src).then_inc(S("x_in"), 16)
            with nc.allow_non_contiguous_dma(reason="small vectors"):
                sp.dma_start(cc[:, 0, :], a["c_ctx"].rearrange("(p k) -> p k", k=KD)).then_inc(S("cond_in"), 16)
                sp.dma_start(cc[:, 1, :], a["c"][0].rearrange("(p k) -> p k", k=KD)).then_inc(S("cond_in"), 16)
            ring_full = [S(f"ring{n}_full") for n in range(RING)]

            def load(n):
                kind, what, _ = weights[n]
                slot = ring[:, n % RING, :]
                if (kind, what) == ("out", (1, 0)):
                    sp.wait_ge(S("odd_sums"), 1)
                if n >= RING:
                    sp.wait_ge(*computed(*weights[n - RING][2]))
                if kind == "ada":
                    l, i, half = what
                    src = a["ada_w"][l].rearrange("(p k) n -> p k n", k=KD)[:, 4 * half:4 * half + 4, i * D:(i + 1) * D]
                    dst = slot.rearrange("p (k n) -> p k n", k=4)
                elif kind == "out":
                    l, half = what
                    w = a["w_out_even" if l == 0 else "w_out_odd"][0]
                    src = w.rearrange("(k p) n -> p k n", p=P)[:, 4 * half:4 * half + 4, :]
                    dst = slot.rearrange("p (k n) -> p k n", k=4)
                elif kind == "even":
                    w = a["w_in_even"][0].rearrange("(p k) n -> p k n", k=KD)
                    n0, n1 = what * 512, min(what * 512 + 512, IN_EVEN)
                    src = w[:, :, n0:n1]
                    dst = slot.rearrange("p (k n) -> p k n", k=KD)[:, :, 0:n1 - n0]
                else:
                    w = a["w_in_odd"][0].rearrange("(p k) n -> p k n", k=KD)
                    dst = slot.rearrange("p (k n) -> p k n", k=KD)
                    if what < 7:
                        n0, width = ODD_COLS[what]
                        src = w[:, :, n0:n0 + width]
                    else:
                        sp.dma_start(dst[:, :, 0:16], w[:, :, DT:DT + 16]).then_inc(ring_full[n % RING], 16)
                        src, dst = w[:, :, GA:GA + 16], dst[:, :, 16:32]
                sp.dma_start(dst, src).then_inc(ring_full[n % RING], 16)

            def h_rows_out(l):
                for c in range(TILES):
                    for half in range(2):
                        sp.wait_ge(*taken("hr", l, c, half))
                    sp.dma_start(h_dram[c * P:(c + 1) * P, :], hrows[:, c, :]).then_inc(S("h_rows_out"), 16)

            def experts(l, dense):
                wg, wu, wd = (a[n][l] for n in ("moe_w_gate", "moe_w_up", "moe_w_down"))
                kind = f"{'dense' if dense else 'gathered'}{l}_"
                per_gu, per_y = (2, 6) if dense else (2, 2)

                def load_expert(e, u):
                    for w, m in ((0, wg), (1, wu)):
                        sp.dma_start(gu[u][:, w], m[bass.ds(e, 1)].rearrange("e (p k) f -> p (e k) f", k=KD))\
                          .then_inc(S(f"{kind}gu{u}_in"), 16)
                    return lambda: sp.dma_start(dn[u], wd[bass.ds(e, 1)].rearrange("e (p j) d -> p (e j) d", j=2))\
                        .then_inc(S(f"{kind}dn{u}_in"), 16)

                for u in range(2):
                    load_expert(u, u)()
                if not dense:
                    h_rows_out(l)
                with sp.Fori(1, EXPERTS // 2) as i:
                    for u in range(2):
                        e = i * 2 + u
                        sp.wait_ge(S(f"{kind}gu_computed"), e * per_gu - per_gu)
                        down = load_expert(e, u)
                        sp.wait_ge(S(f"{kind}y_computed"), e * per_y - per_y)
                        down()

            def moe(l):
                sp.wait_ge(*x_ready(2 * l + 1))
                if l == 0:
                    sp.wait_ge(S("even_out"), 32)
                else:
                    sp.wait_ge(S("odd_out"), 64)
                experts(l, dense=False)
                with overflow(sp, l):
                    sp.wait_ge(S(f"gathered{l}_gu_computed"), 2 * EXPERTS)
                    sp.wait_ge(S(f"gathered{l}_y_computed"), 2 * EXPERTS)
                    experts(l, dense=True)

            n_even = weight_at[("odd", 3)]
            for n in range(n_even):
                load(n)
            moe(0)
            sp.wait_ge(S(f"chosen{TILES - 1}_in"), 16)
            for n in range(n_even, len(weights)):
                load(n)
            moe(1)

        @block.gpsimd
        def _(pool):
            count = [0]

            def small_load(dst, src):
                pool.dma_start(dst, src).then_inc(S("small_in"), 16)
                count[0] += 1

            def along(v):
                return v.partition_broadcast(P)

            with nc.allow_non_contiguous_dma(reason="small vectors"):
                for l in range(2):
                    pool.dma_start(adab[:, l], a["ada_b"][l].rearrange("(i p k) -> p i k", i=6, k=KD)).then_inc(S("bias_in"), 16)
                for n, v in enumerate((a["norm_mix"][0], a["norm_mix"][1], a["norm_ffn"][0], a["norm_ffn"][1], a["norm_final"])):
                    pool.dma_start(gains[:, n, :], v.rearrange("(p k) -> p k", k=KD)).then_inc(S("gains_in"), 16)
                small_load(row_ids[:], a["row_ids"])
                for l in range(2):
                    small_load(wr[:, l, :, 0:GROUPS], a["moe_w_group"][l].rearrange("(p k) n -> p k n", k=KD))
                    small_load(wr[:, l, :, GROUPS:ROUTES], a["moe_w_expert"][l].rearrange("(p k) n -> p k n", k=KD))
                    small_load(br[:, l, 0:GROUPS], along(a["moe_b_group"][l]))
                    small_load(br[:, l, GROUPS:ROUTES], along(a["moe_b_expert"][l]))
                small_load(rows[0:40, :], a["ssd_conv_w"][0].rearrange("w (i p) -> (w i) p", p=P))
                small_load(rows[40:100, :], a["gdn_conv_w"][0].rearrange("w (i p) -> (w i) p", p=P))
                small_load(rows[100:108, :], a["ssd_conv_b"][0].rearrange("(i p) -> i p", p=P))
                small_load(rows[108:120, :], a["gdn_conv_b"][0].rearrange("(i p) -> i p", p=P))
                small_load(rows[120:128, :], a["state_mlstm_n"][0, 0].rearrange("d h k -> (d h) k"))
                small_load(bias_e[:, 0:8], along(a["ml_i_bias"][0].rearrange("d h -> (d h)")))
                small_load(bias_e[:, 8:16], along(a["ml_f_bias"][0].rearrange("d h -> (d h)")))
                for d in range(2):
                    small_load(bias_o[:, d, 0:8], along(a["ssd_dt_bias"][0, d]))
                    small_load(bias_o[:, d, 8:12], along(a["gdn_dt_bias"][0, d]))
                    small_load(alog[:, d, 0:8], along(a["ssd_A_log"][0, d]))
                    small_load(alog[:, d, 8:12], along(a["gdn_A_log"][0, d]))
                small_load(dskip[:], along(a["ssd_D"][0]))
                small_load(mprev0[:], along(a["state_mlstm_m"][0, 0].rearrange("d h -> (d h)")))
                small_load(gml, along(a["ml_norm"][0].rearrange("h v -> (h v)")))
                small_load(gq, along(a["mla_q_norm"][0]))
                small_load(gkv, along(a["mla_kv_norm"][0]))
                small_load(w_uq, a["mla_w_uq"][0].rearrange("(k p) n -> p k n", p=P))
                small_load(w_ukv, a["mla_w_ukv"][0].rearrange("(k p) n -> p k n", p=P))
                small_load(kvpast, a["cache_mla_kv"][0, 0])
                pool.dma_start(kpin[:, NOPE:QK_DIM], a["cache_mla_krope"][0, 0]).then_inc(S("small_in"), 16)
                count[0] += 1
                for d in range(2):
                    small_load(mlC[:, 1, d, :].rearrange("p (h v) -> p h v", h=4),
                               a["state_mlstm_C"][0, 0, d].rearrange("h k v -> k h v"))
                build.n_small = count[0]
                zero_row = route[:].rearrange("p a c n -> p (a c n)")[:, 0:D]
                last_slot, last_token, last_choice = (pool.to_reg(n - 1) for n in (EXPERTS * CAP, T, 2 * T))
                pool.wait_ge(S("zeroed"), 1)
                for l in range(2):
                    pool.dma_start(tab_dram[l].rearrange("(p n) w -> p (n w)", p=P), unused[:]).then_inc(S("tables_empty"), 16)
                pool.dma_start(y_dram.rearrange("(p n) d -> p n d", p=P), bc(zero_row, 1, [P, 2 * T // P, D]))\
                    .then_inc(S("rows_zero"), 16)

                def gathered(l):
                    def carry(e, n, *waits):
                        for sem, value in waits:
                            pool.wait_ge(sem, value)
                        nc.gpsimd.tensor_copy(carrier[:, l, n, bass.ds(e, 1)], row_ids[0:1, 0, 0, 0:1])

                    pool.wait_ge(S("tables_empty"), 32)
                    pool.wait_ge(S("rows_zero"), 16)
                    pool.wait_ge(S("slots"), l + 1)
                    for w in range(2):
                        for c in range(TILES):
                            pool.indirect_dma_start(
                                out=tab_dram[l], out_offset=bass.IndirectOffsetOnAxis(ap=slots_i[:, w, c:c + 1].bitcast(U32), axis=0),
                                in_=row_ids[:, w, c, :], in_offset=None, bounds_check=last_slot,
                                oob_is_err=False).then_inc(S("table_set"), 16)
                    pool.wait_ge(S("table_set"), 16 * 2 * TILES * (l + 1))
                    pool.dma_start(table[0:CAP], tab_dram[l].rearrange("(e s) w -> s e w", s=CAP)).then_inc(S("table_in"), 16)
                    pool.wait_ge(S("table_in"), 16 * (l + 1))
                    pool.wait_ge(S("h_rows_out"), 16 * TILES * (l + 1))
                    pool.wait_ge(S("rows_clear"), l + 1)

                    def gather(e, u):
                        nc.gpsimd.tensor_copy(index[0:CAP, u, :], table[0:CAP, bass.ds(e, 1), :].rearrange("p e w -> p (e w)"))\
                            .then_inc(S(f"gathered{l}_index"), 1)
                        carry(e, 0, (S(f"gathered{l}_index"), e + 1))
                        pool.indirect_dma_start(
                            out=hrow[u][0:CAP, :], out_offset=None, in_=h_dram,
                            in_offset=bass.IndirectOffsetOnAxis(ap=index[0:CAP, u, 0:1].bitcast(U32), axis=0),
                            bounds_check=last_token, oob_is_err=False).then_inc(S(f"gathered{l}_hrow{u}_in"), 16)

                    def scatter(e, u):
                        carry(e, 1, (S(f"gathered{l}_sindex"), e + 1), (S(f"gathered{l}_ya"), e + 1),
                              (S(f"gathered{l}_yb"), e + 1))
                        pool.indirect_dma_start(
                            out=y_dram, out_offset=bass.IndirectOffsetOnAxis(ap=sindex[u][0:CAP, :].bitcast(U32), axis=0),
                            in_=yrow[u][0:CAP, :], in_offset=None, bounds_check=last_choice,
                            oob_is_err=False).then_inc(S(f"gathered{l}_yrow{u}_out"), 16)

                    def scatter_index(e, u):
                        nc.gpsimd.tensor_copy(sindex[u][0:CAP, :], table[0:CAP, bass.ds(e, 1), 1:2].rearrange("p e w -> p (e w)"))\
                            .then_inc(S(f"gathered{l}_sindex"), 1)

                    for u in range(2):
                        gather(u, u)
                    for u in range(2):
                        pool.wait_ge(S(f"gathered{l}_turned"), u + 1)
                        gather(u + 2, u)
                        scatter_index(u, u)
                        scatter(u, u)
                    with pool.Fori(1, EXPERTS // 2 - 1) as i:
                        for u in range(2):
                            e = i * 2 + u
                            pool.wait_ge(S(f"gathered{l}_turned"), e + 1)
                            gather(e + 2, u)
                            pool.wait_ge(S(f"gathered{l}_yrow{u}_out"), i * 16)
                            scatter_index(e, u)
                            scatter(e, u)
                    for u in range(2):
                        e = EXPERTS - 2 + u
                        pool.wait_ge(S(f"gathered{l}_yrow{u}_out"), 16 * (EXPERTS // 2 - 1))
                        scatter_index(e, u)
                        scatter(e, u)
                    for u in range(2):
                        pool.wait_ge(S(f"gathered{l}_yrow{u}_out"), 16 * EXPERTS // 2)
                    for c in range(TILES):
                        pool.dma_start(ysel[:, c], y_dram.rearrange("(c p w) d -> c p w d", c=TILES, w=2)[c])\
                            .then_inc(S(f"chosen{c}_in"), 16)

                pool.wait_ge(*taken("tb", 0))
                pool.dma_start(o["krope"][0, 0], tail[:, 0, KPE0:KPE0 + ROPE]).then_inc(S("even_out"), 16)
                for u in range(2):
                    pool.wait_ge(*taken("NU", u))
                for d in range(2):
                    pool.dma_start(o["C"][0, 0, d].rearrange("h k v -> k h v"),
                                   mlC[:, 0, d, :].rearrange("p (h v) -> p h v", h=4)).then_inc(S("ml_out"), 16)
                    pool.dma_start(o["n"][0, 0, d].rearrange("h k -> k h"), mln[:, 0, d, :]).then_inc(S("ml_out"), 16)
                pool.dma_start(o["m"][0, 0].rearrange("d h -> (d h)").unsqueeze(0),
                               mst[0:1, 0, :, :].rearrange("p d h -> p (d h)")).then_inc(S("ml_out"), 16)

                pool.wait_ge(S("kv_norm"), 1)
                pool.dma_start(o["kv"][0, 0], ckn[:, 0, :]).then_inc(S("even_out"), 16)

                gathered(0)

                pool.wait_ge(*x_ready(2))
                pool.dma_start(gssd, along(a["ssd_norm"][0])).then_inc(S("odd_in"), 16)
                pool.dma_start(ggdn, along(a["gdn_norm"][0])).then_inc(S("odd_in"), 16)
                pool.wait_ge(S("l2_done"), 1)
                for d in range(2):
                    pool.dma_start(h0[:, d], a["state_ssd"][0, 0, d].rearrange("(i g) q n -> (g q) i n", g=2))\
                        .then_inc(S("odd_in"), 16)
                pool.wait_ge(S("conv_tile"), CONV_TILES)
                for d in range(2):
                    pool.dma_start(Sg[:, 1, d, :].rearrange("p (h v) -> p h v", h=4),
                                   a["state_gdn"][0, 0, d].rearrange("h k v -> k h v")).then_inc(S("gdn_in"), 16)
                pool.wait_ge(*taken("tx", TILES - 1))
                for c in range(TILES):
                    ins = nc.gpsimd.tensor_tensor(heads(skip[:, c, :], 8), heads(xN[:, c, :], 8),
                                                  bc(dskip[:], 2, [P, 8, SSD_P]), ALU.mult)
                ins.then_inc(S("skip"), 1)
                pool.wait_ge(S("odd_in"), 64)
                pool.wait_ge(*taken("zg", TILES - 1))
                gate = zg.rearrange("p c (h n) -> p (c h) n", h=4)
                nc.gpsimd.tensor_tensor(gate, gate, bc(ggdn, 1, [P, 12, P]), ALU.mult).then_inc(S("gate_gain"), 1)
                for d in range(2):
                    pool.wait_ge(*taken("SU", d))
                    pool.dma_start(o["gdn"][0, 0, d].rearrange("h k v -> k h v"),
                                   Sg[:, 0, d, :].rearrange("p (h v) -> p h v", h=4)).then_inc(S("odd_out"), 16)
                    pool.wait_ge(*taken("hT", d))
                    pool.dma_start(o["ssd"][0, 0, d].rearrange("(i g) q n -> (g q) i n", g=2),
                                   hsO[:, d, :].rearrange("p (i n) -> p i n", i=4)).then_inc(S("odd_out"), 16)
                gathered(1)
                for c in range(TILES):
                    pool.wait_ge(S("y_rows"), 2 * (c + 1))
                    dst = o["yp"][0] if c == 0 else o["ys"][0, (c - 1) * P:c * P, :]
                    pool.dma_start(dst, mix[:].rearrange("p k t -> p (k t)")[:, c * D:(c + 1) * D]).then_inc(S("out"), 16)
                pool.wait_ge(S("odd_out"), 64)
                pool.wait_ge(S("out"), 16 * TILES)
                pool.wait_ge(S("even_out"), 32)
                pool.wait_ge(S("ml_out"), 80)

        SMALL = 16 * build.n_small

        @block.tensor
        def _(pe):
            at = [0]
            mm = nc.tensor.matmul

            def issue(*job):
                assert jobs[at[0]] == job, (jobs[at[0]], job)
                n = at[0]
                at[0] += 1
                if n >= BANKS:
                    pe.wait_ge(free[n % BANKS], n // BANKS)
                return psum[:, n % BANKS, :]

            def ready(ins, *job):
                n = job_at[job] if job else at[0] - 1
                ins.then_inc(full[n % BANKS], 1)

            ring_count = [0] * RING
            ring_at = [0]

            def weight(kind, what):
                n = ring_at[0]
                assert weights[n][0:2] == (kind, what), (weights[n], kind, what)
                ring_at[0] += 1
                ring_count[n % RING] += 32 if (kind, what) == ("odd", 7) else 16
                pe.wait_ge(S(f"ring{n % RING}_full"), ring_count[n % RING])
                return ring[:, n % RING, :]

            def wview(slot):
                return slot.rearrange("p (k n) -> p k n", k=KD)

            def contract(out, lhs, rhs, n, first_of=None):
                for k in range(n):
                    if first_of is not None:
                        pe.wait_ge(S("h"), KD * first_of + k + 1)
                    ins = mm(out, lhs(k), rhs(k), start=(k == 0), stop=(k == n - 1))
                return ins

            def tok(c):
                return slice(c * P, (c + 1) * P)

            pe.wait_ge(S("x_in"), 16 * (TILES + 1))
            for k in range(KD):
                b = issue("xt", k)
                for c in range(TILES):
                    ins = nc.tensor.transpose(b[:, tok(c)], x_rows[:, c, k::KD], ident)
                ready(ins)

            def modulate(name, l, i):
                if name == "mod_rows":
                    w = [weight("ada", (l, i, half)).rearrange("p (k n) -> p k n", k=4) for half in range(2)]
                    b = issue(name, l, i)
                    for k in range(4):
                        for parity in range(2):
                            for half in range(2):
                                at_ = 32 * (2 * parity + half)
                                ins = mm(b[at_:at_ + 32, :], sil[:, 4 * half + k, :], w[half][:, k, parity::2],
                                         start=(k == 0), stop=(k == 3), tile_position=(0, at_))
                    ready(ins)
                else:
                    b = issue(name, l, i)
                    pe.wait_ge(*taken("mod_rows", l, i))
                    for m in range(4):
                        ins = mm(b[:, 4 * m:4 * m + 4], mod_rows[:, m::4], pick, start=True, stop=True)
                    ready(ins)

            def beside(*job):
                for one in parts_at.get(job, []):
                    modulate(*one)

            pe.wait_ge(S("silu_c"), 1)
            for l, i in MOD_PARTS[:MODS_FIRST]:
                modulate("mod_rows", l, i)
                modulate("mod", l, i)

            def norm(n):
                b = issue("ss", n)
                for k in range(KD):
                    pe.wait_ge(S("squares"), KD * n + k + 1)
                    ins = mm(b[:, 0:T], ones, hT[:, k, :], start=(k == 0), stop=(k == KD - 1))
                ready(ins)

            norm(0)
            for n, name in ((0, "qT"), (1, "kT")):
                w = wview(weight("even", n))
                for h in range(4):
                    b = issue(name, h)
                    ready(contract(b[:, 0:T], lambda k: w[:, k, h * P:(h + 1) * P], lambda k: hT[:, k, :], KD,
                                   first_of=0 if (n, h) == (0, 0) else None))
            for n, name in ((1, "kN"), (2, "vN"), (3, "oN"), (4, "ta"), (5, "tb")):
                if n > 1:
                    w = wview(weight("even", n))
                width = 512 if n < 5 else IN_EVEN - 5 * 512
                for c in range(TILES):
                    b = issue(name, c)
                    ready(contract(b[:, 0:width], lambda k: hT[:, k, tok(c)], lambda k: w[:, k, 0:width], KD))

            def cumulate(n, lf_, tri, width):
                pe.wait_ge(S("log_decay"), n + 1)
                b = issue("cum", n)
                for d in range(2):
                    mm(b[:, d * width:(d + 1) * width], tri[d], lf_[:, d].rearrange("p c h -> p (c h)"),
                       start=True, stop=True)
                ready(mm(b[:, 2 * width:4 * width], ones, lf_.rearrange("p d c h -> p (d c h)"), start=True, stop=True))

            pe.wait_ge(S("small_in"), SMALL)
            b = issue("cols")
            ready(nc.tensor.transpose(b[:, 0:P], rows[:], ident))
            cumulate(0, lf, cum01, 12)

            def spread(b, col):
                for h in range(4):
                    ins = mm(b[:, tok(h)], col(h).to_broadcast([P, P]), ident, start=True, stop=True)
                ready(ins)

            def four(b, lhs, rhs, width=P):
                for h in range(4):
                    ins = mm(b[:, h * width:(h + 1) * width], lhs(h), rhs(h), start=True, stop=True)
                ready(ins)

            pe.wait_ge(S("r"), 1)
            for pair in range(3):
                two = [(u, *units[u]) for u in (2 * pair, 2 * pair + 1)]
                sequence, moves_on = pair > 0, pair < 2
                for u, d, c in two:
                    spread(issue("R", u), lambda h: rr[:, d, c, h:h + 1])
                beside("MR", 2 * pair)
                pe.wait_ge(S("neg_m"), pair + 1)
                for u, d, c in two:
                    spread(issue("MR", u), lambda h: nmr[:, d, h:h + 1])
                pe.wait_ge(*taken("kT", 3))
                for u, d, c in two:
                    four(issue("SK", u), lambda h: kT[:, h, tok(c)], lambda h: qT[:, h, tok(c)])
                pe.wait_ge(*taken("vN", 2))
                for u, d, c in two:
                    b = issue("N1", u)
                    pe.wait_ge(*taken("SK", u))
                    four(b, lambda h: ST[d][:, tok(h)], lambda h: vN[:, c, tok(h)])
                for u, d, c in two:
                    b = issue("DN", u)
                    for h in range(4):
                        ins = mm(b[:, h:h + 1], ST[d][:, tok(h)], ones[:, 0:1], start=True, stop=True)
                    if sequence:
                        if pair == 1:
                            pe.wait_ge(S("n_start"), 1)
                        else:
                            pe.wait_ge(*taken("NU", u - 2))
                        for h in range(4):
                            ins = mm(b[:, 4 + h:5 + h], qT[:, h, tok(c)], mln[:, 1, d, h:h + 1], start=True, stop=True)
                    ready(ins)
                if sequence:
                    for u, d, c in two:
                        four(issue("N2", u), lambda h: qT[:, h, tok(c)], lambda h: mlC[:, 1, d, tok(h)])
                if moves_on:
                    pe.wait_ge(S("kw"), 2 * pair + 2)
                    for u, d, c in two:
                        four(issue("CU", u), lambda h: kw[d][:, tok(h)], lambda h: vN[:, c, tok(h)])
                    for u, d, c in two:
                        four(issue("NU", u), lambda h: kw[d][:, tok(h)], lambda h: ones[:, 0:1], width=1)

            beside("cqT", 0)
            pe.wait_ge(S("mla_norm"), 1)
            for k in range(3):
                b = issue("cqT", k)
                for c in range(TILES):
                    ins = nc.tensor.transpose(b[:, tok(c)], cqn[:, c, tok(k)], ident)
                ready(ins)
            for k in range(2):
                b = issue("kvT", k)
                for n, src in enumerate((ckn[:, 0], kvpast, ckn[:, 1], ckn[:, 2])):
                    ins = nc.tensor.transpose(b[:, tok(n)], src[:, tok(k)], ident)
                ready(ins)
            b = issue("kpT")
            for n, src in enumerate((tail[:, 0], None, tail[:, 1], tail[:, 2])):
                src = kpin[:, 0:QK_DIM] if src is None else src[:, KPE0 - NOPE:KPE0 + ROPE]
                ins = nc.tensor.transpose(b[0:QK_DIM, tok(n)], src, ident)
            ready(ins)
            b = issue("kpR")
            pe.wait_ge(*taken("kpT"))
            ready(mm(b[NOPE:QK_DIM, 0:SAMPLE], rot[NOPE:QK_DIM, :], kpe[NOPE:QK_DIM, 2 * P:4 * P], start=True, stop=True))
            beside("hmT", 0)
            pe.wait_ge(S("hm"), 1)
            for h in range(4):
                b = issue("hmT", h)
                for c in range(TILES):
                    ins = nc.tensor.transpose(b[:, tok(c)], hsum[:, c, tok(h)], ident)
                ready(ins)

            for h in range(MLA_H):
                b = issue("qf", h)
                pe.wait_ge(*taken("cqT", 2))
                ready(contract(b[0:QK_DIM, 0:T], lambda k: w_uq[:, k, h * QK_DIM:(h + 1) * QK_DIM],
                               lambda k: cqT[:, k, :], 3))
            for i in range(4):
                b = issue("qR", i)
                pe.wait_ge(*taken("qf", 2 * i + 1))
                ready(mm(b[NOPE:QK_DIM, :].rearrange("p (h t) -> p h t", h=2), rot[NOPE:QK_DIM, :],
                         qfT[NOPE:QK_DIM, 2 * i:2 * i + 2, PROMPT:T], start=True, stop=True))
            for h in range(MLA_H):
                b = issue("kn", h)
                pe.wait_ge(*taken("kvT", 1))
                ready(contract(b[0:NOPE, :], lambda k: w_ukv[:, k, h * P:h * P + NOPE], lambda k: kvT[:, k, :], 2))
            for n in range(4):
                b = issue("vv", n)
                ready(contract(b[:, :].rearrange("p (h v) -> p h v", h=MLA_H), lambda k: kvT[:, k, tok(n)],
                               lambda k: w_ukv[:, k, :].rearrange("p (h v) -> p h v", h=MLA_H)[:, :, NOPE:P], 2))
            pe.wait_ge(*taken("vv", 3))
            pe.wait_ge(*taken("kn", 7))
            pe.wait_ge(S("keys"), 1)
            pe.wait_ge(S("q_rot"), 4)
            for c in range(TILES):
                tiles = [0] if c == 0 else [1, 2, 3]
                nk = len(tiles) * P

                def scores(h):
                    b = issue("sc", c, h)
                    ready(mm(b[:, 0:nk], qfT[0:QK_DIM, h, tok(c)], kfT[0:QK_DIM, h, tiles[0] * P:tiles[0] * P + nk],
                             start=True, stop=True))

                scores(0)
                for h in range(MLA_H):
                    n = c * MLA_H + h
                    if h + 1 < MLA_H:
                        scores(h + 1)
                    beside("pT", c, h)
                    b = issue("pT", c, h)
                    pe.wait_ge(S("probs"), n + 1)
                    for t in range(len(tiles)):
                        ins = nc.tensor.transpose(b[:, tok(t)], pr[:, n % 2, tok(t)], ident)
                    ready(ins)
                    if h % 2:
                        b = issue("pv", c, h // 2)
                        for g in range(2):
                            hh = h - 1 + g
                            pe.wait_ge(*taken("pT", c, hh))
                            for t, kt in enumerate(tiles):
                                ins = mm(b[64 * g:64 * g + 64, 0:P], vv[:, kt, hh * 64:hh * 64 + 64],
                                         prT[:, (n - 1 + g) % 2, tok(t)], start=(t == 0), stop=(t == len(tiles) - 1))
                        ready(ins)

            def project_out(l):
                w = [weight("out", (l, half)).rearrange("p (k n) -> p k n", k=4) for half in range(2)]
                for m in range(KD):
                    b = issue("o", l, m)
                    ready(contract(b[:, 0:T], lambda k: w[k // 4][:, k % 4, m::KD], lambda k: mix[:, k, :], KD))

            def router(l):
                b = issue("rt", l)
                for c in range(TILES):
                    ins = contract(b[:, c * ROUTES:(c + 1) * ROUTES], lambda k: hT[:, k, tok(c)],
                                   lambda k: wr[:, l, k, :], KD, first_of=2 * l + 1 if c == 0 else None)
                ready(ins)

            def ranks(l):
                b = issue("rk", l)
                pe.wait_ge(S("chosen"), l + 1)
                for c in range(TILES):
                    for k in range(c + 1):
                        ins = mm(b[:, c * EXPERTS:(c + 1) * EXPERTS], cum01[0] if k == c else ones, comb[:, k, :],
                                 start=(k == 0), stop=(k == c))
                for k in range(TILES):
                    ins = mm(b[:, TILES * EXPERTS:(TILES + 1) * EXPERTS], ones, comb[:, k, :], start=(k == 0), stop=(k == TILES - 1))
                ready(ins)

            def rows_out(l):
                for c in range(TILES):
                    for half in range(2):
                        b = issue("hr", l, c, half)
                        for k in range(4):
                            ins = nc.tensor.transpose(b[:, tok(k)], hT[:, 4 * half + k, tok(c)], ident)
                        ready(ins)

            def clear_banks():
                for n in range(at[0] - BANKS, at[0]):
                    pe.wait_ge(free[n % BANKS], n // BANKS + 1)

            def gathered(l):
                clear_banks()
                kind = f"gathered{l}_"


                def turn(e, u, i):
                    pe.wait_ge(S(f"{kind}hrow{u}_in"), i * 16 + 16)
                    if not (isinstance(e, int) and e == 0):
                        pe.wait_ge(S(f"{kind}hg"), e)
                    for k in range(KD):
                        ins = nc.tensor.transpose(psum[:, k // 4, k % 4 * CAP:(k % 4 + 1) * CAP],
                                                  hrow[u][0:CAP, k * P:(k + 1) * P], ident[0:CAP, 0:CAP])
                    ins.then_inc(S(f"{kind}turned"), 1)

                def expert(e, u, i, more):
                    pe.wait_ge(S(f"{kind}hg"), e + 1)
                    pe.wait_ge(S(f"{kind}gu{u}_in"), i * 32 + 32)
                    for j in range(2):
                        for w in range(2):
                            ins = contract(psum[:, 2 + j, w * CAP:(w + 1) * CAP], lambda k: gu[u][:, w, k, j::2],
                                           lambda k: hg[u][:, k, :], KD)
                        ins.then_inc(S(f"{kind}gu_computed"), 1)
                    if more:
                        turn(e + 1, 1 - u, i + u)
                    pe.wait_ge(S(f"{kind}act"), e * 2 + 2)
                    pe.wait_ge(S(f"{kind}dn{u}_in"), i * 16 + 16)
                    for half in range(2):
                        ins = contract(psum[0:CAP, 4 + 2 * u + half, :], lambda j: act_s[u][:, j, :],
                                       lambda j: dn[u][:, j, half * 512:half * 512 + 512], 2)
                        ins.then_inc(S(f"{kind}y_computed"), 1)

                turn(0, 0, 0)
                with pe.Fori(0, EXPERTS // 2 - 1) as i:
                    for u in range(2):
                        expert(i * 2 + u, u, i, True)
                for u in range(2):
                    expert(EXPERTS - 2 + u, u, EXPERTS // 2 - 1, u == 0)
                pe.wait_ge(S(f"{kind}ya"), EXPERTS)
                pe.wait_ge(S(f"{kind}yb"), EXPERTS)

            def dense(l):
                kind = f"dense{l}_"
                with pe.Fori(0, EXPERTS // 2) as i:
                    for u in range(2):
                        e = i * 2 + u
                        pe.wait_ge(S(f"{kind}gu{u}_in"), i * 32 + 32)
                        for j in range(2):
                            pe.wait_ge(S(f"{kind}act"), e * 2 + (j + 1))
                            for w in range(2):
                                ins = contract(psum[:, 2 * j + w, 0:T], lambda k: gu[u][:, w, k, j::2],
                                               lambda k: hT[:, k, :], KD)
                            ins.then_inc(S(f"{kind}gu_computed"), 1)
                        pe.wait_ge(S(f"{kind}dn{u}_in"), i * 16 + 16)
                        pe.wait_ge(S(f"{kind}act"), e * 2 + 4)
                        for q in range(6):
                            c, half = q // 2, q % 2
                            pe.wait_ge(S(f"{kind}y_taken"), e * 6 + (q + 1))
                            ins = contract(psum[:, 4 + (6 * u + q) % 4, :], lambda j: actT[u][:, j, tok(c)],
                                           lambda j: dn[u][:, j, half * 512:half * 512 + 512], 2)
                            ins.then_inc(S(f"{kind}y_computed"), 1)
                pe.wait_ge(S(f"{kind}y_taken"), 6 * EXPERTS + 4)

            def moe(l):
                router(l)
                rows_out(l)
                ranks(l)
                gathered(l)
                with overflow(pe, l):
                    dense(l)
                    pe.wait_ge(S(f"dense{l}_merged"), 2 * TILES + 1)
                pe.wait_ge(S("diag"), l + 1)
                banks = [issue("yt", l, m) for m in range(KD)]
                for c in range(TILES):
                    pe.wait_ge(S(f"chosen{c}_in"), 16 * (l + 1))
                    for m in range(KD):
                        for w in range(2):
                            ins = mm(banks[m][:, tok(c)], ysel[:, c, w, m::KD], diag[:, c, w, :], start=(w == 0), stop=(w == 1))
                        if c == TILES - 1:
                            ready(ins, "yt", l, m)

            for m in range(4):
                pe.wait_ge(*taken("hmT", m))
                pe.wait_ge(*taken("pv", 2, m))
            project_out(0)
            norm(1)
            moe(0)
            norm(2)

            for n, i in enumerate(CONV_ORDER):
                if n == 8:
                    w = wview(weight("odd", 7))
                    b = issue("dg")
                    for c in range(TILES):
                        ins = contract(b[:, c * 32:c * 32 + 32], lambda k: hT[:, k, tok(c)], lambda k: w[:, k, 0:32], KD)
                    ready(ins)
                if n == 12:
                    cumulate(1, lg, cum01, 36)
                    for head in range(8):
                        b = issue("l2", head)
                        pe.wait_ge(S("l2_squares"), 2)
                        ready(mm(b[:, 0:T], ones, l2[:, head, :], start=True, stop=True))
                if i % 4 == 0:
                    w = wview(weight("odd", 1 + i // 4))
                b = issue("xb", i)
                ready(contract(b[:, 0:T], lambda k: w[:, k, tok(i % 4)], lambda k: hT[:, k, :], KD,
                               first_of=2 if n == 0 else None))
            for name, n in (("zs", 0), ("zg", 6)):
                w = wview(weight("odd", n))
                for c in range(TILES):
                    b = issue(name, c)
                    ready(contract(b, lambda k: hT[:, k, tok(c)], lambda k: w[:, k, :], KD))

            pe.wait_ge(S("l2_done"), 1)
            pe.wait_ge(S("conv_act"), CONV_TILES)
            for c in range(TILES):
                for name, i0, n in (("tk", 12, 4), ("tv", 16, 4), ("tx", 0, 4), ("tB", 4, 2)):
                    b = issue(name, c)
                    for i in range(n):
                        ins = nc.tensor.transpose(b[:, tok(i)], conv[:, i0 + i, CO[c]:CO[c] + P], ident)
                    ready(ins)

            pe.wait_ge(S("odd_gates"), 1)
            pe.wait_ge(*taken("tv", 2))
            pe.wait_ge(*taken("tk", 2))
            for pair in range(3):
                two = [(u, *units[u]) for u in (2 * pair, 2 * pair + 1)]
                sequence, moves_on = pair > 0, pair < 2

                def cols(c):
                    return slice(CO[c], CO[c] + P)

                for u, d, c in two:
                    spread(issue("Eg", u), lambda h: cb[:, d, c, 8 + h:9 + h])
                    four(issue("KK", u), lambda h: conv[:, 12 + h, cols(c)], lambda h: conv[:, 12 + h, cols(c)])
                    four(issue("KQ", u), lambda h: conv[:, 12 + h, cols(c)], lambda h: conv[:, 8 + h, cols(c)])
                for u, d, c in two:
                    b = issue("X0", u)
                    pe.wait_ge(S("xt_first"), u + 1)
                    for h in range(4):
                        ins = nc.tensor.transpose(b[:, tok(h)], XT[d][:, tok(h)], ident)
                    ready(ins)
                for n in range(1, 7):
                    for u, d, c in two:
                        b = issue("T1", u, n)
                        if n == 1:
                            pe.wait_ge(*taken("X0", u))
                        else:
                            pe.wait_ge(*taken("XX", u, n - 1))
                        pe.wait_ge(S("lt"), 12 * pair + 2 * (n - 1) + d + 1)
                        four(b, lambda h: LT[d][:, tok(h)], lambda h: X[d][:, tok(h)])
                    for u, d, c in two:
                        if n <= 2:
                            g = n - 1
                            spread(issue("Es", u, g), lambda h: cb[:, d, c, 4 * g + h:4 * g + h + 1])
                            ready(mm(issue("GB", u, g)[:, 0:P], conv[:, 4 + g, cols(c)], conv[:, 6 + g, cols(c)],
                                     start=True, stop=True))
                        elif n == 3:
                            b = issue("Y1", u)
                            pe.wait_ge(S("ssd_in"), u + 1)
                            for h in range(SSD_H):
                                ins = mm(b[:, h * SSD_P:(h + 1) * SSD_P], G[d][:, tok(h)],
                                         xdt[d][:, h * SSD_P:(h + 1) * SSD_P], start=True, stop=True)
                            ready(ins)
                        elif n == 4 and sequence:
                            b = issue("Y2", u)
                            if pair == 2:
                                pe.wait_ge(*taken("HU", u - 2))
                            for g in range(2):
                                ins = mm(b[:, g * 256:(g + 1) * 256], conv[:, 6 + g, cols(c)],
                                         hsT[:, 1, d, g * 256:(g + 1) * 256], start=True, stop=True)
                            ready(ins)
                        elif n == 5 and moves_on:
                            b = issue("HU", u)
                            for g in range(2):
                                ins = mm(b[:, g * 256:(g + 1) * 256], BN[:, c, tok(g)],
                                         xw[d][:, g * 256:(g + 1) * 256], start=True, stop=True)
                            ready(ins)
                        elif n == 6 and sequence:
                            b = issue("KS", u)
                            if pair == 2:
                                pe.wait_ge(*taken("SU", u - 2))
                            four(b, lambda h: conv[:, 12 + h, cols(c)], lambda h: Sg[:, 1, d, tok(h)])
                            four(issue("O2", u), lambda h: conv[:, 8 + h, cols(c)], lambda h: Sg[:, 1, d, tok(h)])
                    for u, d, c in two:
                        b = issue("XT", u, n)
                        pe.wait_ge(*taken("T1", u, n))
                        four(b, lambda h: TT[d][:, tok(h)], lambda h: XT[d][:, tok(h)])
                        if n < 6:
                            four(issue("XX", u, n), lambda h: XT[d][:, tok(h)], lambda h: TT[d][:, tok(h)])
                for u, d, c in two:
                    b = issue("U", u)
                    pe.wait_ge(*taken("XT", u, 6))
                    if sequence:
                        pe.wait_ge(S("rhs"), u - 1)
                        four(b, lambda h: XT[d][:, tok(h)], lambda h: Rg[d][:, tok(h)])
                    else:
                        four(b, lambda h: XT[d][:, tok(h)], lambda h: gv[:, c, tok(h)])
                for u, d, c in two:
                    b = issue("O1", u)
                    pe.wait_ge(*taken("U", u))
                    four(b, lambda h: PT[d][:, tok(h)], lambda h: U[d][:, tok(h)])
                if moves_on:
                    for u, d, c in two:
                        b = issue("SU", u)
                        pe.wait_ge(S("uw"), u + 1)
                        four(b, lambda h: gk[:, c, tok(h)], lambda h: Uw[d][:, tok(h)])
                if pair == 0:
                    for u, d, c in two:
                        b = issue("hT", d)
                        pe.wait_ge(*taken("HU", u))
                        for i in range(4):
                            ins = nc.tensor.transpose(b[:, tok(i)], hsT[:, 0, d, tok(i)], ident)
                        ready(ins)
                    pe.wait_ge(S("odd_in"), 64)
                    for d in range(2):
                        b = issue("h0T", d)
                        for i in range(4):
                            ins = nc.tensor.transpose(b[:, tok(i)], h0[:, d, i, :], ident)
                        ready(ins)
                    pe.wait_ge(S("gdn_in"), 32)

            for f in range(8):
                b = issue("mT", f)
                src = ysum if f < 4 else ogsum
                pe.wait_ge(S("odd_rows"), 1 if f < 4 else 2)
                for c in range(TILES):
                    ins = nc.tensor.transpose(b[:, tok(c)], src[:, c, tok(f % 4)], ident)
                ready(ins)
            for f in range(8):
                pe.wait_ge(*taken("mT", f))
            project_out(1)
            norm(3)
            moe(1)
            norm(4)
            pe.wait_ge(S("h_final"), KD)
            for c in range(TILES):
                for half in range(2):
                    b = issue("fin", c, half)
                    for k in range(4):
                        ins = nc.tensor.transpose(b[:, tok(k)], hT[:, 4 * half + k, tok(c)], ident)
                    ready(ins)
            assert at[0] == len(jobs)

        @block.scalar
        def _(act):
            done, take = every(act)
            fn = nc.scalar.activation
            act.wait_ge(S("cond_in"), 32)
            act.wait_ge(S("zeroed"), 1)
            done(fn(sil[:, :, 0:2], cc[:].rearrange("p j k -> p k j"), ACT.Silu), "silu_c")

            def mod_row_copy(l, i):
                n = MOD_PARTS.index((l, i))
                act.wait_ge(*computed("mod_rows", l, i))
                if n:
                    act.wait_ge(*computed("mod", *MOD_PARTS[n - 1]))
                take(fn(mod_rows[:], bank("mod_rows", l, i), ACT.Copy), "mod_rows", l, i)

            def beside(*job):
                for name, l, i in parts_at.get(job, []):
                    if name == "mod_rows":
                        mod_row_copy(l, i)

            for l, i in MOD_PARTS[:MODS_FIRST]:
                mod_row_copy(l, i)

            def norm(n):
                for k in range(KD):
                    act.wait_ge(*x_ready(n, k))
                    fn(hT[:, k, :], xT[:, k, :], ACT.Square).then_inc(S("squares"), 1)
                act.wait_ge(*computed("ss", n))
                take(fn(rB[:], bank("ss", n)[:, 0:T], ACT.Sqrt, scale=1.0 / D, bias=eps[:, 0:1]), "ss", n)
                if n == 4:
                    return
                l, w = n // 2, n % 2
                for k in range(KD):
                    act.wait_ge(S("scaled"), KD * n + k + 1)
                    for j, t0, t1 in SEGS:
                        ins = fn(hT[:, k, t0:t1], hT[:, k, t0:t1], ACT.Identity, bias=modT[:, l, 3 * w, k, j:j + 1])
                    ins.then_inc(S("h"), 1)

            norm(0)
            for h in range(4):
                act.wait_ge(*computed("qT", h))
                take(fn(qT[:, h, :], bank("qT", h)[:, 0:T], ACT.Copy, scale=DK ** -0.5), "qT", h)
            for h in range(4):
                act.wait_ge(*computed("kT", h))
                take(fn(kT[:, h, :], bank("kT", h)[:, 0:T], ACT.Copy), "kT", h)
            for c in range(TILES):
                act.wait_ge(*computed("oN", c))
                take(fn(oS[:, c, :], bank("oN", c), ACT.Sigmoid), "oN", c)
            act.wait_ge(S("log_inputs"), 1)
            done(fn(tf, tf, ACT.Exp, scale=-1.0), "act_own")
            done(fn(tf, tf, ACT.Ln, bias=1.0), "logarithms")
            act.wait_ge(*taken("tb", TILES - 1))
            for c in range(TILES):
                for lo, n, sums in ((CQ0, Q_RANK, ms3), (CKV0, KV_RANK, ms6)):
                    done(fn(squares[:, 0:n], tail[:, c, lo:lo + n], ACT.Square, accum_out=sums[:, c:c + 1]), "act_own")
            fn(ms3, ms3, ACT.Sqrt, scale=1.0 / Q_RANK, bias=eps[:, 0:1])
            done(fn(ms6, ms6, ACT.Sqrt, scale=1.0 / KV_RANK, bias=eps[:, 0:1]), "roots")

            def head_squares(c, n):
                act.wait_ge(S("hm_sum"), n)
                for h in range(4):
                    done(fn(squares[:, 0:P], hsum[:, c, h * P:(h + 1) * P], ACT.Square,
                            accum_out=ms12[:, 4 * c + h:4 * c + h + 1]), "act_own")

            for pair in range(3):
                two = [(u, *units[u]) for u in (2 * pair, 2 * pair + 1)]
                if pair == 1:
                    head_squares(0, 1)
                act.wait_ge(S("ml_small"), pair + 1)
                fn(aexp, mx, ACT.Exp)
                fn(emq, emq, ACT.Exp)
                fn(dec, dec, ACT.Exp)
                fn(wk, wk, ACT.Exp).then_inc(S("ml_exps"), 1)
                beside("MR", 2 * pair)
                for u, d, c in two:
                    act.wait_ge(*taken("MR", u))
                    for h in range(4):
                        ins = fn(ET[d][:, h * P:(h + 1) * P], mrt[d][:, h * P:(h + 1) * P], ACT.Exp,
                                 bias=rr[:, d, c, h:h + 1])
                    ins.then_inc(S("et"), 1)
            head_squares(2, 2)
            head_squares(1, 3)
            done(fn(ms12, ms12, ACT.Sqrt, scale=1.0 / DK, bias=eps[:, 0:1]), "roots")
            beside("cqT", 0)
            for k in range(3):
                act.wait_ge(*computed("cqT", k))
                take(fn(cqT[:, k, :], bank("cqT", k)[:, 0:T], ACT.Copy), "cqT", k)
            for k in range(2):
                act.wait_ge(*computed("kvT", k))
                take(fn(kvT[:, k, :], bank("kvT", k), ACT.Copy), "kvT", k)
            act.wait_ge(*computed("kpT"))
            take(fn(kpe[NOPE:QK_DIM, :], bank("kpT")[NOPE:QK_DIM, :], ACT.Copy), "kpT")
            beside("hmT", 0)
            act.wait_ge(S("even_out"), 32)
            for h in range(4):
                act.wait_ge(*computed("hmT", h))
                take(fn(mix[:, h, :], bank("hmT", h)[:, 0:T], ACT.Copy), "hmT", h)
            act.wait_ge(S("ml_out"), 80)
            for h in range(MLA_H):
                act.wait_ge(*computed("qf", h))
                take(fn(qfT[0:QK_DIM, h, :], bank("qf", h)[0:QK_DIM, 0:T], ACT.Copy), "qf", h)
            for h in range(MLA_H):
                act.wait_ge(*computed("kn", h))
                take(fn(kfT[0:NOPE, h, :], bank("kn", h)[0:NOPE, :], ACT.Copy), "kn", h)
            act.wait_ge(S("k_rot"), 1)
            done(fn(kfT[NOPE:QK_DIM, :, :], bc(kpe[NOPE:QK_DIM, :], 1, [ROPE, MLA_H, KEYS]), ACT.Copy), "keys")
            scale = QK_DIM ** -0.5
            for c in range(TILES):
                nk = P if c == 0 else 3 * P

                def exponentials(h):
                    n = c * MLA_H + h
                    act.wait_ge(S("score_max"), n + 1)
                    if n >= 2:
                        act.wait_ge(*computed("pT", (n - 2) // MLA_H, (n - 2) % MLA_H))
                        act.wait_ge(S("probs"), n - 1)
                    take(fn(pr[:, n % 2, 0:nk], bank("sc", c, h)[:, 0:nk], ACT.Exp, scale=scale,
                            bias=nb[:, n % 2:n % 2 + 1], accum_out=rs[:, n % 2:n % 2 + 1]), "sc", c, h)

                exponentials(0)
                for h in range(MLA_H):
                    n = c * MLA_H + h
                    if h + 1 < MLA_H:
                        exponentials(h + 1)
                    beside("pT", c, h)
                    act.wait_ge(*computed("pT", c, h))
                    take(fn(prT[:, n % 2, 0:nk], bank("pT", c, h)[:, 0:nk], ACT.Copy), "pT", c, h)
                    if h % 2:
                        act.wait_ge(*computed("pv", c, h // 2))
                        take(fn(mix[:, 4 + h // 2, c * P:(c + 1) * P], bank("pv", c, h // 2)[:, 0:P], ACT.Copy),
                             "pv", c, h // 2)

            def router(l):
                act.wait_ge(S("route_shift"), 2 * l + 1)
                done(fn(route[:, 3, :, 0:GROUPS], route[:, 3, :, 0:GROUPS], ACT.Exp), "route_exp")
                act.wait_ge(S("route_shift"), 2 * l + 2)
                done(fn(route[:, 10, :, 2:3], route[:, 10, :, 2:3], ACT.Exp), "route_exp")

            def rows_out(l):
                for c in range(TILES):
                    for half in range(2):
                        act.wait_ge(*computed("hr", l, c, half))
                        if c == 0 and half == 0:
                            act.wait_ge(*computed("ss", 2 * l + 1))
                        take(fn(hrows[:, c, 512 * half:512 * half + 512], bank("hr", l, c, half), ACT.Copy), "hr", l, c, half)

            def gathered(l):
                kind = f"gathered{l}_"

                def copy_turned(e, u):
                    act.wait_ge(S(f"{kind}turned"), e + 1)
                    fn(hg[u].rearrange("p (w k) s -> p w (k s)", w=2), psum[:, 0:2, 0:4 * CAP], ACT.Copy)\
                        .then_inc(S(f"{kind}hg"), 1)

                def expert(e, u, i, more, first):
                    for j in range(2):
                        act.wait_ge(S(f"{kind}gu_computed"), e * 2 + (j + 1))
                        fn(sgs[:, j, :], psum[:, 2 + j, 0:CAP], ACT.Silu).then_inc(S(f"{kind}silu"), 1)
                    if more:
                        copy_turned(e + 1, 1 - u)
                    act.wait_ge(S(f"{kind}y_computed"), e * 2 + 1)
                    if not first:
                        act.wait_ge(S(f"{kind}yrow{u}_out"), i * 16)
                    fn(yrow[u][0:CAP, 0:512], psum[0:CAP, 4 + 2 * u, :], ACT.Copy).then_inc(S(f"{kind}ya"), 1)

                copy_turned(0, 0)
                for u in range(2):
                    expert(u, u, 0, True, True)
                with act.Fori(1, EXPERTS // 2 - 1) as i:
                    for u in range(2):
                        expert(i * 2 + u, u, i, True, False)
                for u in range(2):
                    expert(EXPERTS - 2 + u, u, EXPERTS // 2 - 1, u == 0, False)

            def dense(l):
                with act.Fori(0, EXPERTS // 2) as i:
                    for u in range(2):
                        e = i * 2 + u
                        for j in range(2):
                            act.wait_ge(S(f"dense{l}_gu_computed"), e * 2 + (j + 1))
                            fn(sg[:, j, :], psum[:, 2 * j, 0:T], ACT.Silu).then_inc(S(f"dense{l}_silu"), 1)

            def moe(l):
                router(l)
                rows_out(l)
                gathered(l)
                with overflow(act, l):
                    dense(l)

            norm(1)
            moe(0)
            norm(2)
            act.wait_ge(S("pads"), 1)

            def conv_activation(n):
                i = CONV_ORDER[n]
                act.wait_ge(S("conv_tile"), n + 1)
                done(fn(conv[:, i, :], conv[:, i, :], ACT.Silu), "conv_act")

            for n, i in enumerate(CONV_ORDER):
                if n == 8:
                    act.wait_ge(*computed("dg"))
                    take(fn(dg.rearrange("p c n -> p (c n)"), bank("dg")[:, 0:TILES * 32], ACT.Copy), "dg")
                    act.wait_ge(S("log_inputs"), 2)
                    done(fn(sp, sp, ACT.Exp, scale=-1.0), "act_own")
                    done(fn(sp, sp, ACT.Ln, bias=1.0), "logarithms")
                    fn(wA, alog[:].rearrange("p d h -> p (d h)"), ACT.Exp).then_inc(S("odd_gate_exps"), 1)
                    for d in range(2):
                        ins = fn(beta[:, d], dg[:, :, 24 + 4 * d:28 + 4 * d], ACT.Sigmoid)
                    ins.then_inc(S("odd_gate_exps"), 1)
                if n == 12:
                    for head in range(8):
                        act.wait_ge(*computed("l2", head))
                        take(fn(l2[:, head, :], bank("l2", head)[:, 0:T], ACT.Sqrt, bias=eps[:, 0:1]), "l2", head)
                act.wait_ge(*computed("xb", i))
                fn(cin[:, i, PAD:PAD + PROMPT], bank("xb", i)[:, 0:PROMPT], ACT.Copy)
                take(fn(cin[:, i, 3 * PAD + PROMPT:3 * PAD + T], bank("xb", i)[:, PROMPT:T], ACT.Copy), "xb", i)
                if n >= 2:
                    conv_activation(n - 2)
                if n == 9:
                    for t0, t1, pads in l2_segs:
                        fn(l2[:, :, t0:t1], conv[:, 8:16, t0 + pads:t1 + pads], ACT.Square)\
                            .then_inc(S("l2_squares"), 1)
                if n == 12:
                    act.wait_ge(S("odd_cum"), 1)
                    fn(ecb, cb, ACT.Exp)
                    fn(etot, tot, ACT.Exp)
                    fn(edif, edif, ACT.Exp).then_inc(S("odd_gate_exps"), 1)
            conv_activation(CONV_TILES - 2)
            conv_activation(CONV_TILES - 1)
            for name, dst in (("zs", zs), ("zg", zg)):
                for c in range(TILES):
                    act.wait_ge(*computed(name, c))
                    take(fn(dst[:, c, :], bank(name, c), ACT.Silu), name, c)
            for c in range(TILES):
                for name, dst in (("tk", gk), ("tv", gv)):
                    act.wait_ge(*computed(name, c))
                    take(fn(dst[:, c, :], bank(name, c), ACT.Copy), name, c)

            def decays(tile_, u, d, c, first_head, name):
                for h in range(4):
                    ins = fn(tile_[:, h * P:(h + 1) * P], tile_[:, h * P:(h + 1) * P], ACT.Exp,
                             bias=ncb[:, d, c, first_head + h:first_head + h + 1])
                ins.then_inc(S(name), 1)

            for pair in range(3):
                two = [(u, *units[u]) for u in (2 * pair, 2 * pair + 1)]
                for u, d, c in two:
                    act.wait_ge(*taken("Eg", u))
                    decays(EB[d], u, d, c, 8, "eg_done")
                for u, d, c in two:
                    act.wait_ge(*computed("X0", u))
                    take(fn(X[d], bank("X0", u), ACT.Copy), "X0", u)
                for n in range(1, 7):
                    for u, d, c in two:
                        act.wait_ge(*computed("T1", u, n))
                        take(fn(TT[d], bank("T1", u, n), ACT.Copy), "T1", u, n)
                    if n <= 2:
                        for u, d, c in two:
                            act.wait_ge(*taken("Es", u, n - 1))
                            decays(E1[d], u, d, c, 4 * (n - 1), "es_done")
                for u, d, c in two:
                    act.wait_ge(*computed("U", u))
                    take(fn(U[d], bank("U", u), ACT.Copy), "U", u)
                if pair == 0:
                    for d in range(2):
                        act.wait_ge(*computed("hT", d))
                        take(fn(hsO[:, d, :], bank("hT", d), ACT.Copy), "hT", d)
            scratch = G[0][:, 0:512]
            for c in range(TILES):
                act.wait_ge(S("odd_sums"), c + 1)
                done(fn(scratch, ysum[:, c, :], ACT.Square, accum_out=ms3[:, c:c + 1]), "act_own")
            done(fn(ms3, ms3, ACT.Sqrt, scale=1.0 / 512, bias=eps[:, 0:1]), "roots")
            for c in range(TILES):
                for h in range(4):
                    done(fn(scratch[:, 0:P], ogsum[:, c, h * P:(h + 1) * P], ACT.Square,
                            accum_out=ms12[:, 4 * c + h:4 * c + h + 1]), "act_own")
            done(fn(ms12, ms12, ACT.Sqrt, scale=1.0 / DK, bias=eps[:, 0:1]), "roots")
            for f in range(8):
                act.wait_ge(*computed("mT", f))
                take(fn(mix[:, f, :], bank("mT", f)[:, 0:T], ACT.Copy), "mT", f)
            norm(3)
            moe(1)
            norm(4)
            for c in range(TILES):
                for half in range(2):
                    act.wait_ge(*computed("fin", c, half))
                    dst = mix[:].rearrange("p k t -> p (k t)")[:, c * D:(c + 1) * D]\
                        .rearrange("p (q k) -> p k q", k=KD)[:, 4 * half:4 * half + 4, :]
                    fn(dst, heads(bank("fin", c, half), 4), ACT.Copy).then_inc(S("y_rows"), 1)

        @block.vector
        def _(dve):
            done, take = every(dve)
            v = nc.vector
            tt, ts, stt = v.tensor_tensor, v.tensor_scalar, v.scalar_tensor_tensor
            own = "dve_own"

            def o_(ins):
                done(ins, own)

            o_(v.memset(sil[:], 0.0))
            o_(v.memset(eps[:], EPS))
            o_(v.memset(unused[:], OOB))
            zero_row = route[:].rearrange("p a c n -> p (a c n)")[:, 0:D]
            done(v.memset(zero_row, 0.0), "zeroed")
            o_(v.memset(kpin[:, 0:NOPE], 0.0))
            for k in range(KD):
                dve.wait_ge(*computed("xt", k))
                take(v.tensor_copy(xT[:, k, :], bank("xt", k)[:, 0:T]), "xt", k)

            def modulation(l, i):
                dve.wait_ge(*computed("mod", l, i))
                take(tt(modT[:, l, i], bank("mod", l, i)[:, 0:16].rearrange("p (m j) -> p m j", j=2),
                        bc(adab[:, l, i], 2, [P, KD, 2]), ALU.add), "mod", l, i)
                if i % 3 == 1:
                    w = i // 3
                    o_(stt(amp[:, l, w], modT[:, l, i], 1.0, bc(gains[:, 2 * w + l, :], 2, [P, KD, 2]), ALU.add, ALU.mult))

            def beside(*job):
                for name, l, i in parts_at.get(job, []):
                    if name == "mod":
                        modulation(l, i)

            dve.wait_ge(S("bias_in"), 32)
            dve.wait_ge(S("gains_in"), 80)
            for l, i in MOD_PARTS[:MODS_FIRST]:
                modulation(l, i)

            def norm(n):
                dve.wait_ge(*taken("ss", n))
                o_(v.reciprocal(rB[:], rB[:]))
                l, w = n // 2, n % 2
                for k in range(KD):
                    if n == 4:
                        stt(hT[:, k, :], xT[:, k, :], gains[:, 4, k:k + 1], rB[:], ALU.mult, ALU.mult)\
                            .then_inc(S("h_final"), 1)
                        continue
                    for j, t0, t1 in SEGS:
                        ins = stt(hT[:, k, t0:t1], xT[:, k, t0:t1], amp[:, l, w, k, j:j + 1], rB[:, t0:t1],
                                  ALU.mult, ALU.mult)
                    ins.then_inc(S("scaled"), 1)

            def b4(ap):
                return bc(ap, 2, [P, 4, P])

            norm(0)
            for name, dst in (("kN", kN), ("vN", vN)):
                for c in range(TILES):
                    dve.wait_ge(*computed(name, c))
                    take(v.tensor_copy(dst[:, c, :], bank(name, c)), name, c)
            for c in range(TILES):
                dve.wait_ge(*computed("ta", c))
                take(v.tensor_copy(tail[:, c, 0:512], bank("ta", c)), "ta", c)
            for c in range(TILES):
                dve.wait_ge(*computed("tb", c))
                take(v.tensor_copy(tail[:, c, 512:TAIL], bank("tb", c)[:, 0:TAIL - 512]), "tb", c)
            dve.wait_ge(S("small_in"), SMALL)
            dve.wait_ge(*computed("cols"))
            take(v.tensor_copy(colsT[:], bank("cols")[:, 0:P]), "cols")
            done(v.tensor_copy(mln[:, 1].rearrange("p d h -> p (d h)"), colsT[:, 120:128]), "n_start")
            for d in range(2):
                o_(tt(li[:, d], tail[:, :, 4 * d:4 * d + 4], bc(bias_e[:, 4 * d:4 * d + 4], 1, [P, TILES, 4]), ALU.add))
                o_(tt(lf[:, d], tail[:, :, 8 + 4 * d:12 + 4 * d], bc(bias_e[:, 8 + 4 * d:12 + 4 * d], 1, [P, TILES, 4]), ALU.add))
            done(stt(tf, lf, -1.0, lf, ALU.mult, ALU.max), "log_inputs")
            o_(ts(lf, lf, 0.0, None, ALU.min))
            dve.wait_ge(S("logarithms"), 1)
            done(tt(lf, lf, tf, ALU.subtract), "log_decay")
            dve.wait_ge(*computed("cum", 0))
            take(v.tensor_copy(sm(72, 48), bank("cum", 0)[:, 0:48]), "cum", 0)
            o_(v.tensor_copy(mst[:, 1].rearrange("p d h -> p (d h)"), mprev0[:]))
            o_(v.memset(mst[:, 0], 0.0))
            done(tt(rr, li, bcum, ALU.subtract), "r")

            for pair in range(3):
                two = [(u, *units[u]) for u in (2 * pair, 2 * pair + 1)]
                sequence, moves_on, s = pair > 0, pair < 2, int(pair > 0)
                m = mst[:, s]
                at_0, at_1 = (TILES * d + c for u, d, c in two)

                def of_pair(x):
                    return x.rearrange("p d c h -> p (d c) h")[:, at_0:at_1 + 1:at_1 - at_0, :]

                if pair:
                    dve.wait_ge(S("ml_exps"), pair)
                for u, d, c in two:
                    dve.wait_ge(*computed("R", u))
                    v.tensor_reduce(mxa[:, d], heads(bank("R", u), 4), AX, ALU.max)
                    take(tt(heads(Rm[d], 4), heads(bank("R", u), 4), bc(neg_ts[d], 1, [P, 4, P]), ALU.add), "R", u)
                    ins = v.tensor_reduce(mx[:, d], heads(Rm[d], 4), AX, ALU.max)
                o_(ins)
                tt(mxa, mxa, m, ALU.max)
                o_(tt(mx, mx, m, ALU.max))
                done(ts(nmr, mx, -1.0, None, ALU.mult), "neg_m")
                tt(emq, nmr, of_pair(bcum), ALU.subtract)
                tt(dec, m, mxa, ALU.subtract)
                tt(wk, of_pair(rr), mxa, ALU.subtract)
                o_(tt(mx, m, mx, ALU.subtract))
                done(tt(m, mxa, of_pair(btot), ALU.add), "ml_small")
                for u, d, c in two:
                    dve.wait_ge(*computed("MR", u))
                    take(tt(heads(mrt[d], 4), heads(bank("MR", u), 4), bc(neg_st[d], 1, [P, 4, P]), ALU.add), "MR", u)
                beside("MR", 2 * pair)
                if moves_on:
                    dve.wait_ge(S("ml_exps"), pair + 1)
                    for u, d, c in two:
                        done(tt(heads(kw[d], 4), heads(kN[:, c, :], 4), b4(wk[:, d]), ALU.mult), "kw")
                for u, d, c in two:
                    dve.wait_ge(*computed("SK", u))
                    dve.wait_ge(S("et"), u + 1)
                    take(tt(ST[d], ET[d], bank("SK", u), ALU.mult), "SK", u)
                dve.wait_ge(S("ml_exps"), pair + 1)
                for u, d, c in two:
                    dve.wait_ge(*computed("DN", u))
                    if sequence:
                        o_(tt(den[:, d], aexp[:, d], bank("DN", u)[:, 4:8], ALU.mult))
                        take(tt(den[:, d], den[:, d], bank("DN", u)[:, 0:4], ALU.add), "DN", u)
                    else:
                        take(v.tensor_copy(den[:, d], bank("DN", u)[:, 0:4]), "DN", u)
                o_(stt(den, den, -1.0, den, ALU.mult, ALU.max))
                o_(tt(den, den, emq, ALU.max))
                o_(v.reciprocal(den2, den))
                for u, d, c in two:
                    first = (d, c) in ((0, 0), (0, 1), (1, 2))
                    dst = hsum[:, c, :] if first else num[d]
                    if sequence:
                        dve.wait_ge(*computed("N2", u))
                        take(tt(heads(carried[d], 4), heads(bank("N2", u), 4), b4(aexp[:, d]), ALU.mult), "N2", u)
                        take(tt(carried[d], carried[d], bank("N1", u), ALU.add), "N1", u)
                        o_(tt(heads(dst, 4), heads(carried[d], 4), b4(den2[:, d]), ALU.mult))
                    else:
                        dve.wait_ge(*computed("N1", u))
                        take(tt(heads(dst, 4), heads(bank("N1", u), 4), b4(den2[:, d]), ALU.mult), "N1", u)
                    if not first:
                        done(tt(hsum[:, c, :], hsum[:, c, :], num[d], ALU.add), "hm_sum")
                if pair == 0:
                    dve.wait_ge(S("roots"), 1)
                    o_(v.reciprocal(ms3, ms3))
                    o_(v.reciprocal(ms6, ms6))
                    for c in range(TILES):
                        ins = stt(ckn[:, c], tail[:, c, CKV0:CKV0 + KV_RANK], ms6[:, c:c + 1], gkv, ALU.mult, ALU.mult)
                    done(ins, "kv_norm")
                    for c in range(TILES):
                        ins = stt(cqn[:, c], tail[:, c, CQ0:CQ0 + Q_RANK], ms3[:, c:c + 1], gq, ALU.mult, ALU.mult)
                    done(ins, "mla_norm")
                    dve.wait_ge(*taken("oN", 2))
                    o_(tt(oS, oS, bc(gml, 1, [P, TILES, 512]), ALU.mult))
                if moves_on:
                    for u, d, c in two:
                        dve.wait_ge(*computed("CU", u))
                        if sequence:
                            o_(tt(heads(mlC[:, 1, d, :], 4), heads(mlC[:, 1, d, :], 4), b4(dec[:, d]), ALU.mult))
                            take(tt(mlC[:, 1, d, :], mlC[:, 1, d, :], bank("CU", u), ALU.add), "CU", u)
                        else:
                            take(v.tensor_copy(mlC[:, 0, d, :], bank("CU", u)), "CU", u)
                    for u, d, c in two:
                        dve.wait_ge(*computed("NU", u))
                        if sequence:
                            o_(tt(mln[:, 1, d, :], mln[:, 1, d, :], dec[:, d], ALU.mult))
                            take(tt(mln[:, 1, d, :], mln[:, 1, d, :], bank("NU", u)[:, 0:4], ALU.add), "NU", u)
                        else:
                            take(v.tensor_copy(mln[:, 0, d, :], bank("NU", u)[:, 0:4]), "NU", u)

            dve.wait_ge(S("roots"), 2)
            o_(v.reciprocal(ms12, ms12))
            for c in range(TILES):
                for h in range(4):
                    at_ = slice(h * P, (h + 1) * P)
                    ins = stt(hsum[:, c, at_], hsum[:, c, at_], ms12[:, 4 * c + h:4 * c + h + 1], oS[:, c, at_],
                              ALU.mult, ALU.mult)
            done(ins, "hm")
            beside("cqT", 0)
            beside("hmT", 0)
            r = slice(NOPE, QK_DIM)
            dve.wait_ge(*computed("kpR"))
            dve.wait_ge(*taken("kpT"))
            take(tt(rtmp[r, 0:SAMPLE], sinT[r], bank("kpR")[r, 0:SAMPLE], ALU.mult), "kpR")
            o_(tt(kpe[r, 2 * P:4 * P], kpe[r, 2 * P:4 * P], cosT[r], ALU.mult))
            done(tt(kpe[r, 2 * P:4 * P], kpe[r, 2 * P:4 * P], rtmp[r, 0:SAMPLE], ALU.add), "k_rot")
            for i in range(4):
                q = qfT[r, 2 * i:2 * i + 2, PROMPT:T]
                dve.wait_ge(*computed("qR", i))
                tmp = rtmp[r, :].rearrange("p (h t) -> p h t", h=2)
                take(tt(tmp, bc(sinT[r], 1, [ROPE, 2, SAMPLE]), bank("qR", i)[r, :].rearrange("p (h t) -> p h t", h=2),
                        ALU.mult), "qR", i)
                o_(tt(q, q, bc(cosT[r], 1, [ROPE, 2, SAMPLE]), ALU.mult))
                done(tt(q, q, tmp, ALU.add), "q_rot")
            for n in range(4):
                dve.wait_ge(*computed("vv", n))
                take(v.tensor_copy(vv[:, n, :], bank("vv", n)), "vv", n)
            scale = QK_DIM ** -0.5
            for c in range(TILES):
                nk = P if c == 0 else 3 * P

                def score_max(h):
                    k = (c * MLA_H + h) % 2
                    dve.wait_ge(*computed("sc", c, h))
                    o_(v.tensor_reduce(nbm[:, k:k + 1], bank("sc", c, h)[:, 0:nk], AX, ALU.max))
                    done(ts(nb[:, k:k + 1], nbm[:, k:k + 1], -scale, None, ALU.mult), "score_max")

                score_max(0)
                for h in range(MLA_H):
                    n = c * MLA_H + h
                    k = n % 2
                    if h + 1 < MLA_H:
                        score_max(h + 1)
                    dve.wait_ge(*taken("sc", c, h))
                    o_(v.reciprocal(rsi[:, k:k + 1], rs[:, k:k + 1]))
                    done(ts(pr[:, k, 0:nk], pr[:, k, 0:nk], rsi[:, k:k + 1], None, ALU.mult), "probs")
                    beside("pT", c, h)

            def residual(name, l, part):
                for m in range(KD):
                    dve.wait_ge(*computed(name, l, m))
                    for j, t0, t1 in SEGS:
                        ins = stt(xT[:, m, t0:t1], bank(name, l, m)[:, t0:t1], modT[:, l, part, m, j:j + 1],
                                  xT[:, m, t0:t1], ALU.mult, ALU.add)
                    take(ins, name, l, m)

            def router(l):
                R = [route[:, n] for n in range(12)]

                def col(n, k=0):
                    return R[10][:, :, n:n + 1] if k == 0 else R[10][:, :, n:n + 1].to_broadcast([P, TILES, k])

                dve.wait_ge(S("rows_zero"), 16)
                dve.wait_ge(*computed("rt", l))
                take(tt(R[0], bank("rt", l)[:, 0:TILES * ROUTES].rearrange("p (c n) -> p c n", c=TILES),
                        bc(br[:, l, :], 1, [P, TILES, ROUTES]), ALU.add), "rt", l)
                g, el = R[0][:, :, 0:GROUPS], R[0][:, :, GROUPS:ROUTES]

                def first_max(dst, top, src, n, sc):
                    rk = rank[:, EXPERTS - n:EXPERTS]
                    o_(v.tensor_reduce(col(top), src, AX, ALU.max))
                    o_(tt(dst, src, col(top, n), ALU.is_equal))
                    o_(tt(dst, dst, bc(rk, 1, [P, TILES, n]), ALU.mult))
                    o_(v.tensor_reduce(col(sc), dst, AX, ALU.max))
                    o_(tt(dst, dst, col(sc, n), ALU.is_equal))

                gs = R[1][:, :, 0:GROUPS]
                first_max(gs, 0, g, GROUPS, 9)
                done(tt(R[3][:, :, 0:GROUPS], g, col(0, GROUPS), ALU.subtract), "route_shift")
                pen = R[2][:, :, 0:GROUPS]
                o_(ts(pen, gs, -NEG, NEG, ALU.mult, ALU.add))
                em = R[4][:, :, 0:EXPERTS]

                def by_group(x):
                    return x.rearrange("p c (g e) -> p c g e", g=GROUPS)

                full4 = [P, TILES, GROUPS, EXPERTS // GROUPS]
                o_(tt(by_group(em), by_group(el), bc(gs, 3, full4), ALU.mult))
                o_(tt(by_group(em), by_group(em), bc(pen, 3, full4), ALU.add))
                o1, o2 = R[5][:, :, 0:EXPERTS], R[6][:, :, 0:EXPERTS]
                first_max(o1, 3, em, EXPERTS, 9)
                o_(stt(em, o1, 2 * NEG, em, ALU.mult, ALU.add))
                first_max(o2, 4, em, EXPERTS, 9)
                done(tt(col(2), col(4), col(3), ALU.subtract), "route_shift")
                done(tt(comb[:], o1, o2, ALU.add), "chosen")
                oh = [o1, o2]
                rk, ex, keep, slot, wt = (slots_f[:, n] for n in range(5))
                prod = R[7][:, :, 0:EXPERTS]
                for w in range(2):
                    o_(tt(prod, oh[w], bc(rank, 1, [P, TILES, EXPERTS]), ALU.mult))
                    o_(v.tensor_reduce(ex[:, w, :], prod, AX, ALU.max))
                dve.wait_ge(*computed("rk", l))
                for w in range(2):
                    o_(tt(prod, oh[w], bank("rk", l)[:, 0:TILES * EXPERTS].rearrange("p (c e) -> p c e", c=TILES), ALU.mult))
                    o_(v.tensor_reduce(rk[:, w, :], prod, AX, ALU.max))
                inc = R[8][:, :, 0:EXPERTS]
                o_(ts(inc, bank("rk", l)[:, 0:TILES * EXPERTS].rearrange("p (c e) -> p c e", c=TILES), CAP + 0.5, None, ALU.is_gt))
                take(v.tensor_reduce(slots_f[:, 5, 0, 0:1], bank("rk", l)[:, TILES * EXPERTS:(TILES + 1) * EXPERTS], AX, ALU.max), "rk", l)
                done(ts(flag[0:1, l:l + 1], slots_f[0:1, 5, 0, 0:1], CAP + 0.5, None, ALU.is_gt), "flag")
                o_(ts(keep, rk, CAP + 0.5, None, ALU.is_le))
                o_(stt(slot, ex, -float(CAP), rk, ALU.mult, ALU.add))
                o_(ts(slot, slot, float(EXPERTS * CAP - 1 - OOB), None, ALU.add))
                o_(tt(slot, slot, keep, ALU.mult))
                o_(ts(slot, slot, float(OOB), None, ALU.add))
                done(v.tensor_copy(slots_i[:], slot), "slots")
                dve.wait_ge(S("route_exp"), 2 * l + 1)
                o_(v.tensor_reduce(col(5), R[3][:, :, 0:GROUPS], AX, ALU.add))
                dve.wait_ge(S("route_exp"), 2 * l + 2)
                o_(ts(col(6), col(2), 1.0, None, ALU.add))
                o_(tt(col(6), col(6), col(5), ALU.mult))
                o_(v.reciprocal(col(7), col(6)))
                o_(tt(col(8), col(7), col(2), ALU.mult))
                for w in range(2):
                    o_(tt(wt[:, w, :], col(7 + w).rearrange("p c n -> p (c n)"), keep[:, w, :], ALU.mult))
                o_(tt(o1, o1, col(7, EXPERTS), ALU.mult))
                o_(tt(o2, o2, col(8, EXPERTS), ALU.mult))
                o_(tt(comb[:], o1, o2, ALU.add))
                o_(tt(comb[:], comb[:], inc, ALU.mult))

            def gathered(l):
                kind = f"gathered{l}_"

                def expert(e, u, i, first):
                    for j in range(2):
                        dve.wait_ge(S(f"{kind}silu"), e * 2 + (j + 1))
                        tt(act_s[u][:, j, :], sgs[:, j, :], psum[:, 2 + j, CAP:2 * CAP], ALU.mult).then_inc(S(f"{kind}act"), 1)
                    dve.wait_ge(S(f"{kind}y_computed"), e * 2 + 2)
                    if not first:
                        dve.wait_ge(S(f"{kind}yrow{u}_out"), i * 16)
                    v.tensor_copy(yrow[u][0:CAP, 512:D], psum[0:CAP, 5 + 2 * u, :]).then_inc(S(f"{kind}yb"), 1)

                for u in range(2):
                    expert(u, u, 0, True)
                with dve.Fori(1, EXPERTS // 2) as i:
                    for u in range(2):
                        expert(i * 2 + u, u, i, False)

            def dense(l):
                kind = f"dense{l}_"
                dve.wait_ge(S("h_rows_out"), 16 * TILES * (l + 1))
                done(v.memset(mix[:], 0.0), f"{kind}merged")
                v.memset(ms3, 0.0).then_inc(S(f"{kind}act"), 2)
                v.memset(ms6, 0.0).then_inc(S(f"{kind}y_taken"), 4)
                with dve.Fori(0, EXPERTS // 2) as i:
                    for u in range(2):
                        e = i * 2 + u
                        for j in range(2):
                            dve.wait_ge(S(f"{kind}silu"), e * 2 + (j + 1))
                            tt(actT[u][:, j, :], sg[:, j, :], psum[:, 2 * j + 1, 0:T], ALU.mult)\
                                .then_inc(S(f"{kind}act"), 1)
                        for q in range(6):
                            c, half = q // 2, slice(q % 2 * 512, q % 2 * 512 + 512)
                            dve.wait_ge(S(f"{kind}y_computed"), e * 6 + (q + 1))
                            stt(yacc[:, c, half], psum[:, 4 + (6 * u + q) % 4, :], comb[:, c, bass.ds(e, 1)],
                                yacc[:, c, half], ALU.mult, ALU.add).then_inc(S(f"{kind}y_taken"), 1)
                        dve.wait_ge(S(f"{kind}y_taken"), e * 6 + 10)
                for c in range(TILES):
                    dve.wait_ge(S(f"chosen{c}_in"), 16 * (l + 1))
                    done(stt(ysel[:, c, 0, :], ysel[:, c, 0, :], slots_f[:, 4, 0, c:c + 1], yacc[:, c, :],
                             ALU.mult, ALU.add), f"{kind}merged")
                    done(v.tensor_copy(diag[:, c, 0, :], ident), f"{kind}merged")

            def moe(l):
                if l == 0:
                    dve.wait_ge(S("even_out"), 32)
                else:
                    dve.wait_ge(S("odd_out"), 64)
                o_(v.memset(hrow[0], 0.0))
                done(v.memset(hrow[1], 0.0), "rows_clear")
                router(l)
                for c in range(TILES):
                    for w in range(2):
                        ins = ts(diag[:, c, w, :], ident, slots_f[:, 4, w, c:c + 1], None, ALU.mult)
                ins.then_inc(S("diag"), 1)
                gathered(l)
                with overflow(dve, l):
                    dense(l)

            residual("o", 0, 2)
            norm(1)
            moe(0)
            residual("yt", 0, 5)
            norm(2)
            for t0, t1 in ((0, PAD), (PAD + PROMPT, 3 * PAD + PROMPT), (CIN - PAD, CIN)):
                ins = v.memset(cin[:, :, t0:t1], 0.0)
            done(ins, "pads")

            def query_key_norms():
                for i in range(8):
                    dve.wait_ge(*taken("l2", i))
                    o_(v.reciprocal(l2[:, i, :], l2[:, i, :]))
                for t0, t1, pads in l2_segs:
                    at_ = slice(t0 + pads, t1 + pads)
                    stt(conv[:, 8:12, at_], conv[:, 8:12, at_], DK ** -0.5, l2[:, 0:4, t0:t1], ALU.mult, ALU.mult)
                    ins = tt(conv[:, 12:16, at_], conv[:, 12:16, at_], l2[:, 4:8, t0:t1], ALU.mult)
                done(ins, "l2_done")

            for n, i in enumerate(CONV_ORDER):
                if n == 8:
                    dve.wait_ge(*taken("dg"))
                    for d in range(2):
                        for lo, n, src in ((0, 8, dg[:, :, 8 * d:8 * d + 8]), (8, 4, dg[:, :, 16 + 4 * d:20 + 4 * d])):
                            o_(tt(spin[:, d, :, lo:lo + n], src, bc(bias_o[:, d, lo:lo + n], 1, [P, TILES, n]), ALU.add))
                    done(stt(sp, spin, -1.0, spin, ALU.mult, ALU.max), "log_inputs")
                    o_(ts(spin, spin, 0.0, None, ALU.max))
                    dve.wait_ge(S("logarithms"), 2)
                    o_(tt(sp, sp, spin, ALU.add))
                    dve.wait_ge(S("odd_gate_exps"), 1)
                    o_(ts(wA, wA, -1.0, None, ALU.mult))
                    for d in range(2):
                        ins = tt(lg[:, d], sp[:, d], bc(wA[:, 12 * d:12 * d + 12], 1, [P, TILES, 12]), ALU.mult)
                        o_(ins) if d == 0 else done(ins, "log_decay")
                if n == 12:
                    dve.wait_ge(*computed("cum", 1))
                    o_(v.tensor_copy(cb.rearrange("p d c h -> p (d c h)"), bank("cum", 1)[:, 0:72]))
                    take(v.tensor_copy(tot.rearrange("p d c h -> p (d c h)"), bank("cum", 1)[:, 72:144]), "cum", 1)
                    o_(tt(edif, tot, cb, ALU.subtract))
                    done(ts(ncb, cb, -1.0, None, ALU.mult), "odd_cum")
                    query_key_norms()
                if i < 8:
                    wcol = [colsT[:, w * 8 + i:w * 8 + i + 1] for w in range(CONV_W)]
                    bcol = colsT[:, 100 + i:101 + i]
                else:
                    wcol = [colsT[:, 40 + w * 12 + i - 8:41 + w * 12 + i - 8] for w in range(CONV_W)]
                    bcol = colsT[:, 108 + i - 8:109 + i - 8]
                dve.wait_ge(*taken("xb", i))
                o_(ts(conv[:, i, :], cin[:, i, 0:COUT], wcol[0], bcol, ALU.mult, ALU.add))
                for w in range(1, CONV_W):
                    ins = stt(conv[:, i, :], cin[:, i, w:w + COUT], wcol[w], conv[:, i, :], ALU.mult, ALU.add)
                    o_(ins) if w < CONV_W - 1 else done(ins, "conv_tile")

            for c in range(TILES):
                for name, dst, n in (("tx", xN, 512), ("tB", BN, 256)):
                    dve.wait_ge(*computed(name, c))
                    take(v.tensor_copy(dst[:, c, :], bank(name, c)[:, 0:n]), name, c)
            dve.wait_ge(S("odd_gate_exps"), 3)
            done(tt(edb, edif[:, :, :, 8:12], beta, ALU.mult), "odd_gates")

            def b8(ap):
                return bc(ap, 2, [P, 8, SSD_P])

            dve.wait_ge(S("skip"), 1)
            for pair in range(3):
                two = [(u, *units[u]) for u in (2 * pair, 2 * pair + 1)]
                sequence, moves_on, s = pair > 0, pair < 2, int(pair > 0)

                def first(d, c):
                    return (d, c) in ((0, 0), (0, 1), (1, 2))

                def level(n, u, d):
                    if n > 1:
                        dve.wait_ge(*computed("T1", u, n - 1))
                    done(tt(heads(LT[d], 4), heads(AT[d], 4), bc(lvl[n], 1, [P, 4, P]), ALU.mult), "lt")

                for u, d, c in two:
                    if pair:
                        dve.wait_ge(*computed("O1", u - 2))
                    dve.wait_ge(*computed("Eg", u))
                    take(tt(heads(EB[d], 4), heads(bank("Eg", u), 4), bc(neg_st[d], 1, [P, 4, P]), ALU.add), "Eg", u)
                for u, d, c in two:
                    dve.wait_ge(S("eg_done"), u + 1)
                    o_(tt(heads(EB[d], 4), heads(EB[d], 4), b4(beta[:, d, c]), ALU.mult))
                    dve.wait_ge(*computed("KK", u))
                    take(tt(AT[d], EB[d], bank("KK", u), ALU.mult), "KK", u)
                    o_(tt(heads(LT[d], 4), heads(AT[d], 4), bc(lvl[0], 1, [P, 4, P]), ALU.mult))
                    done(tt(heads(XT[d], 4), bc(ident, 1, [P, 4, P]), heads(LT[d], 4), ALU.subtract), "xt_first")
                    dve.wait_ge(*computed("KQ", u))
                    take(tt(PT[d], EB[d], bank("KQ", u), ALU.mult), "KQ", u)
                for u, d, c in two:
                    level(1, u, d)
                for n in range(1, 7):
                    if n < 6:
                        for u, d, c in two:
                            level(n + 1, u, d)
                    for u, d, c in two:
                        ys, og, hs = ysum[:, c, :], ogsum[:, c, :], hsT[:, s, d, :]
                        if n <= 2:
                            dve.wait_ge(*computed("Es", u, n - 1))
                            take(tt(heads(E1[d], 4), heads(bank("Es", u, n - 1), 4), bc(neg_st[d], 1, [P, 4, P]), ALU.add),
                                 "Es", u, n - 1)
                        elif n == 3:
                            dve.wait_ge(*computed("Y1", u))
                            if first(d, c):
                                take(tt(ys, skip[:, c, :], bank("Y1", u), ALU.add), "Y1", u)
                            else:
                                take(tt(ys, ys, bank("Y1", u), ALU.add), "Y1", u)
                        elif n == 4 and sequence:
                            dve.wait_ge(*computed("Y2", u))
                            take(tt(heads(y2[d], 8), heads(bank("Y2", u), 8), b8(ecb[:, d, c, 0:8]), ALU.mult), "Y2", u)
                            o_(tt(ys, ys, y2[d], ALU.add))
                        elif n == 5 and moves_on:
                            dve.wait_ge(*computed("HU", u))
                            if sequence:
                                o_(tt(heads(hs, 8), heads(hs, 8), b8(etot[:, d, c, 0:8]), ALU.mult))
                                take(tt(hs, hs, bank("HU", u), ALU.add), "HU", u)
                            else:
                                take(v.tensor_copy(hs, bank("HU", u)), "HU", u)
                        elif n == 6 and sequence:
                            dve.wait_ge(*computed("KS", u))
                            take(tt(heads(Rg[d], 4), heads(bank("KS", u), 4), b4(ecb[:, d, c, 8:12]), ALU.mult), "KS", u)
                            done(tt(Rg[d], gv[:, c, :], Rg[d], ALU.subtract), "rhs")
                            dve.wait_ge(*computed("O2", u))
                            dst = og if first(d, c) else y2[d]
                            take(tt(heads(dst, 4), heads(bank("O2", u), 4), b4(ecb[:, d, c, 8:12]), ALU.mult), "O2", u)
                            if not first(d, c):
                                o_(tt(og, og, y2[d], ALU.add))
                    for u, d, c in two:
                        dve.wait_ge(*computed("XT", u, n))
                        if n < 6:
                            dve.wait_ge(*computed("XX", u, n))
                        take(tt(XT[d], XT[d], bank("XT", u, n), ALU.subtract), "XT", u, n)
                        if n < 6:
                            dve.wait_ge(*taken("X0", u))
                            take(tt(X[d], X[d], bank("XX", u, n), ALU.subtract), "XX", u, n)
                    if n <= 2:
                        for u, d, c in two:
                            g = n - 1
                            dve.wait_ge(S("es_done"), 4 * pair + 2 * g + d + 1)
                            dve.wait_ge(*computed("GB", u, g))
                            take(tt(heads(G[d][:, g * 512:(g + 1) * 512], 4), heads(E1[d], 4),
                                    bc(bank("GB", u, g)[:, 0:P], 1, [P, 4, P]), ALU.mult), "GB", u, g)
                            if g:
                                o_(tt(heads(xdt[d], 8), heads(xN[:, c, :], 8), b8(sp[:, d, c, 0:8]), ALU.mult))
                                done(tt(heads(xw[d], 8), heads(xdt[d], 8), b8(edif[:, d, c, 0:8]), ALU.mult), "ssd_in")
                if moves_on:
                    for u, d, c in two:
                        dve.wait_ge(*taken("U", u))
                        done(tt(heads(Uw[d], 4), heads(U[d], 4), b4(edb[:, d, c]), ALU.mult), "uw")
                for u, d, c in two:
                    og = ogsum[:, c, :]
                    dve.wait_ge(*computed("O1", u))
                    if first(d, c) and not sequence:
                        take(v.tensor_copy(og, bank("O1", u)), "O1", u)
                    else:
                        take(tt(og, og, bank("O1", u), ALU.add), "O1", u)
                if moves_on:
                    for u, d, c in two:
                        sg_ = Sg[:, s, d, :]
                        dve.wait_ge(*computed("SU", u))
                        if sequence:
                            o_(tt(heads(sg_, 4), heads(sg_, 4), b4(etot[:, d, c, 8:12]), ALU.mult))
                            take(tt(sg_, sg_, bank("SU", u), ALU.add), "SU", u)
                        else:
                            take(v.tensor_copy(sg_, bank("SU", u)), "SU", u)
                if pair == 0:
                    for d in range(2):
                        dve.wait_ge(*computed("h0T", d))
                        take(v.tensor_copy(hsT[:, 1, d, :], bank("h0T", d)), "h0T", d)
                    dve.wait_ge(S("gdn_in"), 32)

            for c in range(TILES):
                done(tt(ysum[:, c, :], ysum[:, c, :], zs[:, c, :], ALU.mult), "odd_sums")
            dve.wait_ge(S("gate_gain"), 1)
            dve.wait_ge(S("odd_in"), 64)
            dve.wait_ge(S("roots"), 3)
            o_(v.reciprocal(ms3, ms3))
            for c in range(TILES):
                ins = stt(ysum[:, c, :], ysum[:, c, :], ms3[:, c:c + 1], gssd, ALU.mult, ALU.mult)
            done(ins, "odd_rows")
            dve.wait_ge(S("roots"), 4)
            o_(v.reciprocal(ms12, ms12))
            for c in range(TILES):
                for h in range(4):
                    at_ = slice(h * P, (h + 1) * P)
                    ins = stt(ogsum[:, c, at_], ogsum[:, c, at_], ms12[:, 4 * c + h:4 * c + h + 1], zg[:, c, at_],
                              ALU.mult, ALU.mult)
            done(ins, "odd_rows")
            residual("o", 1, 2)
            norm(3)
            moe(1)
            residual("yt", 1, 5)
            norm(4)
        build.free_words = room - used[1]


_INS = ['x_prompt', 'x_sample', 'c', 'cache_mla_kv', 'cache_mla_krope', 'state_mlstm_C', 'state_mlstm_n',
        'state_mlstm_m', 'state_ssd', 'state_gdn', 'c_ctx', 'ada_w', 'ada_b', 'norm_mix', 'norm_ffn',
        'w_in_even', 'ml_i_bias', 'ml_f_bias', 'ml_norm', 'mla_q_norm', 'mla_w_uq', 'mla_kv_norm', 'mla_w_ukv',
        'w_out_even', 'w_in_odd', 'ssd_conv_w', 'ssd_conv_b', 'ssd_dt_bias', 'ssd_A_log', 'ssd_D', 'ssd_norm',
        'gdn_conv_w', 'gdn_conv_b', 'gdn_dt_bias', 'gdn_A_log', 'gdn_norm', 'w_out_odd',
        'moe_w_group', 'moe_b_group', 'moe_w_expert', 'moe_b_expert', 'moe_w_gate', 'moe_w_up', 'moe_w_down',
        'norm_final']
_OUTS = [("yp", (1, PROMPT, D)), ("ys", (1, SAMPLE, D)), ("kv", (1, 1, PROMPT, KV_RANK)),
         ("krope", (1, 1, PROMPT, ROPE)), ("C", (1, 1, 2, ML_H, DK, DK)), ("n", (1, 1, 2, ML_H, DK)),
         ("m", (1, 1, 2, ML_H)), ("ssd", (1, 1, 2, SSD_H, SSD_P, SSD_N)), ("gdn", (1, 1, 2, GDN_H, DK, DK))]


def kernel(**inputs):
    import concourse.bacc as _bacc
    from concourse.bass_utils import run_bass_kernel_spmd as _run

    nc = _bacc.Bacc("TRN2", target_bir_lowering=False, num_devices=1)
    arrays, a, o = {}, {}, {}
    for name in _INS:
        x = np.ascontiguousarray(inputs[name])
        arrays[f"in_{name}"] = x
        a[name] = nc.dram_tensor(f"in_{name}", x.shape, mybir.dt.from_np(x.dtype), kind="ExternalInput").ap()
    arrays["in_row_ids"] = row_id_table()
    a["row_ids"] = nc.dram_tensor("in_row_ids", (P, 2, TILES, 2), I32, kind="ExternalInput").ap()
    arrays["in_consts"] = const_table()
    a["consts"] = nc.dram_tensor("in_consts", (P, C_ALL), F32, kind="ExternalInput").ap()
    for name, shape in _OUTS:
        o[name] = nc.dram_tensor(f"out_{name}", shape, F32, kind="ExternalOutput").ap()
    build(nc, a, o)
    r = _run(nc, [arrays], core_ids=[0])
    return tuple(r.results[0][f"out_{name}"] for name, _ in _OUTS)
```
